# Optimizing a Trainium2 kernel written in Bass

```python
import math
import jax, jax.numpy as jnp
from jax import lax
import numpy as np

D_MODEL = 1024
BATCH = 1
SEQ = 256
DEPTH = 2

GRID_W = 64
CTX_LEN = 256
N_BRANCH = 4
BRANCH_WIDTH = 256
POOL_WIDTH = 256
POOL_GROUPS = 4
POOL_GROUP_DIM = POOL_WIDTH // POOL_GROUPS
POOL_WINDOWS = (2, 4, 8, 16)
NA_HEADS = 4
NA_HEAD_DIM = 64
NA_WIDTH = NA_HEADS * NA_HEAD_DIM
NA_ROWS = 8
NA_COLS = 16
DIFF_HEADS = 4
DIFF_HEAD_DIM = 32
DIFF_QK_WIDTH = DIFF_HEADS * 2 * DIFF_HEAD_DIM
DIFF_V_WIDTH = DIFF_HEADS * 2 * DIFF_HEAD_DIM
MLA_HEADS = 4
MLA_NOPE_DIM = 64
MLA_ROPE_DIM = 32
MLA_V_DIM = 64
MLA_Q_RANK = 256
MLA_KV_RANK = 128
FFN_HIDDEN = 2816
N_ADA = 9
ROPE_BASE = 10000.0
Q_BLOCK = 128
NORM_EPS = 1e-6
NEG_INF = -1e30
MIX_SPLITS = (POOL_WIDTH, NA_WIDTH, NA_WIDTH, NA_WIDTH, DIFF_QK_WIDTH, DIFF_QK_WIDTH, DIFF_V_WIDTH, MLA_Q_RANK, MLA_KV_RANK, MLA_ROPE_DIM, N_BRANCH * D_MODEL)
MIX_IN_WIDTH = sum(MIX_SPLITS)

kernel_name = 'hybrid_pool_na_diff_mla_dit_block'

def rmsnorm(x, g):
    xf = x.astype(jnp.float32)
    y = xf * lax.rsqrt(jnp.mean(xf * xf, axis=-1, keepdims=True) + NORM_EPS)
    return (y * g.astype(jnp.float32)).astype(x.dtype)

def modulate(xn, shift, scale):
    return xn * (1 + scale) + shift

def swiglu(x, w_in, w_out):
    a, b = jnp.split(x @ w_in, 2, axis=-1)
    return (jax.nn.silu(a) * b) @ w_out

def split_heads(t, h):
    b, n, _ = t.shape
    return t.reshape(b, n, h, -1).transpose(0, 2, 1, 3)

def merge_heads(t):
    b, h, n, d = t.shape
    return t.transpose(0, 2, 1, 3).reshape(b, n, h * d)

def split_mix(proj):
    points, acc = [], 0
    for w in MIX_SPLITS[:-1]:
        acc += w
        points.append(acc)
    return jnp.split(proj, points, axis=-1)

def rope_tables(n, rot_dim):
    t = jnp.arange(n, dtype=jnp.int32)
    pos = jnp.stack([t // GRID_W, t % GRID_W], axis=0).astype(jnp.float32)
    half = rot_dim // 2
    inv = ROPE_BASE ** (-jnp.arange(0, half, 2, dtype=jnp.float32) / half)
    ang = pos[:, :, None] * inv
    return jnp.cos(ang), jnp.sin(ang)

def apply_axial_rope(x, cos, sin):
    half = x.shape[-1] // 2
    quarter = half // 2
    outs = []
    for a in range(2):
        xa = x[..., a * half:(a + 1) * half].astype(jnp.float32)
        x1, x2 = xa[..., :quarter], xa[..., quarter:]
        outs.append(x1 * cos[a] - x2 * sin[a])
        outs.append(x1 * sin[a] + x2 * cos[a])
    return jnp.concatenate(outs, axis=-1).astype(x.dtype)

def sweep_query_blocks(fn, q, axis):
    n = q.shape[axis]
    nb = n // Q_BLOCK
    qb = q.reshape(q.shape[:axis] + (nb, Q_BLOCK) + q.shape[axis + 1:])
    qb = jnp.moveaxis(qb, axis, 0)
    out = lax.map(fn, qb)
    out = jnp.moveaxis(out, 0, 2)
    return out.reshape(out.shape[:2] + (n, out.shape[-1]))

def softmax_attend(q, k, v, scale):
    s = jnp.einsum('bhqd,bhkd->bhqk', q, k).astype(jnp.float32) * scale
    p = jax.nn.softmax(s, axis=-1).astype(v.dtype)
    return jnp.einsum('bhqk,bhkd->bhqd', p, v)

def centred_mean_minus_self(u, w):
    n = u.shape[1]
    cs = jnp.cumsum(u.astype(jnp.float32), axis=1)
    cs = jnp.pad(cs, ((0, 0), (1, 0), (0, 0)))
    i = jnp.arange(n)
    lo = jnp.clip(i - w // 2, 0, n)
    hi = jnp.clip(i - w // 2 + w, 0, n)
    cnt = (hi - lo).astype(jnp.float32)
    mean = (cs[:, hi] - cs[:, lo]) / cnt[None, :, None]
    return mean.astype(u.dtype) - u

def pool_mixer(u, w_grp, scale):
    b, n, _ = u.shape
    ug = u.reshape(b, n, POOL_GROUPS, POOL_GROUP_DIM)
    pooled = jnp.stack([centred_mean_minus_self(ug[:, :, g], w) for g, w in enumerate(POOL_WINDOWS)], axis=2)
    y = jnp.einsum('bngc,gce->bnge', pooled, w_grp).reshape(b, n, POOL_WIDTH)
    return y * scale

def neighbourhood_attention(q, k, v, kc, vc, rpb):
    b, h, n, dh = q.shape
    rows = n // GRID_W
    kr = min(NA_ROWS, rows)
    scale = dh ** -0.5
    r = jnp.arange(rows)
    key_rows = jnp.clip(r - kr // 2, 0, rows - kr)[:, None] + jnp.arange(kr)[None, :]
    j = jnp.arange(GRID_W)
    col_start = jnp.clip(j - NA_COLS // 2, 0, GRID_W - NA_COLS)
    col_ok = (j[None, :] >= col_start[:, None]) & (j[None, :] < col_start[:, None] + NA_COLS)
    dr = key_rows - r[:, None]
    dc = jnp.clip(j[None, :] - j[:, None] + NA_COLS - 1, 0, 2 * NA_COLS - 2)
    bias = jnp.take(rpb[:, dr + NA_ROWS - 1], dc, axis=-1).astype(jnp.float32)
    bias = jnp.where(col_ok, bias, NEG_INF).transpose(0, 1, 3, 2, 4)
    qg = q.reshape(b, h, rows, GRID_W, dh)
    kg = k.reshape(b, h, rows, GRID_W, dh)[:, :, key_rows]
    vg = v.reshape(b, h, rows, GRID_W, dh)[:, :, key_rows]
    s_loc = jnp.einsum('bhrqd,bhrikd->bhrqik', qg, kg).astype(jnp.float32) * scale + bias[None]
    s_ctx = jnp.einsum('bhrqd,bhld->bhrql', qg, kc).astype(jnp.float32) * scale
    n_loc = kr * GRID_W
    s = jnp.concatenate([s_loc.reshape(b, h, rows, GRID_W, n_loc), s_ctx], axis=-1)
    p = jax.nn.softmax(s, axis=-1).astype(v.dtype)
    p_loc = p[..., :n_loc].reshape(b, h, rows, GRID_W, kr, GRID_W)
    out = jnp.einsum('bhrqik,bhrikd->bhrqd', p_loc, vg) + jnp.einsum('bhrql,bhld->bhrqd', p[..., n_loc:], vc)
    return out.reshape(b, h, n, dh)

def diff_heads(t):
    b, n, _ = t.shape
    return t.reshape(b, n, DIFF_HEADS, 2, DIFF_HEAD_DIM).transpose(0, 2, 3, 1, 4)

def diff_attend(q, k, v, lam):
    s = jnp.einsum('bhcqd,bhckd->bhcqk', q, k).astype(jnp.float32) * DIFF_HEAD_DIM ** -0.5
    p = jax.nn.softmax(s, axis=-1)
    w = (p[:, :, 0] - lam * p[:, :, 1]).astype(v.dtype)
    return jnp.einsum('bhqk,bhke->bhqe', w, v)

def mla_project(qa, kva, kr, lp, rope):
    q = split_heads(rmsnorm(qa, lp['mla_q_norm_g']) @ lp['mla_w_qb'], MLA_HEADS)
    kv = split_heads(rmsnorm(kva, lp['mla_kv_norm_g']) @ lp['mla_w_kvb'], MLA_HEADS)
    q_nope, q_rope = q[..., :MLA_NOPE_DIM], q[..., MLA_NOPE_DIM:]
    k_nope, v = kv[..., :MLA_NOPE_DIM], kv[..., MLA_NOPE_DIM:]
    kr = kr[:, None]
    if rope is not None:
        q_rope = apply_axial_rope(q_rope, *rope)
        kr = apply_axial_rope(kr, *rope)
    q = jnp.concatenate([q_nope, q_rope], axis=-1)
    k = jnp.concatenate([k_nope, jnp.broadcast_to(kr, k_nope.shape[:-1] + (MLA_ROPE_DIM,))], axis=-1)
    return q, k, v

def merge_branches(ys, gate, w_branch, w_out):
    b, n, _ = gate.shape
    g = jax.nn.sigmoid(gate).reshape(b, n, N_BRANCH, D_MODEL)
    merged = g[:, :, 0] * (ys[0] @ w_branch[0])
    for i in range(1, N_BRANCH):
        merged = merged + g[:, :, i] * (ys[i] @ w_branch[i])
    return merged @ w_out

def token_mixing(u, uc, lp, lam_init, rope_diff, rope_mla, ctx_out):
    (a_pool, a_nq, a_nk, a_nv, a_dq, a_dk, a_dv, a_mq, a_mkv, a_mkr, a_gate) = split_mix(u @ lp['mix_w_in'])
    (c_pool, c_nq, c_nk, c_nv, c_dq, c_dk, c_dv, c_mq, c_mkv, c_mkr, c_gate) = split_mix(uc @ lp['mix_w_in'])
    y_pool = pool_mixer(a_pool, lp['pool_w'], lp['pool_scale'])
    nk_c, nv_c = split_heads(c_nk, NA_HEADS), split_heads(c_nv, NA_HEADS)
    y_na = merge_heads(neighbourhood_attention(split_heads(a_nq, NA_HEADS), split_heads(a_nk, NA_HEADS), split_heads(a_nv, NA_HEADS), nk_c, nv_c, lp['na_rpb']))
    dl = lp['diff_lambda'].astype(jnp.float32)
    lam = jnp.exp(jnp.sum(dl[0] * dl[1])) - jnp.exp(jnp.sum(dl[2] * dl[3])) + lam_init
    dq = apply_axial_rope(diff_heads(a_dq), *rope_diff)
    dk = apply_axial_rope(diff_heads(a_dk), *rope_diff)
    dv = split_heads(a_dv, DIFF_HEADS)
    dq_c, dk_c, dv_c = diff_heads(c_dq), diff_heads(c_dk), split_heads(c_dv, DIFF_HEADS)
    dk_all = jnp.concatenate([dk, dk_c], axis=3)
    dv_all = jnp.concatenate([dv, dv_c], axis=2)
    d_out = sweep_query_blocks(lambda qb: diff_attend(qb, dk_all, dv_all, lam), dq, axis=3)
    def diff_post(o):
        return merge_heads(rmsnorm(o, lp['diff_subln_g']) * (1.0 - lam_init))
    y_diff = diff_post(d_out)
    mla_scale = (MLA_NOPE_DIM + MLA_ROPE_DIM) ** -0.5
    mq, mk, mv = mla_project(a_mq, a_mkv, a_mkr, lp, rope_mla)
    mq_c, mk_c, mv_c = mla_project(c_mq, c_mkv, c_mkr, lp, None)
    mk_all = jnp.concatenate([mk, mk_c], axis=2)
    mv_all = jnp.concatenate([mv, mv_c], axis=2)
    y_mla = merge_heads(sweep_query_blocks(lambda qb: softmax_attend(qb, mk_all, mv_all, mla_scale), mq, axis=2))
    y = merge_branches([y_pool, y_na, y_diff, y_mla], a_gate, lp['branch_w_out'], lp['mix_w_out'])
    if not ctx_out:
        return y, None
    yc_pool = pool_mixer(c_pool, lp['pool_w'], lp['pool_scale'])
    yc_na = merge_heads(softmax_attend(split_heads(c_nq, NA_HEADS), nk_c, nv_c, NA_HEAD_DIM ** -0.5))
    yc_diff = diff_post(diff_attend(dq_c, dk_c, dv_c, lam))
    yc_mla = merge_heads(softmax_attend(mq_c, mk_c, mv_c, mla_scale))
    yc = merge_branches([yc_pool, yc_na, yc_diff, yc_mla], c_gate, lp['branch_w_out'], lp['mix_w_out'])
    return y, yc

def trunk_layer(h, hc, ada_lat, ada_ctx, lp, lam_init, rope_diff, rope_mla, ctx_out):
    m = jnp.split(ada_lat[:, None, :], N_ADA, axis=-1)
    mc = jnp.split(ada_ctx[None, :], N_ADA, axis=-1)

    def ffn_update(t, mod, sub, ffn_idx):
        tn = modulate(rmsnorm(t, lp['norm_g'][sub]), mod[3 * sub], mod[3 * sub + 1])
        return t + 0.5 * mod[3 * sub + 2] * swiglu(tn, lp['ffn_w_in'][ffn_idx], lp['ffn_w_out'][ffn_idx])

    h = ffn_update(h, m, 0, 0)
    hc = ffn_update(hc, mc, 0, 0)
    u = modulate(rmsnorm(h, lp['norm_g'][1]), m[3], m[4])
    uc = modulate(rmsnorm(hc, lp['norm_g'][1]), mc[3], mc[4])
    y, yc = token_mixing(u, uc, lp, lam_init, rope_diff, rope_mla, ctx_out)
    h = h + m[5] * y
    h = ffn_update(h, m, 2, 1)
    if ctx_out:
        hc = hc + mc[5] * yc
        hc = ffn_update(hc, mc, 2, 1)
    return h, hc

def setup_inputs(seed: int = 0) -> dict:
    key = jax.random.key(seed)
    ks = jax.random.split(key, 22)
    f32 = jnp.float32

    def dense(k, shape, fan_in, gain=1.0):
        return (gain * fan_in ** -0.5) * jax.random.normal(k, shape, f32)

    def gains(k, shape):
        return 1.0 + 0.05 * jax.random.normal(k, shape, f32)

    return {
        'x': jax.random.normal(ks[0], (BATCH, SEQ, D_MODEL), f32),
        'c': jax.random.normal(ks[1], (BATCH, D_MODEL), f32),
        'ctx': jax.random.normal(ks[2], (BATCH, CTX_LEN, D_MODEL), f32),
        'c_ctx': jax.random.normal(ks[3], (D_MODEL,), f32),
        'ada_w': dense(ks[4], (DEPTH, D_MODEL, N_ADA * D_MODEL), D_MODEL, 0.5),
        'ada_b': 0.02 * jax.random.normal(ks[5], (DEPTH, N_ADA * D_MODEL), f32),
        'norm_g': gains(ks[6], (DEPTH, 3, D_MODEL)),
        'ffn_w_in': dense(ks[7], (DEPTH, 2, D_MODEL, 2 * FFN_HIDDEN), D_MODEL),
        'ffn_w_out': dense(ks[8], (DEPTH, 2, FFN_HIDDEN, D_MODEL), FFN_HIDDEN),
        'mix_w_in': dense(ks[9], (DEPTH, D_MODEL, MIX_IN_WIDTH), D_MODEL),
        'pool_w': dense(ks[10], (DEPTH, POOL_GROUPS, POOL_GROUP_DIM, POOL_GROUP_DIM), POOL_GROUP_DIM),
        'pool_scale': gains(ks[11], (DEPTH, POOL_WIDTH)),
        'na_rpb': 0.5 * jax.random.normal(ks[12], (DEPTH, NA_HEADS, 2 * NA_ROWS - 1, 2 * NA_COLS - 1), f32),
        'diff_lambda': 0.1 * jax.random.normal(ks[13], (DEPTH, 4, DIFF_HEAD_DIM), f32),
        'diff_subln_g': gains(ks[14], (DEPTH, 2 * DIFF_HEAD_DIM)),
        'mla_q_norm_g': gains(ks[15], (DEPTH, MLA_Q_RANK)),
        'mla_kv_norm_g': gains(ks[16], (DEPTH, MLA_KV_RANK)),
        'mla_w_qb': dense(ks[17], (DEPTH, MLA_Q_RANK, MLA_HEADS * (MLA_NOPE_DIM + MLA_ROPE_DIM)), MLA_Q_RANK),
        'mla_w_kvb': dense(ks[18], (DEPTH, MLA_KV_RANK, MLA_HEADS * (MLA_NOPE_DIM + MLA_V_DIM)), MLA_KV_RANK),
        'branch_w_out': dense(ks[19], (DEPTH, N_BRANCH, BRANCH_WIDTH, D_MODEL), BRANCH_WIDTH),
        'mix_w_out': dense(ks[20], (DEPTH, D_MODEL, D_MODEL), D_MODEL),
        'final_norm_g': gains(ks[21], (D_MODEL,)),
    }

def reference(x, c, ctx, c_ctx, ada_w, ada_b, norm_g, ffn_w_in, ffn_w_out, mix_w_in, pool_w, pool_scale, na_rpb, diff_lambda, diff_subln_g, mla_q_norm_g, mla_kv_norm_g, mla_w_qb, mla_w_kvb, branch_w_out, mix_w_out, final_norm_g):
    n = x.shape[1]
    rope_diff = rope_tables(n, DIFF_HEAD_DIM)
    rope_mla = rope_tables(n, MLA_ROPE_DIM)
    sc = jax.nn.silu(c)
    scc = jax.nn.silu(c_ctx)
    h, hc = x, ctx
    for l in range(DEPTH):
        lp = {
            'norm_g': norm_g[l], 'ffn_w_in': ffn_w_in[l], 'ffn_w_out': ffn_w_out[l],
            'mix_w_in': mix_w_in[l], 'pool_w': pool_w[l], 'pool_scale': pool_scale[l],
            'na_rpb': na_rpb[l], 'diff_lambda': diff_lambda[l], 'diff_subln_g': diff_subln_g[l],
            'mla_q_norm_g': mla_q_norm_g[l], 'mla_kv_norm_g': mla_kv_norm_g[l],
            'mla_w_qb': mla_w_qb[l], 'mla_w_kvb': mla_w_kvb[l],
            'branch_w_out': branch_w_out[l], 'mix_w_out': mix_w_out[l],
        }
        ada_lat = sc @ ada_w[l] + ada_b[l]
        ada_ctx = scc @ ada_w[l] + ada_b[l]
        lam_init = 0.8 - 0.6 * math.exp(-0.3 * l)
        h, hc = trunk_layer(h, hc, ada_lat, ada_ctx, lp, lam_init, rope_diff, rope_mla, l < DEPTH - 1)
    return rmsnorm(h, final_norm_g)


_drawn_inputs = setup_inputs


def setup_inputs(seed=0):
    import zlib

    import numpy as np

    out = dict(_drawn_inputs(seed))
    spreads = {}
    factors = {'pool_scale': 5.122,
     'na_rpb': 8.0,
     'diff_lambda': 8.0,
     'diff_subln_g': 6.715,
     'mla_q_norm_g': 8.0,
     'mla_kv_norm_g': 8.0}
    for name, (base, spread) in spreads.items():
        noise = np.random.default_rng([zlib.crc32(name.encode()), seed]).standard_normal(out[name].shape)
        drawn = base * np.exp(spread * noise) if base else spread * noise
        out[name] = __import__('jax').numpy.asarray(drawn.astype(out[name].dtype))
    for name, factor in factors.items():
        out[name] = (out[name] * factor).astype(out[name].dtype)
    return out
```

```python
from contextlib import ExitStack

import numpy as np

import concourse.bass as bass
from concourse import mybir

F32 = mybir.dt.float32
F32R = mybir.dt.float32r
ALU = mybir.AluOpType
ACT = mybir.ActivationFunctionType
AX_X = mybir.AxisListType.X

P = 128
D = 1024
KT = D // P
LAT = 256
CTX = 256
TOK = LAT + CTX
DEPTH = 2
FFN = 2816
HT = FFN // P
EPS = 1e-6
GRID_W = 64
NA_ROWS, NA_COLS = 8, 16
RPB_ROWS, RPB_COLS = 2 * NA_ROWS - 1, 2 * NA_COLS - 1
GRID_ROWS = LAT // GRID_W
RPB_USED = 2 * GRID_ROWS - 1
POOL_WINDOWS = (2, 4, 8, 16)
ROT = 32
ROPE_STEPS = 3 * (5 + 4)
LAM_INIT = [0.8 - 0.6 * float(np.exp(-0.3 * l)) for l in range(DEPTH)]

RING = 4
AHEAD = 3

PROJ = (
    [("pool", c, c * P) for c in range(2)]
    + [("qa", c, 1792 + c * P) for c in range(2)]
    + [("kva", 0, 2048), ("kr", 0, 2176)]
    + [("dq", c, 1024 + c * P) for c in range(2)]
    + [("dk", c, 1280 + c * P) for c in range(2)]
    + [("dv", c, 1536 + c * P) for c in range(2)]
    + [("nq", c, 256 + c * P) for c in range(2)]
    + [("nk", c, 512 + c * P) for c in range(2)]
    + [("nv", c, 768 + c * P) for c in range(2)]
)
GATE_COL = 2208
TOKEN_MAJOR = ("pool", "dv", "nv")
QUERY_ONLY = ("pool", "qa", "dq", "nq")
POOL_BR, NA_BR, DIFF_BR, MLA_BR = range(4)

ADA_SLOTS, IN_SLOTS, OUT_SLOTS, PROJ_SLOTS, GB_SLOTS, MIX_OUT_SLOTS = 24, 2 * HT, 3 * KT, len(PROJ), 5 * KT, KT
OUT_PARTS = ((0, 8), (8, 8), (16, 6))


def slot_bases():
    base, at = {}, 0
    for l in range(DEPTH):
        for sub in range(3):
            base[l, sub, "ada"] = at
            at += ADA_SLOTS
            phases = ([("proj", PROJ_SLOTS), ("gb", GB_SLOTS), ("mixout", MIX_OUT_SLOTS)] if sub == 1
                      else [("in", IN_SLOTS), ("out", OUT_SLOTS)])
            for name, n in phases:
                base[l, sub, name] = at
                at += n
    return base, at


def attention_units(l):
    units = []
    for ctx in ((False, True) if l < DEPTH - 1 else (False,)):
        for br in (DIFF_BR, MLA_BR, NA_BR):
            for h in range(4):
                units += [(br, h, b, ctx) for b in range(2)]
    return units


def host_constants():
    t = np.arange(LAT)
    pos = np.stack([t // GRID_W, t % GRID_W]).astype(np.float32)
    half, quarter = ROT // 2, ROT // 4
    inv = (np.float32(10000.0) ** (-np.arange(0, half, 2, dtype=np.float32) / np.float32(half))).astype(np.float32)
    cos = np.zeros((P, LAT), np.float32)
    sin = np.zeros((P, LAT), np.float32)
    perm = np.zeros((P, P), np.float32)
    for f in range(P):
        a, r = (f % ROT) // half, f % half
        ang = pos[a] * inv[r % quarter]
        cos[f], sin[f] = np.cos(ang), np.sin(ang)
        if r < quarter:
            perm[f + quarter, f] = -1.0
        else:
            perm[f - quarter, f] = 1.0
    ident = np.eye(P, dtype=np.float32)
    blocks = np.kron(np.eye(2), np.ones((64, 64))).astype(np.float32)
    ones = np.ones((P, P), np.float32)
    j = np.arange(P) % GRID_W
    start = np.clip(j - NA_COLS // 2, 0, GRID_W - NA_COLS)[:, None]
    key = np.arange(GRID_W)[None, :]
    mask = np.where((key >= start) & (key < start + NA_COLS), 0.0, -1e30).astype(np.float32)
    return np.concatenate([cos, sin, perm, ident, blocks, ones, mask], axis=1)


def pool_matrices():
    out = np.zeros((LAT, 4, LAT), np.float32)
    for g, w in enumerate(POOL_WINDOWS):
        for i in range(LAT):
            lo, hi = max(i - w // 2, 0), min(i - w // 2 + w, LAT)
            out[lo:hi, g, i] += np.float32(1.0) / np.float32(hi - lo)
            out[i, g, i] -= 1.0
    return np.ascontiguousarray(out.reshape(2, P, 4, LAT).transpose(1, 2, 0, 3))


def backbone(nc, x, c, ctx, c_ctx, ada_w, ada_b, norm_g, ffn_w_in, ffn_w_out, mix_w_in, pool_w,
             pool_scale, na_rpb, diff_lambda, diff_subln_g, mla_q_norm_g, mla_kv_norm_g, mla_w_qb,
             mla_w_kvb, branch_w_out, mix_w_out, final_norm_g, tables, pool_mats, out):
    with ExitStack() as stack:
        build(nc, stack, locals())


def build(nc, stack, t):
    base, total_slots = slot_bases()

    def sb(name, shape, dt=F32):
        return stack.enter_context(nc.sbuf_tensor(name, shape, dt))

    def sem(name):
        return stack.enter_context(nc.semaphore(name))

    raw = sb("w_raw", [P, RING, KT, P])
    w_hi = sb("w_hi", [P, RING, KT, P], F32R)
    w_lo = sb("w_lo", [P, RING, KT, P], F32R)
    h = sb("h", [P, KT, TOK])
    xh = sb("xh", [P, KT, TOK], F32R)
    xl = sb("xl", [P, KT, TOK], F32R)
    silu = sb("silu", [P, 2, TOK])
    prod = sb("prod", [P, 2, TOK])
    ssq = sb("ssq", [P, TOK])
    sq = sb("sq", [P, 2, TOK])
    rstd = sb("rstd", [P, TOK])
    tab = sb("tab", [P, 2 * LAT + 4 * P + GRID_W])
    cos, sin = tab[:, 0:LAT], tab[:, LAT:2 * LAT]
    perm, ident, blocks, ones = [tab[:, 2 * LAT + n * P:2 * LAT + (n + 1) * P] for n in range(4)]
    mask = tab[:, 2 * LAT + 4 * P:]
    cols = sb("cols", [P, 2 * P])
    s4 = sb("s4", [P, KT, 4], F32R)
    sc = sb("sc", [P, 2, KT])
    mod_tmp = sb("mod_tmp", [P, 24, 2])
    mods = sb("mods", [P, 2, 24, 2])
    small = sb("small", [P, 96])
    UNITS = 2 * HT
    arena = sb("arena", [P, UNITS, TOK])
    start_of_arena = arena_offset(nc, arena)

    def view(name, unit, n, dt=F32):
        return nc.alloc_sbuf_tensor_at(name, [P, n, TOK], dt, offset=start_of_arena + unit * TOK * 4)

    hid_h = view("hid_h", 0, HT, F32R)
    hid_l = view("hid_l", HT, HT, F32R)
    y_h = view("y_h", 0, 8, F32R)
    y_l = view("y_l", 8, 8, F32R)
    m_h = view("m_h", 20, 8, F32R)
    m_l = view("m_l", 28, 8, F32R)
    feat = {("nq", 0): 0, ("nq", 1): 1, ("nk", 0): 2, ("nk", 1): 3, ("dq", 0): 4, ("dq", 1): 5,
            ("dk", 0): 6, ("dk", 1): 7, ("qa", 0): 24, ("qa", 1): 25, ("kva", 0): 26, ("kr", 0): 27}
    MQ, MK, U_PT, U_P, U_BIAS, U_Y = 8, 12, 24, 28, 32, 36
    tok_unit = {"pool": 16, "nv": 18, "dv": 20, "mv": 22}

    def unit(n):
        return arena[:, n, :]

    def token_major(what):
        u = tok_unit[what]
        return arena[:, u:u + 2, :].rearrange("p a (t c) -> p (a t) c", c=256)

    x_tok = arena[:, 0:8, :].rearrange("p (t a) n -> p t (a n)", t=4)
    out_tok = arena[:, 0:4, :].rearrange("p (t a) n -> p t (a n)", t=2)
    rows = arena[:, 8, :].rearrange("p (a n) -> p a n", a=4)
    lam_row = arena[0:1, 9, :]
    norm_tmp = [unit(40 + n) for n in range(4)]
    pool_mat = arena[:, U_P:U_P + 4, :].rearrange("p g (t n) -> p g t n", t=2)
    pooled = arena[:, 38:40, :]
    bias = arena[:, U_BIAS:U_BIAS + 4, :].rearrange("p h (b i k) -> p h b i k", b=2, i=GRID_ROWS)
    y = arena[:, U_Y:U_Y + 8, :]
    tanh_buf = [unit(16 + n) for n in range(4)]
    macc, mtmp = [unit(36), unit(37)], unit(38)
    w_qb = silu[:, :, :].rearrange("p a n -> p (a n)")[:, 0:768].rearrange("p (k n) -> p k n", k=2)
    w_kvb = prod[:, 0, :]
    w_pool = prod[:, 1, 0:256].rearrange("p (g n) -> p g n", g=2)

    rpb_rows = nc.dram_tensor("rpb_rows", [DEPTH, 4, RPB_USED, GRID_W, RPB_COLS], F32).ap()
    ps = stack.enter_context(nc.psum_tensor("ps", [P, 8, TOK], F32))
    SUM_BANK, ADA_BANK = 6, 0

    def ada_b_cols(l, sub):
        return cols[:, l * P + sub * 24:l * P + sub * 24 + 24]

    def norm_g_cols(l, sub):
        return cols[:, 72 + (l * 3 + sub) * KT:72 + (l * 3 + sub + 1) * KT]

    final_g = cols[:, 120:128]
    cond_cols = cols[:, P + 72:P + 88]

    def pool_scale_col(l, p):
        return cols[:, P + 88 + 2 * l + p:P + 89 + 2 * l + p]

    def q_g_col(l, p):
        return cols[:, P + 92 + 2 * l + p:P + 93 + 2 * l + p]

    def kv_g_col(l):
        return cols[:, P + 96 + l:P + 97 + l]

    def subln_col(l):
        return cols[:, P + 98 + l:P + 99 + l]

    eps_col = small[:, 0:1]
    subln_g = [small[:, 1 + l:2 + l] for l in range(DEPTH)]
    neg_lam = [small[:, 3 + l:4 + l] for l in range(DEPTH)]

    def neg_max(comp):
        return small[:, 8 + comp % 8:9 + comp % 8]

    def exp_bias(comp):
        return small[:, 16 + comp % 8:17 + comp % 8]

    def exp_sum(comp):
        return small[:, 24 + comp % 8:25 + comp % 8]

    def exp_inv(comp):
        return small[:, 32 + comp % 8:33 + comp % 8]

    def exp_inv2(comp):
        return small[:, 40 + comp % 8:41 + comp % 8]

    def norm_tmp_final(k):
        return unit(8 + k // 2)[:, k % 2 * LAT:(k % 2 + 1) * LAT]

    w_loaded = [sem(f"w_loaded{s}") for s in range(RING)]
    w_hi_ready, w_lo_ready = sem("w_hi_ready"), sem("w_lo_ready")
    w_used = sem("w_used")
    in_loaded, rows_loaded, tab_loaded, lam_loaded = sem("in_loaded"), sem("rows_loaded"), sem("tab_loaded"), sem("lam_loaded")
    consts_set, eps_set, ssq_reset = sem("consts_set"), sem("eps_set"), sem("ssq_reset")
    xt_ready, xt_copied = sem("xt_ready"), sem("xt_copied")
    cols_t_ready, cols_ready, cond_ready, s4_ready = sem("cols_t_ready"), sem("cols_ready"), sem("cond_ready"), sem("s4_ready")
    lam_step, lam_exp, lam_bc, lam_ready = sem("lam_step"), sem("lam_exp"), sem("lam_bc"), sem("lam_ready")
    mod_step, mods_ready = sem("mod_step"), sem("mods_ready")
    h_ready, sq_ready, ssq_ready = sem("h_ready"), sem("sq_ready"), sem("ssq_ready")
    sums_ready, std_ready, rstd_ready = sem("sums_ready"), sem("std_ready"), sem("rstd_ready")
    xn_ready, xm_ready, xh_ready, xl_ready = sem("xn_ready"), sem("xm_ready"), sem("xh_ready"), sem("xl_ready")
    silu_ready, prod_ready, hid_h_ready, hid_l_ready = sem("silu_ready"), sem("prod_ready"), sem("hid_h_ready"), sem("hid_l_ready")
    mix_loaded, pool_loaded, bias_loaded, bias_ready = sem("mix_loaded"), sem("pool_loaded"), sem("bias_loaded"), sem("bias_ready")
    rpb_stored = sem("rpb_stored")
    proj_ready = sem("proj_ready")
    pooled_t, pooled_ready, pool_y_t, y_pool_ready = sem("pooled_t"), sem("pooled_ready"), sem("pool_y_t"), sem("y_pool_ready")
    msq_ready, msum_ready, mstd_ready, mrstd_ready, mnorm_ready = [sem(n) for n in ("msq_ready", "msum_ready", "mstd_ready", "mrstd_ready", "mnorm_ready")]
    rot_ready, rope_step = sem("rot_ready"), sem("rope_step")
    mla_t, mla_ready, kr_spread, mrot_ready = [sem(n) for n in ("mla_t", "mla_ready", "kr_spread", "mrot_ready")]
    score_ready, biased, max_step, max_ready = [sem(n) for n in ("score_ready", "biased", "max_step", "max_ready")]
    exp_ready, inv_step, probs_ready = [sem(n) for n in ("exp_ready", "inv_step", "probs_ready")]
    probs_t, probs_t_copied, attn_t, attn_ready = [sem(n) for n in ("probs_t", "probs_t_copied", "attn_t", "attn_ready")]
    dsq_ready, dsum_ready, dstd_ready, dinv_ready, dnorm_ready = [sem(n) for n in ("dsq_ready", "dsum_ready", "dstd_ready", "dinv_ready", "dnorm_ready")]
    y_h_ready, y_l_ready = sem("y_h_ready"), sem("y_l_ready")
    tanh_ready, gated, macc_ready, m_h_ready, m_l_ready = [sem(n) for n in ("tanh_ready", "gated", "macc_ready", "m_h_ready", "m_l_ready")]
    fin_ready, fin_t, fin_copied, out_stored = [sem(n) for n in ("fin_ready", "fin_t", "fin_copied", "out_stored")]

    def update_index(l, sub):
        return 1 + 3 * l + sub

    def tokens(l, sub):
        return LAT if (l, sub) == (DEPTH - 1, 2) else TOK

    def query_tokens(l):
        return TOK if l < DEPTH - 1 else LAT

    def halves(n):
        return [(0, slice(0, LAT)), (1, slice(LAT, TOK))][:n // LAT]

    units = [attention_units(l) for l in range(DEPTH)]
    unit0 = [0, len(units[0])]
    comp_at, n_comps = {}, 0
    for l in range(DEPTH):
        for n, u in enumerate(units[l]):
            k = 2 if u[0] == DIFF_BR else 1
            comp_at[l, n] = list(range(n_comps, n_comps + k))
            n_comps += k
    unit_of_comp = {cc: unit0[l] + n for (l, n), v in comp_at.items() for cc in v}
    na_before = {}
    seen = 0
    for l in range(DEPTH):
        for n, u in enumerate(units[l]):
            na_before[l, n] = seen
            seen += u[0] == NA_BR and not u[3]

    def steps(eng, iters, body_slots, body, peel=False):
        if peel:
            for i in range(iters):
                body(i)
        else:
            with eng.Fori(0, iters) as i:
                body(i)

    rotary_slots = {base[l, 1, "proj"] + [what for what, _, _ in PROJ].index("kr") for l in range(DEPTH)}

    def rotary_slot(b, i, s):
        return isinstance(i, int) and b + s + AHEAD in rotary_slots

    def four(w, at):
        return w[:, at].rearrange("p k (a n) -> p k a n", n=ROT)

    def four_of(w, at):
        return w[:, at, :, 0:ROT].unsqueeze(2).to_broadcast([P, KT, P // ROT, ROT])

    block = stack.enter_context(nc.Block())

    @block.sync
    def _(sp):
        sp.dma_start(x_tok[:, 0:2, :], t["x"][0].rearrange("(t p) n -> p t n", p=P)).then_inc(in_loaded, 16)
        sp.dma_start(x_tok[:, 2:4, :], t["ctx"][0].rearrange("(t p) n -> p t n", p=P)).then_inc(in_loaded, 16)

        def repeat(first, last, body):
            with sp.Fori(first + 1, last + 1) as r:
                body(lambda m, c: r * m + (c - m))

        def fixed(i):
            return lambda m, c: i * m + c

        def load(b, i, body_slots, s, src, col, kt=KT):
            at = (b + s) % RING
            freed = i(body_slots, b + s - RING + 1)
            if not isinstance(freed, int) or freed > 0:
                sp.wait_ge(w_lo_ready, freed)
            sp.dma_start(raw[:, at, 0:kt, :], src(col)).then_inc(w_loaded[at], 16)

        for l in range(DEPTH):
            for sub in range(3):
                ada = t["ada_w"][l].rearrange("(k p) n -> p k n", p=P)
                b = base[l, sub, "ada"]

                def load_ada(i, b=b, ada=ada, sub=sub):
                    for s in range(4):
                        load(b, i, 4, s, lambda col: ada[:, :, bass.ds(col, P)], i(4 * P, sub * 3 * D + s * P))
                if b == 0:
                    load_ada(fixed(0))
                    repeat(1, ADA_SLOTS // 4, load_ada)
                else:
                    repeat(0, ADA_SLOTS // 4, load_ada)
                if sub != 1:
                    w_in = t["ffn_w_in"][l, sub // 2].rearrange("(k p) n -> p k n", p=P)
                    w_out = t["ffn_w_out"][l, sub // 2].rearrange("(k p) n -> p k n", p=P)
                    b = base[l, sub, "in"]

                    def load_in(i, b=b, w_in=w_in):
                        for s in range(4):
                            load(b, i, 4, s, lambda col: w_in[:, :, bass.ds(col, P)], i(2 * P, s // 2 * P + s % 2 * FFN))
                    repeat(0, HT // 2, load_in)
                    b = base[l, sub, "out"]

                    def load_out(i, b=b, w_out=w_out):
                        for s in range(12):
                            k0, kn = OUT_PARTS[s % 3]
                            load(b, i, 12, s, lambda col: w_out[:, k0:k0 + kn, bass.ds(col, P)], i(4 * P, s // 3 * P), kn)
                    repeat(0, 2, load_out)
                else:
                    w_mix = t["mix_w_in"][l].rearrange("(k p) n -> p k n", p=P)
                    b = base[l, sub, "proj"]
                    for s, (_, _, col) in enumerate(PROJ):
                        load(b, fixed(0), 0, s, lambda c, w_mix=w_mix: w_mix[:, :, c:c + P], col)
                    w_br = t["branch_w_out"][l].rearrange("b (k p) n -> p (b k) n", p=P)
                    b = base[l, sub, "gb"]

                    def load_gb(i, b=b, w_mix=w_mix, w_br=w_br):
                        for s in range(20):
                            n, what = s // 5, s % 5
                            if what == 2:
                                load(b, i, 20, s, lambda col: w_br[:, :, bass.ds(col, P)], i(4 * P, n * P))
                            else:
                                gate = what - (what > 2)
                                load(b, i, 20, s, lambda col: w_mix[:, :, bass.ds(col, P)], i(4 * P, GATE_COL + gate * D + n * P))
                    repeat(0, 2, load_gb)
                    w_mo = t["mix_w_out"][l].rearrange("(k p) n -> p k n", p=P)
                    b = base[l, sub, "mixout"]

                    def load_mo(i, b=b, w_mo=w_mo):
                        for s in range(4):
                            load(b, i, 4, s, lambda col: w_mo[:, :, bass.ds(col, P)], i(4 * P, s * P))
                    repeat(0, 2, load_mo)
        for tt in range(2):
            sp.wait_ge(fin_copied, 2 * (tt + 1))
            sp.dma_start(t["out"][0, tt * P:(tt + 1) * P, :], out_tok[:, tt, :]).then_inc(out_stored, 16)
        sp.wait_ge(out_stored, 32)

    @block.gpsimd
    def _(pool):
        def load_rows(r0, n, a, src):
            pool.dma_start(rows[r0:r0 + n, a, :], src).then_inc(rows_loaded, 16)

        ada_rows = t["ada_b"].rearrange("l (r n) -> l r n", n=P)
        load_rows(0, 72, 0, ada_rows[0])
        load_rows(72, 48, 0, t["norm_g"].rearrange("l s (k n) -> (l s k) n", n=P))
        load_rows(120, 8, 0, t["final_norm_g"].rearrange("(k n) -> k n", n=P))
        load_rows(0, 72, 1, ada_rows[1])
        load_rows(72, 8, 1, t["c"].rearrange("b (k n) -> (b k) n", n=P))
        load_rows(80, 8, 1, t["c_ctx"].rearrange("(k n) -> k n", n=P))
        load_rows(88, 4, 1, t["pool_scale"].rearrange("l (k n) -> (l k) n", n=P))
        load_rows(92, 4, 1, t["mla_q_norm_g"].rearrange("l (k n) -> (l k) n", n=P))
        load_rows(96, 2, 1, t["mla_kv_norm_g"])
        for half in range(2):
            pool.dma_start(rows[98:100, 1, half * 64:half * 64 + 64], t["diff_subln_g"]).then_inc(rows_loaded, 16)
        pool.dma_start(tab[:, :], t["tables"]).then_inc(tab_loaded, 16)
        pool.dma_start(lam_row[:, 0:256], t["diff_lambda"].rearrange("l q d -> (l q d)").rearrange("(a n) -> a n", a=1)).then_inc(lam_loaded, 16)

        for l in range(DEPTH):
            for hd in range(4):
                first = NA_ROWS - GRID_ROWS
                src = t["na_rpb"][l, hd, first:first + RPB_USED, :].unsqueeze(1).to_broadcast([RPB_USED, GRID_W, RPB_COLS])
                pool.dma_start(rpb_rows[l, hd], src).then_inc(rpb_stored, 16)
        pool.wait_ge(rpb_stored, 16 * 4 * DEPTH)

        def norm(q, n):
            pool.wait_ge(rstd_ready, q + 1)
            for k in range(KT):
                if k >= 2:
                    pool.wait_ge(xm_ready, q * KT + k - 1)
                pool.tensor_tensor(norm_tmp[k % 2][:, 0:n], h[:, k, 0:n], rstd[:, 0:n], ALU.mult).then_inc(xn_ready, 1)

        for l in range(DEPTH):
            norm(3 * l, tokens(l, 0))
            norm(3 * l + 1, tokens(l, 1))
            pool.dma_start(w_qb, t["mla_w_qb"][l].rearrange("(k p) n -> p k n", p=P)).then_inc(mix_loaded, 16)
            pool.dma_start(w_kvb, t["mla_w_kvb"][l]).then_inc(mix_loaded, 16)
            pool.memset(w_pool, 0.0).then_inc(consts_set, 1)
            pool.wait_ge(consts_set, l + 1)
            for g in range(4):
                r = g % 2 * 64
                pool.dma_start(w_pool[r:r + 64, g // 2, r:r + 64], t["pool_w"][l, g]).then_inc(pool_loaded, 16)
            pool.dma_start(pool_mat, t["pool_mats"]).then_inc(pool_loaded, 16)
            for hd in range(4):
                for r in range(GRID_ROWS):
                    src = bass.AP(tensor=rpb_rows.tensor,
                                  offset=(l * 4 + hd) * RPB_USED * GRID_W * RPB_COLS
                                  + (GRID_ROWS - 1 - r) * GRID_W * RPB_COLS + NA_COLS - 1,
                                  ap=[[RPB_COLS - 1, GRID_W], [GRID_W * RPB_COLS, GRID_ROWS], [1, GRID_W]])
                    pool.dma_start(bias[r % 2 * 64:r % 2 * 64 + 64, hd, r // 2], src).then_inc(bias_loaded, 16)
            pool.wait_ge(bias_loaded, 16 * 16 * (l + 1))
            for hd in range(4):
                for b in range(2):
                    pool.tensor_tensor(bias[:, hd, b], bias[:, hd, b],
                                       mask.unsqueeze(1).to_broadcast([P, GRID_ROWS, GRID_W]), ALU.add).then_inc(bias_ready, 1)
            norm(3 * l + 2, tokens(l, 2))

    @block.tensor
    def _(pe):
        pe.wait_ge(tab_loaded, 16)
        pe.wait_ge(rows_loaded, 16 * 11)
        pe.transpose(ps[:, 6, 0:P], rows[:, 0, :], ident)
        pe.transpose(ps[:, 6, P:P + 100], rows[0:100, 1, :], ident[0:100, 0:100]).then_inc(cols_t_ready, 1)
        pe.wait_ge(in_loaded, 32)
        for k in range(KT):
            if k >= 4:
                pe.wait_ge(xt_copied, k - 3)
            for tt in range(4):
                last = pe.transpose(ps[:, k % 4, tt * P:(tt + 1) * P], x_tok[:, tt, k * P:(k + 1) * P], ident)
            last.then_inc(xt_ready, 1)
        pe.wait_ge(lam_step, 3)
        pe.matmul(ps[:, 5, 0:2], ones[0:1, :], lam_row[:, 400:402], start=True, stop=True).then_inc(lam_bc, 1)

        def three_passes(dst, hi, lo, mh, ml, first, last):
            pe.matmul(dst, lo, mh, start=first, stop=False)
            pe.matmul(dst, hi, ml, start=False, stop=False)
            return pe.matmul(dst, hi, mh, start=False, stop=last)

        def slot_products(b, i, body_slots, s, dst, mh, ml, kt=KT, first=True, last=True):
            at = (b + s) % RING
            pe.wait_ge(w_lo_ready, i * body_slots + (b + s + 1))
            for k in range(kt):
                mm = three_passes(dst, w_hi[:, at, k, :], w_lo[:, at, k, :], mh(k), ml(k),
                                  first and k == 0, last and k == kt - 1)
            mm.then_inc(w_used, 1)

        def ada_phase(l, sub):
            b = base[l, sub, "ada"]
            if b == 0:
                pe.wait_ge(s4_ready, 2)

            def body(i):
                for s in range(4):
                    at = (b + s) % RING
                    dst = ps[:, ADA_BANK, bass.ds(i * 16 + s * 4, 4)]
                    pe.wait_ge(w_lo_ready, i * 4 + (b + s + 1))
                    for k in range(KT):
                        pe.matmul(dst, w_lo[:, at, k, :], s4[:, k, :], start=(k == 0), stop=False)
                        mm = pe.matmul(dst, w_hi[:, at, k, :], s4[:, k, :], start=False, stop=(k == KT - 1))
                    mm.then_inc(w_used, 1)
            steps(pe, ADA_SLOTS // 4, 4, body)

        def norm_sum(q, n):
            pe.wait_ge(ssq_ready, KT * (q + 1))
            pe.matmul(ps[:, SUM_BANK, 0:n], ones, ssq[:, 0:n], start=True, stop=True).then_inc(sums_ready, 1)

        def ffn_phase(l, sub, f):
            n = tokens(l, sub)
            q = update_index(l, sub) - 1
            b = base[l, sub, "in"]

            def pair(i, p):
                for s in (2 * p, 2 * p + 1):
                    slot_products(b, i, 4, s, ps[:, s, 0:n], lambda k: xh[:, k, 0:n], lambda k: xl[:, k, 0:n])

            def body(i):
                for p in range(2):
                    if not isinstance(i, int):
                        pe.wait_ge(prod_ready, i * 2 + (f * HT + p - 1))
                    pair(i, p)
            at = b % RING
            pe.wait_ge(w_lo_ready, b + 1)
            for k in range(KT):
                pe.wait_ge(xl_ready, q * KT + k + 1)
                mm = three_passes(ps[:, 0, 0:n], w_hi[:, at, k, :], w_lo[:, at, k, :], xh[:, k, 0:n], xl[:, k, 0:n], k == 0, k == KT - 1)
            mm.then_inc(w_used, 1)
            slot_products(b, 0, 4, 1, ps[:, 1, 0:n], lambda k: xh[:, k, 0:n], lambda k: xl[:, k, 0:n])
            pair(0, 1)
            with pe.Fori(1, HT // 2) as i:
                body(i)

            b = base[l, sub, "out"]
            u = update_index(l, sub)

            def out_body(i):
                for c in range(4):
                    if not (isinstance(i, int) and i == 0):
                        pe.wait_ge(h_ready, i * 4 + ((u - 1) * KT + c - 3))
                    for part, (k0, kn) in enumerate(OUT_PARTS):
                        if isinstance(i, int) and i == 0 and c == 0:
                            pe.wait_ge(hid_l_ready, f * HT + k0 + kn)
                        slot_products(b, i, 12, 3 * c + part, ps[:, 4 + c, 0:n],
                                      lambda k: hid_h[:, k0 + k, 0:n], lambda k: hid_l[:, k0 + k, 0:n],
                                      kn, part == 0, part == 2)
            out_body(0)
            out_body(1)

        def proj_phase(l):
            b = base[l, 1, "proj"]
            q = update_index(l, 1) - 1
            for s, (what, c, _) in enumerate(PROJ):
                if s >= 8:
                    pe.wait_ge(proj_ready, l * PROJ_SLOTS + s - 7)
                if s == 0:
                    pe.wait_ge(xl_ready, (q + 1) * KT)
                at = (b + s) % RING
                n = query_tokens(l) if what in QUERY_ONLY else TOK
                if what in TOKEN_MAJOR:
                    pe.wait_ge(w_lo_ready, b + s + 1)
                    for tt in range(n // P):
                        dst, tokens_of = ps[:, s % 8, tt * P:(tt + 1) * P], slice(tt * P, (tt + 1) * P)
                        for k in range(KT):
                            mm = three_passes(dst, xh[:, k, tokens_of], xl[:, k, tokens_of],
                                              w_hi[:, at, k, :], w_lo[:, at, k, :], k == 0, k == KT - 1)
                    mm.then_inc(w_used, 1)
                else:
                    slot_products(b, 0, 0, s, ps[:, s % 8, 0:n], lambda k: xh[:, k, 0:n], lambda k: xl[:, k, 0:n])

        def pool_phase(l):
            n = query_tokens(l)
            pe.wait_ge(proj_ready, (l + 1) * PROJ_SLOTS)
            pe.wait_ge(pool_loaded, 16 * 5 * (l + 1))
            u = token_major("pool")
            for g in range(4):
                r = g % 2 * 64
                for half in range(n // LAT):
                    for tt in range(2):
                        mm = pe.matmul(ps[r:r + 64, g // 2, half * LAT:(half + 1) * LAT],
                                       u[:, 2 * half + tt, g * 64:(g + 1) * 64], pool_mat[:, g, tt, :],
                                       start=(tt == 0), stop=(tt == 1))
            mm.then_inc(pooled_t, 1)
            pe.wait_ge(pooled_ready, l + 1)
            for p in range(2):
                mm = pe.matmul(ps[:, 2 + p, 0:n], w_pool[:, p, :], pooled[:, p, 0:n], start=True, stop=True)
            mm.then_inc(pool_y_t, 1)

        def rotate_phase(l):
            for n, key in enumerate([("dq", 0), ("dq", 1), ("dk", 0), ("dk", 1), ("kr", 0)]):
                if n == 0:
                    pe.wait_ge(y_pool_ready, l + 1)
                pe.matmul(ps[:, 2 + n, 0:LAT], perm, unit(feat[key])[:, 0:LAT], start=True, stop=True).then_inc(rot_ready, 1)

        def mla_phase(l):
            n = query_tokens(l)
            pe.wait_ge(msq_ready, 3 * l + 3)
            pe.matmul(ps[:, 0, 0:n], ones, unit(U_P)[:, 0:n], start=True, stop=False)
            pe.matmul(ps[:, 0, 0:n], ones, unit(U_P + 1)[:, 0:n], start=False, stop=True)
            pe.matmul(ps[:, 1, :], ones, unit(U_P + 2), start=True, stop=True).then_inc(msum_ready, 1)
            pe.wait_ge(mnorm_ready, l + 1)
            pe.wait_ge(mix_loaded, 32 * (l + 1))
            pe.wait_ge(rope_step, l * ROPE_STEPS + 5 * 3)
            for hd in range(4):
                for k in range(2):
                    mm = pe.matmul(ps[0:96, hd, 0:n], w_qb[:, k, hd * 96:(hd + 1) * 96],
                                   unit(feat["qa", k])[:, 0:n], start=(k == 0), stop=(k == 1))
                mm.then_inc(mla_t, 1)
            for hd in range(4):
                pe.matmul(ps[0:64, 4 + hd, :], w_kvb[:, hd * P:hd * P + 64], unit(feat["kva", 0]),
                          start=True, stop=True).then_inc(mla_t, 1)
            pe.wait_ge(mla_ready, 10 * l + 2)
            w_v = w_kvb.rearrange("p (h c) -> p h c", h=4)[:, :, 64:P]
            for tt in range(4):
                mm = pe.matmul(ps[:, tt // 2, tt % 2 * 256:tt % 2 * 256 + 256],
                               unit(feat["kva", 0])[:, tt * P:(tt + 1) * P], w_v, start=True, stop=True)
                if tt % 2:
                    mm.then_inc(mla_t, 1)
            pe.wait_ge(mla_ready, 10 * l + 8)
            for hd in range(4):
                pe.matmul(ps[64:96, 4 + hd, 0:LAT], perm[64:96, 64:96], unit(MQ + hd)[64:96, 0:LAT],
                          start=True, stop=True).then_inc(mrot_ready, 1)

        def attention_phase(l):
            us = units[l]
            pe.wait_ge(mla_ready, 10 * (l + 1))
            pe.wait_ge(rope_step, (l + 1) * ROPE_STEPS)
            pe.wait_ge(kr_spread, l + 1)

            def scores(n):
                br, hd, b, is_ctx = us[n]
                q0 = (LAT if is_ctx else 0) + b * P
                k0 = LAT if is_ctx else 0
                for j, cc in enumerate(comp_at[l, n]):
                    if cc >= 4:
                        pe.wait_ge(exp_ready, cc - 3)
                    if br == DIFF_BR:
                        r, rn, qt, kt = hd % 2 * 64 + j * 32, 32, feat["dq", hd // 2], feat["dk", hd // 2]
                    elif br == NA_BR:
                        r, rn, qt, kt = hd % 2 * 64, 64, feat["nq", hd // 2], feat["nk", hd // 2]
                    else:
                        r, rn, qt, kt = 0, 96, MQ + hd, MK + hd
                    pe.matmul(ps[:, cc % 4, 0:TOK - k0], unit(qt)[r:r + rn, q0:q0 + P],
                              unit(kt)[r:r + rn, k0:TOK], start=True, stop=True).then_inc(score_ready, 1)

            def transposes(n):
                u = unit0[l] + n
                _, _, _, is_ctx = us[n]
                pe.wait_ge(probs_ready, u + 1)
                if u >= 2:
                    pe.wait_ge(probs_t_copied, u - 1)
                src = unit(U_P + comp_at[l, n][0] % 4)
                for kt in range(2 if is_ctx else 4):
                    mm = pe.transpose(ps[:, 4 + u % 2, kt * P:(kt + 1) * P], src[:, kt * P:(kt + 1) * P], ident)
                mm.then_inc(probs_t, 1)

            def values(n):
                br, hd, _, is_ctx = us[n]
                v = (unit0[l] + n) // 2
                pe.wait_ge(probs_t_copied, unit0[l] + n + 1)
                if v >= 2:
                    pe.wait_ge(attn_ready, v - 1)
                vals = token_major({DIFF_BR: "dv", NA_BR: "nv", MLA_BR: "mv"}[br])
                pt = arena[:, U_PT + v % 2 * 2:U_PT + v % 2 * 2 + 2, :].rearrange("p a (t q) -> p (a t) q", q=256)
                r, kts = hd % 2 * 64, 2 if is_ctx else 4
                for kt in range(kts):
                    mm = pe.matmul(ps[r:r + 64, 6 + v % 2, 0:256],
                                   vals[:, (2 if is_ctx else 0) + kt, hd * 64:(hd + 1) * 64], pt[:, kt, :],
                                   start=(kt == 0), stop=(kt == kts - 1))
                mm.then_inc(attn_t, 1)

            scores(0)
            for n in range(len(us)):
                if n + 1 < len(us):
                    scores(n + 1)
                transposes(n)
                if n % 2 == 0 and n >= 2:
                    values(n - 1)
            values(len(us) - 1)
            nt = query_tokens(l)
            pe.wait_ge(dsq_ready, 2 * (l + 1))
            for p in range(2):
                pe.matmul(ps[:, p, 0:nt], blocks, sq[:, p, 0:nt], start=True, stop=True).then_inc(dsum_ready, 1)

        def merge_phase(l):
            n = query_tokens(l)
            b = base[l, 1, "gb"]

            def body(i, guard):
                for c in range(4):
                    for what in range(5):
                        s = 5 * c + what
                        if what == 2:
                            if not guard and c == 0:
                                pe.wait_ge(y_l_ready, l + 1)
                            if guard or c > 0:
                                pe.wait_ge(gated, i * 16 + (l * 32 + 4 * c))
                            at = (b + s) % RING
                            pe.wait_ge(w_lo_ready, i * 20 + (b + s + 1))
                            for br in range(4):
                                for k in range(2):
                                    kk = 2 * br + k
                                    mm = three_passes(ps[:, br, 0:n], w_hi[:, at, kk, :], w_lo[:, at, kk, :],
                                                      y_h[:, kk, 0:n], y_l[:, kk, 0:n], k == 0, k == 1)
                            mm.then_inc(w_used, 1)
                        else:
                            gate = what - (what > 2)
                            if guard or c > 0:
                                pe.wait_ge(tanh_ready, i * 16 + (l * 32 + 4 * c + gate - 3))
                            slot_products(b, i, 20, s, ps[:, 4 + gate, 0:n], lambda k: xh[:, k, 0:n], lambda k: xl[:, k, 0:n])
            body(0, False)
            body(1, True)

            b = base[l, 1, "mixout"]
            u = update_index(l, 1)
            pe.wait_ge(gated, 32 * (l + 1))
            for i in range(2):
                for s in range(4):
                    at = (b + s) % RING
                    if i > 0:
                        pe.wait_ge(h_ready, (u - 1) * KT + i * 4 + s - 3)
                    pe.wait_ge(w_lo_ready, b + 4 * i + s + 1)
                    for k in range(KT):
                        if i == 0 and s == 0:
                            pe.wait_ge(m_l_ready, l * KT + k + 1)
                        mm = three_passes(ps[:, 4 + s, 0:n], w_hi[:, at, k, :], w_lo[:, at, k, :],
                                          m_h[:, k, 0:n], m_l[:, k, 0:n], k == 0, k == KT - 1)
                    mm.then_inc(w_used, 1)

        for l in range(DEPTH):
            for sub in range(3):
                ada_phase(l, sub)
                norm_sum(3 * l + sub, tokens(l, sub))
                if sub != 1:
                    ffn_phase(l, sub, 2 * l + sub // 2)
                else:
                    proj_phase(l)
                    pool_phase(l)
                    rotate_phase(l)
                    mla_phase(l)
                    attention_phase(l)
                    merge_phase(l)
        norm_sum(3 * DEPTH, LAT)
        for tt in range(2):
            for k in range(KT):
                pe.wait_ge(fin_ready, k + 1)
                mm = pe.transpose(ps[:, 2 * tt + k // 4, k % 4 * P:(k % 4 + 1) * P], norm_tmp_final(k)[:, tt * P:(tt + 1) * P], ident)
                if k % 4 == 3:
                    mm.then_inc(fin_t, 1)

    @block.scalar
    def _(act):
        def split(b, i, body_slots, s):
            at = (b + s + AHEAD) % RING
            act.wait_ge(w_loaded[at], i * (body_slots // RING * 16) + 16 * ((b + s + AHEAD) // RING + 1))
            if not (isinstance(i, int) and i * body_slots + b + s + AHEAD < RING):
                act.wait_ge(w_used, i * body_slots + (b + s + AHEAD - RING + 1))
            if rotary_slot(b, i, s):
                act.copy(four(w_hi, at), four_of(raw, at)).then_inc(w_hi_ready, 1)
                return
            act.copy(w_hi[:, at], raw[:, at]).then_inc(w_hi_ready, 1)

        def maybe_split(b, i, body_slots, s):
            if not isinstance(i, int) or i * body_slots + b + s + AHEAD < total_slots:
                split(b, i, body_slots, s)

        def squares(u, i, step, c, n):
            tile = i * step + c
            act.wait_ge(h_ready, i * step + ((u - 1) * KT + c + 1))
            act.wait_ge(ssq_ready, i * step + (u * KT + c - 1))
            act.activation(sq[:, c % 2, 0:n], h[:, bass.ds(tile, 1), 0:n].rearrange("p a n -> p (a n)"),
                           ACT.Square).then_inc(sq_ready, 1)

        act.wait_ge(cols_ready, 1)
        act.activation(sc[:, :, :].rearrange("p w k -> p (w k)"), cond_cols, ACT.Silu).then_inc(cond_ready, 1)
        act.wait_ge(cond_ready, 1)
        act.copy(s4[:, :, 0:2].rearrange("p k w -> p w k"), sc[:, :, :]).then_inc(s4_ready, 1)
        for m in range(AHEAD):
            split(-AHEAD, 0, 0, m)
        for k in range(KT):
            act.wait_ge(xt_ready, k + 1)
            act.copy(h[:, k, :], ps[:, k % 4, :]).then_inc(xt_copied, 1)
            act.wait_ge(xt_copied, k + 1)
            if k >= 2:
                act.wait_ge(ssq_ready, k - 1)
            act.activation(sq[:, k % 2, :], h[:, k, :], ACT.Square).then_inc(sq_ready, 1)
        act.wait_ge(lam_step, 2)
        act.activation(lam_row[:, 392:396], lam_row[:, 384:388], ACT.Exp).then_inc(lam_exp, 1)

        def ada_phase(l, sub):
            b = base[l, sub, "ada"]

            def body(i):
                for s in range(4):
                    split(b, i, 4, s)
            if b == 0:
                body(0)
                with act.Fori(1, ADA_SLOTS // 4) as i:
                    body(i)
            else:
                steps(act, ADA_SLOTS // 4, 4, body)

        def root(dst, src, width):
            return act.activation(dst, src, ACT.Sqrt, bias=eps_col, scale=1.0 / width)

        def norm(q, n):
            if q == 0:
                act.wait_ge(eps_set, 1)
            act.wait_ge(sums_ready, q + 1)
            root(rstd[:, 0:n], ps[:, SUM_BANK, 0:n], D).then_inc(std_ready, 1)
            if q == 3 * DEPTH:
                return
            for k in range(KT):
                act.wait_ge(xm_ready, q * KT + k + 1)
                act.copy(xh[:, k, 0:n], norm_tmp[2 + k % 2][:, 0:n]).then_inc(xh_ready, 1)

        def ffn_phase(l, sub, f):
            n = tokens(l, sub)
            b = base[l, sub, "in"]

            def body(i):
                for p in range(2):
                    split(b, i, 4, 2 * p)
                    act.wait_ge(w_used, i * 4 + (b + 2 * p + 1))
                    if f * HT + p >= 2 or not isinstance(i, int):
                        act.wait_ge(prod_ready, i * 2 + (f * HT + p - 1))
                    act.activation(silu[:, p, 0:n], ps[:, 2 * p, 0:n], ACT.Silu).then_inc(silu_ready, 1)
                    split(b, i, 4, 2 * p + 1)
                    act.wait_ge(prod_ready, i * 2 + (f * HT + p + 1))
                    act.copy(hid_h[:, bass.ds(i * 2 + p, 1), 0:n].rearrange("p a n -> p (a n)"), prod[:, p, 0:n]).then_inc(hid_h_ready, 1)
            body(0)
            with act.Fori(1, HT // 2) as i:
                body(i)
            b = base[l, sub, "out"]
            u = update_index(l, sub)

            def out_body(i):
                for c in range(4):
                    for part in range(3):
                        maybe_split(b, i, 12, 3 * c + part)
                    squares(u, i, 4, c, n)
            steps(act, 2, 12, out_body, peel=(l, sub) == (DEPTH - 1, 2))

        def mix_phase(l):
            n = query_tokens(l)
            b = base[l, 1, "proj"]
            for s, (what, c, _) in enumerate(PROJ):
                split(b, 0, 0, s)
                act.wait_ge(w_used, b + s + 1)
                m = n if what in QUERY_ONLY else TOK
                if what in TOKEN_MAJOR:
                    dst = token_major(what)[:, 0:m // P, c * P:(c + 1) * P]
                    act.copy(dst, ps[:, s % 8, 0:m].rearrange("p (t n) -> p t n", n=P)).then_inc(proj_ready, 1)
                elif what == "nq":
                    act.mul(unit(feat[what, c])[:, 0:m], ps[:, s % 8, 0:m], 0.125).then_inc(proj_ready, 1)
                else:
                    act.copy(unit(feat[what, c])[:, 0:m], ps[:, s % 8, 0:m]).then_inc(proj_ready, 1)
            act.wait_ge(pooled_t, l + 1)
            act.copy(pooled[:, :, 0:n], ps[:, 0:2, 0:n]).then_inc(pooled_ready, 1)
            act.wait_ge(pool_y_t, l + 1)
            act.activation(y[:, 0, 0:n], ps[:, 2, 0:n], ACT.Copy, scale=pool_scale_col(l, 0))
            act.activation(y[:, 1, 0:n], ps[:, 3, 0:n], ACT.Copy, scale=pool_scale_col(l, 1)).then_inc(y_pool_ready, 1)
            for j, (key, m) in enumerate([(("qa", 0), n), (("qa", 1), n), (("kva", 0), TOK)]):
                act.activation(unit(U_P + j)[:, 0:m], unit(feat[key])[:, 0:m], ACT.Square).then_inc(msq_ready, 1)
            act.wait_ge(msum_ready, l + 1)
            root(unit(U_P)[:, 0:n], ps[:, 0, 0:n], 256)
            root(unit(U_P + 2), ps[:, 1, :], 128).then_inc(mstd_ready, 1)
            for hd in range(4):
                act.wait_ge(mla_t, 10 * l + hd + 1)
                act.copy(unit(MQ + hd)[0:96, 0:n], ps[0:96, hd, 0:n]).then_inc(mla_ready, 1)
            for hd in range(4):
                act.wait_ge(mla_t, 10 * l + 4 + hd + 1)
                act.copy(unit(MK + hd)[0:64, :], ps[0:64, 4 + hd, :]).then_inc(mla_ready, 1)
            mv = token_major("mv")
            for a in range(2):
                act.wait_ge(mla_t, 10 * l + 8 + a + 1)
                act.copy(mv[:, 2 * a:2 * a + 2, :], ps[:, a, :].rearrange("p (t n) -> p t n", t=2)).then_inc(mla_ready, 1)
            us = units[l]

            def exps(m):
                br, _, _, is_ctx = us[m]
                width = CTX if is_ctx else TOK
                scale = {DIFF_BR: 32 ** -0.5, MLA_BR: 96 ** -0.5, NA_BR: 1.0}[br]
                for cc in comp_at[l, m]:
                    act.wait_ge(max_ready, cc + 1)
                    if cc >= 4:
                        act.wait_ge(probs_t, unit_of_comp[cc - 4] + 1)
                    act.activation(unit(U_P + cc % 4)[:, 0:width], ps[:, cc % 4, 0:width], ACT.Exp,
                                   bias=exp_bias(cc), scale=scale, accum_out=exp_sum(cc)).then_inc(exp_ready, 1)

            def copy_t(m):
                u = unit0[l] + m
                _, _, qb, is_ctx = us[m]
                v = u // 2
                act.wait_ge(probs_t, u + 1)
                if v >= 2:
                    act.wait_ge(attn_t, v - 1)
                kts = 2 if is_ctx else 4
                pt = arena[:, U_PT + v % 2 * 2:U_PT + v % 2 * 2 + 2, :].rearrange("p a (t q) -> p (a t) q", q=256)
                act.copy(pt[:, 0:kts, qb * P:(qb + 1) * P],
                         ps[:, 4 + u % 2, 0:kts * P].rearrange("p (t q) -> p t q", q=P)).then_inc(probs_t_copied, 1)

            def copy_out(m):
                br, hd, _, is_ctx = us[m]
                v = (unit0[l] + m) // 2
                act.wait_ge(attn_t, v + 1)
                r, q0 = hd % 2 * 64, LAT if is_ctx else 0
                act.copy(y[r:r + 64, 2 * br + hd // 2, q0:q0 + LAT], ps[r:r + 64, 6 + v % 2, 0:LAT]).then_inc(attn_ready, 1)

            exps(0)
            for m in range(len(us)):
                if m + 1 < len(us):
                    exps(m + 1)
                copy_t(m)
                if m % 2 == 0 and m >= 2:
                    copy_out(m - 1)
            copy_out(len(us) - 1)
            act.wait_ge(attn_ready, (unit0[l] + len(us)) // 2)
            for p in range(2):
                act.activation(sq[:, p, 0:n], y[:, 2 * DIFF_BR + p, 0:n], ACT.Square).then_inc(dsq_ready, 1)
            for p in range(2):
                act.wait_ge(dsum_ready, 2 * l + p + 1)
                root(sq[:, p, 0:n], ps[:, p, 0:n], 64).then_inc(dstd_ready, 1)
            act.wait_ge(dnorm_ready, 2 * (l + 1))
            act.copy(y_h[:, :, 0:n], y[:, :, 0:n]).then_inc(y_h_ready, 1)
            b = base[l, 1, "gb"]

            def body(i):
                for c in range(4):
                    for what in range(5):
                        s = 5 * c + what
                        split(b, i, 20, s)
                        if what != 2:
                            gate = what - (what > 2)
                            act.wait_ge(w_used, i * 20 + (b + s + 1))
                            if gate + 4 * c + l * 32 >= 4 or not isinstance(i, int):
                                act.wait_ge(gated, i * 16 + (l * 32 + 4 * c + gate - 3))
                            act.activation(tanh_buf[gate][:, 0:n], ps[:, 4 + gate, 0:n], ACT.Tanh, scale=0.5).then_inc(tanh_ready, 1)
                    act.wait_ge(gated, i * 16 + (l * 32 + 4 * c + 4))
                    act.copy(m_h[:, bass.ds(i * 4 + c, 1), 0:n].rearrange("p a n -> p (a n)"), macc[c % 2][:, 0:n]).then_inc(m_h_ready, 1)
            body(0)
            with act.Fori(1, 2) as i:
                body(i)
            b = base[l, 1, "mixout"]
            u = update_index(l, 1)

            def out_body(i):
                for c in range(4):
                    split(b, i, 4, c)
                    squares(u, i, 4, c, n)
            steps(act, 2, 4, out_body)

        for l in range(DEPTH):
            for sub in range(3):
                ada_phase(l, sub)
                norm(3 * l + sub, tokens(l, sub))
                if sub != 1:
                    ffn_phase(l, sub, 2 * l + sub // 2)
                else:
                    mix_phase(l)
        norm(3 * DEPTH, LAT)
        for tt in range(2):
            for a in range(2):
                act.wait_ge(fin_t, 2 * tt + a + 1)
                act.copy(out_tok[:, tt, a * 512:(a + 1) * 512], ps[:, 2 * tt + a, :]).then_inc(fin_copied, 1)

    @block.vector
    def _(dve):
        def split(b, i, body_slots, s):
            at = (b + s + AHEAD) % RING
            dve.wait_ge(w_hi_ready, i * body_slots + (b + s + AHEAD + 1))
            if rotary_slot(b, i, s):
                dve.tensor_tensor(four(w_lo, at), four_of(raw, at), four(w_hi, at), ALU.subtract).then_inc(w_lo_ready, 1)
                return
            dve.tensor_tensor(w_lo[:, at], raw[:, at], w_hi[:, at], ALU.subtract).then_inc(w_lo_ready, 1)

        def maybe_split(b, i, body_slots, s):
            if not isinstance(i, int) or i * body_slots + b + s + AHEAD < total_slots:
                split(b, i, body_slots, s)

        def add_squares(u, i, step, c, n):
            dve.wait_ge(sq_ready, i * step + (u * KT + c + 1))
            dve.wait_ge(ssq_ready, i * step + (u * KT + c))
            dve.tensor_tensor(ssq[:, 0:n], ssq[:, 0:n], sq[:, c % 2, 0:n], ALU.add).then_inc(ssq_ready, 1)

        dve.memset(eps_col, EPS).then_inc(eps_set, 1)
        dve.wait_ge(cols_t_ready, 1)
        dve.tensor_copy(cols[:, 0:P + 100], ps[:, 6, 0:P + 100]).then_inc(cols_ready, 1)
        dve.wait_ge(cols_ready, 1)
        for l in range(DEPTH):
            dve.tensor_scalar(subln_g[l], subln_col(l), 1.0 - LAM_INIT[l], None, ALU.mult).then_inc(cols_ready, 1)
        dve.wait_ge(s4_ready, 1)
        dve.tensor_tensor(s4[:, :, 2:4].rearrange("p k w -> p w k"), sc[:, :, :],
                          s4[:, :, 0:2].rearrange("p k w -> p w k"), ALU.subtract).then_inc(s4_ready, 1)
        for m in range(AHEAD):
            split(-AHEAD, 0, 0, m)
        dve.wait_ge(lam_loaded, 16)
        dl = lam_row[:, 0:256].rearrange("o (a b d) -> o a b d", a=4, b=2)
        dve.tensor_tensor(lam_row[:, 256:384].rearrange("o (a d) -> o a d", a=4), dl[:, :, 0, :], dl[:, :, 1, :], ALU.mult).then_inc(lam_step, 1)
        dve.wait_ge(lam_step, 1)
        dve.reduce_sum(lam_row[:, 384:388], lam_row[:, 256:384].rearrange("o (a d) -> o a d", a=4), AX_X).then_inc(lam_step, 1)
        for k in range(KT):
            dve.wait_ge(sq_ready, k + 1)
            if k == 0:
                dve.tensor_copy(ssq[:, :], sq[:, 0, :]).then_inc(ssq_ready, 1)
            else:
                dve.wait_ge(ssq_ready, k)
                dve.tensor_tensor(ssq[:, :], ssq[:, :], sq[:, k % 2, :], ALU.add).then_inc(ssq_ready, 1)
        dve.wait_ge(lam_exp, 1)
        e = lam_row[:, 392:396].rearrange("o (l a) -> o l a", l=2)
        dve.tensor_tensor(lam_row[:, 400:402], e[:, :, 1], e[:, :, 0], ALU.subtract).then_inc(lam_step, 1)
        dve.wait_ge(lam_bc, 1)
        for l in range(DEPTH):
            dve.tensor_scalar(neg_lam[l], ps[:, 5, l:l + 1], -LAM_INIT[l], None, ALU.add).then_inc(lam_ready, 1)

        def ada_phase(l, sub):
            b = base[l, sub, "ada"]

            def body(i):
                for s in range(4):
                    split(b, i, 4, s)
            steps(dve, ADA_SLOTS // 4, 4, body)
            m = mods[:, (3 * l + sub) % 2]
            k = 3 * l + sub
            acc = ps[:, ADA_BANK, 0:96].rearrange("p (n c) -> p n c", c=4)
            dve.wait_ge(w_used, b + ADA_SLOTS)
            dve.tensor_copy(mod_tmp[:, :, :], acc[:, :, 0:2]).then_inc(mod_step, 1)
            dve.wait_ge(mod_step, 3 * k + 1)
            dve.tensor_tensor(mod_tmp[:, :, :], mod_tmp[:, :, :], acc[:, :, 2:4], ALU.add).then_inc(mod_step, 1)
            dve.wait_ge(mod_step, 3 * k + 2)
            dve.tensor_tensor(m, mod_tmp[:, :, :], ada_b_cols(l, sub).unsqueeze(2).to_broadcast([P, 24, 2]), ALU.add).then_inc(mod_step, 1)
            dve.wait_ge(mod_step, 3 * k + 3)
            dve.scalar_tensor_tensor(out=m[:, 8:16, :], in0=m[:, 8:16, :], scalar=1.0,
                                     in1=norm_g_cols(l, sub).unsqueeze(2).to_broadcast([P, KT, 2]), op0=ALU.add, op1=ALU.mult)
            dve.tensor_scalar(m[:, 16:24, :], m[:, 16:24, :], 0.5, None, ALU.mult).then_inc(mods_ready, 1)

        def norm(l, sub):
            q, n = 3 * l + sub, tokens(l, sub)
            m = mods[:, q % 2]
            dve.wait_ge(mods_ready, q + 1)
            dve.wait_ge(std_ready, q + 1)
            dve.reciprocal(rstd[:, 0:n], rstd[:, 0:n]).then_inc(rstd_ready, 1)

            def modulate(k):
                dve.wait_ge(xn_ready, q * KT + k + 1)
                if k >= 2:
                    dve.wait_ge(xl_ready, q * KT + k - 1)
                for w, cols_of in halves(n):
                    last = dve.tensor_scalar(norm_tmp[2 + k % 2][:, cols_of], norm_tmp[k % 2][:, cols_of],
                                             m[:, 8 + k, w:w + 1], m[:, k, w:w + 1], ALU.mult, ALU.add)
                last.then_inc(xm_ready, 1)

            modulate(0)
            for k in range(KT):
                if k + 1 < KT:
                    modulate(k + 1)
                dve.wait_ge(xh_ready, q * KT + k + 1)
                dve.tensor_tensor(xl[:, k, 0:n], norm_tmp[2 + k % 2][:, 0:n], xh[:, k, 0:n], ALU.subtract).then_inc(xl_ready, 1)

        def update(l, sub, i, c, bank, n, used):
            u = update_index(l, sub)
            m = mods[:, (3 * l + sub) % 2]
            tile = i * 4 + c
            dve.wait_ge(w_used, used)
            hk = h[:, bass.ds(tile, 1), :].rearrange("p a n -> p (a n)")
            for w, cols_of in halves(n):
                gate = m[:, bass.ds(tile + 16, 1), w:w + 1].rearrange("p a n -> p (a n)")
                last = dve.scalar_tensor_tensor(out=hk[:, cols_of], in0=ps[:, bank, cols_of], scalar=gate,
                                                in1=hk[:, cols_of], op0=ALU.mult, op1=ALU.add)
            last.then_inc(h_ready, 1)

        def reset_squares(l, sub, n):
            dve.memset(ssq[:, 0:n], 0.0).then_inc(ssq_reset, 1)
            dve.wait_ge(ssq_reset, update_index(l, sub))

        def ffn_phase(l, sub, f):
            n = tokens(l, sub)
            b = base[l, sub, "in"]

            def body(i):
                for p in range(2):
                    split(b, i, 4, 2 * p)
                    split(b, i, 4, 2 * p + 1)
                    dve.wait_ge(w_used, i * 4 + (b + 2 * p + 2))
                    dve.wait_ge(silu_ready, i * 2 + (f * HT + p + 1))
                    if f * HT + p >= 2 or not isinstance(i, int):
                        dve.wait_ge(hid_l_ready, i * 2 + (f * HT + p - 1))
                    dve.tensor_tensor(prod[:, p, 0:n], silu[:, p, 0:n], ps[:, 2 * p + 1, 0:n], ALU.mult).then_inc(prod_ready, 1)
                    dve.wait_ge(hid_h_ready, i * 2 + (f * HT + p + 1))
                    tile = bass.ds(i * 2 + p, 1)
                    dve.tensor_tensor(hid_l[:, tile, 0:n].rearrange("p a n -> p (a n)"), prod[:, p, 0:n],
                                      hid_h[:, tile, 0:n].rearrange("p a n -> p (a n)"), ALU.subtract).then_inc(hid_l_ready, 1)
            body(0)
            with dve.Fori(1, HT // 2) as i:
                body(i)
            b = base[l, sub, "out"]
            reset_squares(l, sub, n)

            def out_body(i):
                for c in range(4):
                    for part in range(3):
                        maybe_split(b, i, 12, 3 * c + part)
                    update(l, sub, i, c, 4 + c, n, i * 12 + (b + 3 * c + 3))
                    add_squares(update_index(l, sub), i, 4, c, n)
            steps(dve, 2, 12, out_body, peel=(l, sub) == (DEPTH - 1, 2))

        rope = [0]

        def rotate(dst, partner, rows_of):
            a, c = sq[rows_of, 0, 0:LAT], sq[rows_of, 1, 0:LAT]
            dve.tensor_tensor(a, partner, sin[rows_of, :], ALU.mult).then_inc(rope_step, 1)
            dve.tensor_tensor(c, dst, cos[rows_of, :], ALU.mult).then_inc(rope_step, 1)
            rope[0] += 2
            dve.wait_ge(rope_step, rope[0])
            rope[0] += 1
            return dve.tensor_tensor(dst, a, c, ALU.add).then_inc(rope_step, 1)

        def mix_phase(l):
            n = query_tokens(l)
            every = slice(0, P)
            b = base[l, 1, "proj"]
            for s in range(PROJ_SLOTS):
                split(b, 0, 0, s)
            for j, key in enumerate([("dq", 0), ("dq", 1), ("dk", 0), ("dk", 1), ("kr", 0)]):
                dve.wait_ge(rot_ready, 5 * l + j + 1)
                if j:
                    dve.wait_ge(rope_step, rope[0])
                rotate(unit(feat[key])[:, 0:LAT], ps[:, 2 + j, 0:LAT], every)
            dve.wait_ge(rope_step, rope[0])
            for hd in range(4):
                last = dve.tensor_copy(unit(MK + hd)[64:96, :], unit(feat["kr", 0])[64:96, :])
            last.then_inc(kr_spread, 1)
            dve.wait_ge(mstd_ready, l + 1)
            dve.reciprocal(unit(U_P + 1)[:, 0:n], unit(U_P)[:, 0:n])
            dve.reciprocal(unit(U_P + 3), unit(U_P + 2)).then_inc(mrstd_ready, 1)
            dve.wait_ge(mrstd_ready, l + 1)
            for p in range(2):
                qa = unit(feat["qa", p])[:, 0:n]
                dve.scalar_tensor_tensor(out=qa, in0=qa, scalar=q_g_col(l, p), in1=unit(U_P + 1)[:, 0:n], op0=ALU.mult, op1=ALU.mult)
            kva = unit(feat["kva", 0])
            dve.scalar_tensor_tensor(out=kva, in0=kva, scalar=kv_g_col(l), in1=unit(U_P + 3), op0=ALU.mult, op1=ALU.mult).then_inc(mnorm_ready, 1)
            rows_of = slice(64, 96)
            for hd in range(4):
                dve.wait_ge(mrot_ready, 4 * l + hd + 1)
                dve.wait_ge(rope_step, rope[0])
                rotate(unit(MQ + hd)[rows_of, 0:LAT], ps[rows_of, 4 + hd, 0:LAT], rows_of)
            us = units[l]

            def maxima(m):
                br, hd, qb, is_ctx = us[m]
                width = CTX if is_ctx else TOK
                for cc in comp_at[l, m]:
                    bank = ps[:, cc % 4, 0:width]
                    dve.wait_ge(score_ready, cc + 1)
                    if br == NA_BR and not is_ctx:
                        dve.wait_ge(bias_ready, 8 * (l + 1))
                        dve.tensor_tensor(bank[:, 0:LAT], bank[:, 0:LAT],
                                          bias[:, hd, qb].rearrange("p i k -> p (i k)"), ALU.add).then_inc(biased, 1)
                        dve.wait_ge(biased, na_before[l, m] + 1)
                    if cc >= 8:
                        dve.wait_ge(exp_ready, cc - 7)
                    dve.tensor_reduce(neg_max(cc), bank, AX_X, ALU.max, negate=True).then_inc(max_step, 1)
                    dve.wait_ge(max_step, cc + 1)
                    scale = {DIFF_BR: 32 ** -0.5, MLA_BR: 96 ** -0.5, NA_BR: 1.0}[br]
                    dve.tensor_scalar(exp_bias(cc), neg_max(cc), scale, None, ALU.mult).then_inc(max_ready, 1)

            def normalise(m):
                br, _, _, is_ctx = us[m]
                width = CTX if is_ctx else TOK
                cs = comp_at[l, m]
                for cc in cs:
                    dve.wait_ge(exp_ready, cc + 1)
                    dve.reciprocal(exp_inv(cc), exp_sum(cc)).then_inc(inv_step, 1)
                dve.wait_ge(inv_step, inv_count(l, m) - (br == DIFF_BR) * 2)
                first = unit(U_P + cs[0] % 4)[:, 0:width]
                if br == DIFF_BR:
                    second = unit(U_P + cs[1] % 4)[:, 0:width]
                    dve.tensor_tensor(exp_inv2(cs[0]), exp_inv(cs[1]), neg_lam[l], ALU.mult).then_inc(inv_step, 1)
                    dve.tensor_scalar(first, first, exp_inv(cs[0]), None, ALU.mult).then_inc(inv_step, 1)
                    dve.wait_ge(inv_step, inv_count(l, m))
                    dve.scalar_tensor_tensor(out=first, in0=second, scalar=exp_inv2(cs[0]), in1=first,
                                             op0=ALU.mult, op1=ALU.add).then_inc(probs_ready, 1)
                else:
                    dve.tensor_scalar(first, first, exp_inv(cs[0]), None, ALU.mult).then_inc(probs_ready, 1)

            if l == 0:
                dve.wait_ge(lam_ready, 2)
            maxima(0)
            for m in range(len(us)):
                if m + 1 < len(us):
                    maxima(m + 1)
                normalise(m)
            for p in range(2):
                dve.wait_ge(dstd_ready, 2 * l + p + 1)
                dve.reciprocal(sq[:, p, 0:n], sq[:, p, 0:n]).then_inc(dinv_ready, 1)
                dve.wait_ge(dinv_ready, 2 * l + p + 1)
                yd = y[:, 2 * DIFF_BR + p, 0:n]
                dve.scalar_tensor_tensor(out=yd, in0=yd, scalar=subln_g[l], in1=sq[:, p, 0:n], op0=ALU.mult, op1=ALU.mult).then_inc(dnorm_ready, 1)
            dve.wait_ge(y_h_ready, l + 1)
            dve.tensor_tensor(y_l[:, :, 0:n], y[:, :, 0:n], y_h[:, :, 0:n], ALU.subtract).then_inc(y_l_ready, 1)
            b = base[l, 1, "gb"]
            dve.wait_ge(y_l_ready, l + 1)

            def term(i, c, br):
                g = l * 32 + 4 * c + br
                acc = macc[c % 2][:, 0:n]
                dve.wait_ge(tanh_ready, i * 16 + (g + 1))
                dst = acc if br == 0 else mtmp[:, 0:n]
                if br == 0:
                    if l * KT + c >= 2 or not isinstance(i, int):
                        dve.wait_ge(m_l_ready, i * 4 + (l * KT + c - 1))
                    ins = dve.scalar_tensor_tensor(out=dst, in0=tanh_buf[br][:, 0:n], scalar=1.0, in1=ps[:, br, 0:n], op0=ALU.add, op1=ALU.mult)
                    ins.then_inc(gated, 1)
                    dve.wait_ge(gated, i * 16 + (g + 1))
                else:
                    ins = dve.scalar_tensor_tensor(out=dst, in0=tanh_buf[br][:, 0:n], scalar=1.0, in1=ps[:, br, 0:n], op0=ALU.add, op1=ALU.mult)
                    ins.then_inc(macc_ready, 1)
                    dve.wait_ge(macc_ready, i * 12 + (l * 24 + 3 * c + br))
                    dve.tensor_tensor(acc, acc, dst, ALU.add).then_inc(gated, 1)
                    dve.wait_ge(gated, i * 16 + (g + 1))

            def body(i):
                for c in range(4):
                    for what in range(5):
                        s = 5 * c + what
                        split(b, i, 20, s)
                        if what == 2:
                            dve.wait_ge(w_used, i * 20 + (b + s + 1))
                            term(i, c, 0)
                            term(i, c, 1)
                        elif what > 2:
                            term(i, c, what - 1)
                    tile = bass.ds(i * 4 + c, 1)
                    dve.wait_ge(m_h_ready, i * 4 + (l * KT + c + 1))
                    dve.tensor_tensor(m_l[:, tile, 0:n].rearrange("p a n -> p (a n)"), macc[c % 2][:, 0:n],
                                      m_h[:, tile, 0:n].rearrange("p a n -> p (a n)"), ALU.subtract).then_inc(m_l_ready, 1)
            body(0)
            with dve.Fori(1, 2) as i:
                body(i)
            b = base[l, 1, "mixout"]
            reset_squares(l, 1, n)

            def out_body(i):
                for c in range(4):
                    split(b, i, 4, c)
                    update(l, 1, i, c, 4 + c, n, i * 4 + (b + c + 1))
                    add_squares(update_index(l, 1), i, 4, c, n)
            steps(dve, 2, 4, out_body)

        def inv_count(l, m):
            total = 0
            for ll in range(l + 1):
                for mm, u in enumerate(units[ll]):
                    if (ll, mm) > (l, m):
                        break
                    total += 4 if u[0] == DIFF_BR else 1
            return total

        for l in range(DEPTH):
            for sub in range(3):
                ada_phase(l, sub)
                norm(l, sub)
                if sub != 1:
                    ffn_phase(l, sub, 2 * l + sub // 2)
                else:
                    mix_phase(l)
        q = 3 * DEPTH
        dve.wait_ge(std_ready, q + 1)
        dve.reciprocal(rstd[:, 0:LAT], rstd[:, 0:LAT]).then_inc(rstd_ready, 1)
        dve.wait_ge(rstd_ready, q + 1)
        for k in range(KT):
            dve.scalar_tensor_tensor(out=norm_tmp_final(k), in0=h[:, k, 0:LAT], scalar=final_g[:, k:k + 1],
                                     in1=rstd[:, 0:LAT], op0=ALU.mult, op1=ALU.mult).then_inc(fin_ready, 1)


def arena_offset(nc, arena):
    return nc.lookup_mloc(arena).addr


_INPUTS = ["x", "c", "ctx", "c_ctx", "ada_w", "ada_b", "norm_g", "ffn_w_in", "ffn_w_out", "mix_w_in",
           "pool_w", "pool_scale", "na_rpb", "diff_lambda", "diff_subln_g", "mla_q_norm_g",
           "mla_kv_norm_g", "mla_w_qb", "mla_w_kvb", "branch_w_out", "mix_w_out", "final_norm_g"]


def kernel(**inputs):
    import concourse.bacc as bacc
    from concourse.bass_utils import run_bass_kernel_spmd

    nc = bacc.Bacc("TRN2", target_bir_lowering=False, num_devices=1)
    arrays = {name: np.ascontiguousarray(inputs[name]) for name in _INPUTS}
    arrays["tables"] = host_constants()
    arrays["pool_mats"] = pool_matrices()
    aps = {name: nc.dram_tensor(f"in_{name}", a.shape, mybir.dt.from_np(a.dtype), kind="ExternalInput").ap()
           for name, a in arrays.items()}
    aps["out"] = nc.dram_tensor("out", (1, LAT, D), F32, kind="ExternalOutput").ap()
    backbone(nc, **aps)
    r = run_bass_kernel_spmd(nc, [{f"in_{name}": a for name, a in arrays.items()}], core_ids=[0])
    return r.results[0]["out"]
```

```python
from contextlib import ExitStack

import numpy as np

import concourse.bass as bass
from concourse import mybir

F32 = mybir.dt.float32
F32R = mybir.dt.float32r
ALU = mybir.AluOpType
ACT = mybir.ActivationFunctionType
AX_X = mybir.AxisListType.X

P = 128
D = 1024
KT = D // P
LAT = 256
CTX = 256
TOK = LAT + CTX
DEPTH = 2
FFN = 2816
HT = FFN // P
EPS = 1e-6
GRID_W = 64
NA_ROWS, NA_COLS = 8, 16
RPB_ROWS, RPB_COLS = 2 * NA_ROWS - 1, 2 * NA_COLS - 1
GRID_ROWS = LAT // GRID_W
RPB_USED = 2 * GRID_ROWS - 1
POOL_WINDOWS = (2, 4, 8, 16)
ROT = 32
ROPE_STEPS = 3 * (5 + 4)
POOL_TILES = (2, 5, 7)
LAM_INIT = [0.8 - 0.6 * float(np.exp(-0.3 * l)) for l in range(DEPTH)]

RING = 4
AHEAD = 3

PROJ = (
    [("qa", c, 1792 + c * P) for c in range(2)]
    + [("kva", 0, 2048), ("kr", 0, 2176)]
    + [("dq", c, 1024 + c * P) for c in range(2)]
    + [("dk", c, 1280 + c * P) for c in range(2)]
    + [("pool", c, c * P) for c in range(2)]
    + [("dv", c, 1536 + c * P) for c in range(2)]
)
PROJ_NA = (
    [("nq", c, 256 + c * P) for c in range(2)]
    + [("nk", c, 512 + c * P) for c in range(2)]
    + [("nv", c, 768 + c * P) for c in range(2)]
)
PROJ_SLOTS = len(PROJ)
ROTATED = [("dq", 0), ("dq", 1), ("dk", 0), ("dk", 1), ("kr", 0)]
GATE_COL = 2208
TOKEN_MAJOR = ("pool", "dv", "nv")
QUERY_ONLY = ("pool", "qa", "dq", "nq")
POOL_BR, NA_BR, DIFF_BR, MLA_BR = range(4)

OUT_PARTS = ((0, 8), (8, 8), (16, 6))
ADA_GROUP = 256
ADA_GROUPS = 3 * D // ADA_GROUP
ADA_SLOTS = 2 * ADA_GROUPS
ADA_ROWS = 4
ADA0_PLACES = 7
ADA0_FIRST = 2 * D // ADA_GROUP


def mixing_stages():
    def gated(br):
        out = []
        for half in range(2):
            out += [("gate", br, 4 * half + n) for n in range(4)] + [("branch", br, half)]
        return out

    def ada(first, last):
        return [("ada", n) for n in range(first, last)]

    def woven(a, b):
        out = []
        for n, x in enumerate(a):
            out += [x]
            if x[0] == "proj" and PROJ_NA[x[1]][:2] == ("nv", 0):
                continue
            out += b[len([y for y in out if y in b]):(n + 1) * len(b) // len(a)]
        return out

    return [
        (DIFF_BR, woven(gated(POOL_BR), ada(0, 8))),
        (MLA_BR, woven([("proj", n) for n in range(len(PROJ_NA))] + gated(DIFF_BR), ada(8, 16))),
        (NA_BR, woven(gated(MLA_BR), ada(16, 24))),
        (None, gated(NA_BR)),
    ]


def out_slots(l, sub):
    return 3 if (l, sub) == (DEPTH - 1, 2) else 6


def slot_bases():
    base, at = {}, 0
    for l in range(DEPTH):
        for sub in range(3):
            phases = ([("proj", PROJ_SLOTS), ("mix", sum(len(items) for _, items in mixing_stages())), ("mixout", KT)]
                      if sub == 1 else [("in", 2 * HT), ("out", out_slots(l, sub) * KT)])
            for name, n in phases:
                base[l, sub, name] = at
                at += n
    return base, at


def attention_units(l):
    units = []
    for br in (DIFF_BR, MLA_BR, NA_BR):
        for ctx in ((False, True) if l < DEPTH - 1 else (False,)):
            for h in range(4):
                units += [(br, h, b, ctx) for b in range(2)]
    return units


def host_constants():
    t = np.arange(LAT)
    pos = np.stack([t // GRID_W, t % GRID_W]).astype(np.float32)
    half, quarter = ROT // 2, ROT // 4
    inv = (np.float32(10000.0) ** (-np.arange(0, half, 2, dtype=np.float32) / np.float32(half))).astype(np.float32)
    cos = np.zeros((P, LAT), np.float32)
    sin = np.zeros((P, LAT), np.float32)
    perm = np.zeros((P, P), np.float32)
    for f in range(P):
        a, r = (f % ROT) // half, f % half
        ang = pos[a] * inv[r % quarter]
        cos[f], sin[f] = np.cos(ang), np.sin(ang)
        if r < quarter:
            perm[f + quarter, f] = -1.0
        else:
            perm[f - quarter, f] = 1.0
    ident = np.eye(P, dtype=np.float32)
    blocks = np.kron(np.eye(2), np.ones((64, 64))).astype(np.float32)
    ones = np.ones((P, P), np.float32)
    j = np.arange(P) % GRID_W
    start = np.clip(j - NA_COLS // 2, 0, GRID_W - NA_COLS)[:, None]
    key = np.arange(GRID_W)[None, :]
    mask = np.where((key >= start) & (key < start + NA_COLS), 0.0, -1e30).astype(np.float32)
    pair = np.tile(np.eye(2, dtype=np.float32), (P // 2, 1))
    return np.concatenate([cos, sin, perm, ident, blocks, ones, mask, pair], axis=1)


def pool_matrices():
    out = np.zeros((LAT, 4, LAT), np.float32)
    for g, w in enumerate(POOL_WINDOWS):
        for i in range(LAT):
            lo, hi = max(i - w // 2, 0), min(i - w // 2 + w, LAT)
            out[lo:hi, g, i] += np.float32(1.0) / np.float32(hi - lo)
            out[i, g, i] -= 1.0
    return np.ascontiguousarray(out.reshape(2, P, 4, LAT).transpose(1, 2, 0, 3))


def backbone(nc, x, c, ctx, c_ctx, ada_w, ada_b, norm_g, ffn_w_in, ffn_w_out, mix_w_in, pool_w,
             pool_scale, na_rpb, diff_lambda, diff_subln_g, mla_q_norm_g, mla_kv_norm_g, mla_w_qb,
             mla_w_kvb, branch_w_out, mix_w_out, final_norm_g, tables, pool_mats, out):
    with ExitStack() as stack:
        build(nc, stack, locals())


def build(nc, stack, t):
    base, total_slots = slot_bases()

    def sb(name, shape, dt=F32):
        return stack.enter_context(nc.sbuf_tensor(name, shape, dt))

    def sem(name):
        return stack.enter_context(nc.semaphore(name))

    raw = sb("w_raw", [P, RING, KT, P])
    w_hi = sb("w_hi", [P, RING, KT, P], F32R)
    w_lo = sb("w_lo", [P, RING, KT, P], F32R)
    h = sb("h", [P, KT, TOK])
    xh = sb("xh", [P, KT, TOK], F32R)
    xl = sb("xl", [P, KT, TOK], F32R)
    work = sb("work", [P, 4, TOK])
    silu, prod = work[:, 0:2, :], work[:, 2:4, :]
    bias = work[:, :, :].rearrange("p h (b i k) -> p h b i k", b=2, i=GRID_ROWS)
    ssq = sb("ssq", [P, TOK])
    sq = sb("sq", [P, 2, TOK])
    rstd = sb("rstd", [P, TOK])
    tab = sb("tab", [P, 2 * LAT + 4 * P + GRID_W + 2])
    cos, sin = tab[:, 0:LAT], tab[:, LAT:2 * LAT]
    perm, ident, blocks, ones = [tab[:, 2 * LAT + n * P:2 * LAT + (n + 1) * P] for n in range(4)]
    mask = tab[:, 2 * LAT + 4 * P:2 * LAT + 4 * P + GRID_W]
    pair = tab[0:ADA_ROWS, 2 * LAT + 4 * P + GRID_W:]
    cols = sb("cols", [P, 2 * P])
    s4 = sb("s4", [P, KT, 4], F32R)
    sc = sb("sc", [P, 2, KT])
    mods = sb("mods", [P, 2, 24, 2])
    small = sb("small", [P, 96])
    UNITS = 2 * HT
    arena = sb("arena", [P, UNITS, TOK])
    start_of_arena = arena_offset(nc, arena)

    def view(name, unit, n, dt=F32):
        return nc.alloc_sbuf_tensor_at(name, [P, n, TOK], dt, offset=start_of_arena + unit * TOK * 4)

    hid_h = view("hid_h", 0, HT, F32R)
    hid_l = view("hid_l", HT, HT, F32R)
    feat = {("dq", 0): 0, ("dq", 1): 1, ("dk", 0): 2, ("dk", 1): 3,
            ("nq", 0): 0, ("nq", 1): 1, ("nk", 0): 2, ("nk", 1): 3,
            ("qa", 0): 16, ("qa", 1): 17, ("kva", 0): 18, ("kr", 0): 19}
    tok_unit = {"dv": 4, "nv": 4, "mv": 14, "pool": 30}
    MQ, MK, U_PT, U_P, U_Y, U_MACC = 6, 10, 16, 20, 24, 30
    y_h = view("y_h", 26, 2, F32R)
    y_l = view("y_l", 28, 2, F32R)
    m_h = view("m_h", 0, 8, F32R)
    m_l = view("m_l", 8, 8, F32R)

    def unit(n):
        return arena[:, n, :]

    def token_major(what):
        u = tok_unit[what]
        return arena[:, u:u + 2, :].rearrange("p a (t c) -> p (a t) c", c=256)

    x_tok = arena[:, 0:8, :].rearrange("p (t a) n -> p t (a n)", t=4)
    out_tok = arena[:, 0:4, :].rearrange("p (t a) n -> p t (a n)", t=2)
    rows = arena[:, 8, :].rearrange("p (a n) -> p a n", a=4)
    lam_row = arena[0:1, 9, :]
    norm_tmp = [unit(40 + n) for n in range(4)]
    pool_mat = arena[:, 32:36, :].rearrange("p g (t n) -> p g t n", t=2)
    pooled = arena[:, 36:38, :]
    y = arena[:, U_Y:U_Y + 2, :]
    tanh_buf = [unit(38 + n) for n in range(4)]
    mtmp = [unit(42), unit(43)]
    ada0 = arena[:, 10:38, :].rearrange("p (c a) n -> p c (a n)", c=ADA0_PLACES).rearrange("p c (k n) -> p c k n", k=KT)
    ada0_rows = [unit(38)[0:2, 0:ADA_GROUP], unit(39)[0:2, 0:ADA_GROUP]]
    ada_rows = rstd[0:ADA_ROWS, 0:ADA_GROUP]
    w_qb = silu.rearrange("p a n -> p (a n)")[:, 0:768].rearrange("p (k n) -> p k n", k=2)
    w_kvb = prod[:, 0, :]
    w_pool = prod[:, 1, 0:256].rearrange("p (g n) -> p g n", g=2)

    rpb_rows = nc.dram_tensor("rpb_rows", [DEPTH, 4, RPB_USED, GRID_W, RPB_COLS], F32).ap()
    ps = stack.enter_context(nc.psum_tensor("ps", [P, 8, TOK], F32))
    SUM_BANK, PT_BANK, O_BANK, S_BANKS = 6, 4, 5, 3
    ADA0_BANKS = (4, 7)

    def ada_bank(sub):
        return 3 if sub == 1 else 0

    def ada_b_cols(l, sub):
        return cols[:, l * P + sub * 24:l * P + sub * 24 + 24]

    def norm_g_cols(l, sub):
        return cols[:, 72 + (l * 3 + sub) * KT:72 + (l * 3 + sub + 1) * KT]

    final_g = cols[:, 120:128]
    cond_cols = cols[:, P + 72:P + 88]

    def pool_scale_col(l, p):
        return cols[:, P + 88 + 2 * l + p:P + 89 + 2 * l + p]

    def q_g_col(l, p):
        return cols[:, P + 92 + 2 * l + p:P + 93 + 2 * l + p]

    def kv_g_col(l):
        return cols[:, P + 96 + l:P + 97 + l]

    def subln_col(l):
        return cols[:, P + 98 + l:P + 99 + l]

    eps_col = small[:, 0:1]
    subln_g = [small[:, 1 + l:2 + l] for l in range(DEPTH)]
    neg_lam = [small[:, 3 + l:4 + l] for l in range(DEPTH)]

    def neg_max(comp):
        return small[:, 8 + comp % 8:9 + comp % 8]

    def exp_bias(comp):
        return small[:, 16 + comp % 8:17 + comp % 8]

    def exp_sum(comp):
        return small[:, 24 + comp % 8:25 + comp % 8]

    def exp_inv(comp):
        return small[:, 32 + comp % 8:33 + comp % 8]

    def exp_inv2(comp):
        return small[:, 40 + comp % 8:41 + comp % 8]

    def scaled_ready(eng, q, k):
        if k in POOL_TILES:
            eng.wait_ge(pool_scaled, q * len(POOL_TILES) + POOL_TILES.index(k) + 1)
        else:
            eng.wait_ge(dve_scaled, q * (KT - len(POOL_TILES)) + k - len([j for j in POOL_TILES if j < k]) + 1)

    def norm_tmp_final(k):
        return unit(8 + k // 2)[:, k % 2 * LAT:(k % 2 + 1) * LAT]

    w_loaded = [sem(f"w_loaded{s}") for s in range(RING)]
    w_hi_ready, w_lo_ready = sem("w_hi_ready"), sem("w_lo_ready")
    w_used = sem("w_used")
    in_loaded, rows_loaded, tab_loaded, lam_loaded = sem("in_loaded"), sem("rows_loaded"), sem("tab_loaded"), sem("lam_loaded")
    consts_set, eps_set, ssq_reset = sem("consts_set"), sem("eps_set"), sem("ssq_reset")
    xt_ready, xt_copied = sem("xt_ready"), sem("xt_copied")
    cols_t_ready, cols_ready, cond_ready, s4_ready = sem("cols_t_ready"), sem("cols_ready"), sem("cond_ready"), sem("s4_ready")
    lam_step, lam_exp, lam_bc, lam_ready = sem("lam_step"), sem("lam_exp"), sem("lam_bc"), sem("lam_ready")
    ada0_rows_ready, ada_rows_copied = sem("ada0_rows_ready"), sem("ada_rows_copied")
    ada_cols_ready, mod_step, mods_ready, gates_ready = [sem(n) for n in ("ada_cols_ready", "mod_step", "mods_ready", "gates_ready")]
    h_ready, sq_ready, ssq_ready = sem("h_ready"), sem("sq_ready"), sem("ssq_ready")
    sums_ready, std_ready, rstd_ready = sem("sums_ready"), sem("std_ready"), sem("rstd_ready")
    dve_scaled, pool_step, pool_scaled = sem("dve_scaled"), sem("pool_step"), sem("pool_scaled")
    xh_ready, xl_ready = sem("xh_ready"), sem("xl_ready")
    silu_ready, prod_ready, hid_h_ready, hid_l_ready = sem("silu_ready"), sem("prod_ready"), sem("hid_h_ready"), sem("hid_l_ready")
    mix_loaded, pool_loaded, bias_loaded, bias_ready = sem("mix_loaded"), sem("pool_loaded"), sem("bias_loaded"), sem("bias_ready")
    rpb_stored = sem("rpb_stored")
    proj_ready = sem("proj_ready")
    pooled_t, pooled_ready, pool_y_t, y_pool_ready = sem("pooled_t"), sem("pooled_ready"), sem("pool_y_t"), sem("y_pool_ready")
    msq_ready, msum_ready, mstd_ready, mrstd_ready, mnorm_ready = [sem(n) for n in ("msq_ready", "msum_ready", "mstd_ready", "mrstd_ready", "mnorm_ready")]
    rot_ready, rope_step = sem("rot_ready"), sem("rope_step")

    mla_t, mla_ready, kr_spread, mrot_ready = [sem(n) for n in ("mla_t", "mla_ready", "kr_spread", "mrot_ready")]
    score_ready, biased, max_step, max_ready = [sem(n) for n in ("score_ready", "biased", "max_step", "max_ready")]
    exp_ready, inv_step, probs_ready = [sem(n) for n in ("exp_ready", "inv_step", "probs_ready")]
    probs_t, probs_t_copied, attn_t, attn_ready = [sem(n) for n in ("probs_t", "probs_t_copied", "attn_t", "attn_ready")]
    dsq_ready, dsum_ready, dstd_ready, dinv_ready, dnorm_ready = [sem(n) for n in ("dsq_ready", "dsum_ready", "dstd_ready", "dinv_ready", "dnorm_ready")]
    y_h_ready, y_l_ready = sem("y_h_ready"), sem("y_l_ready")
    ada0_loaded = [sem(f"ada0_loaded{n}") for n in range(ADA0_PLACES)]
    ada0_used = sem("ada0_used")
    branch_t, tanh_ready, gated, macc_ready, m_h_ready, m_l_ready = [sem(n) for n in ("branch_t", "tanh_ready", "gated", "macc_ready", "m_h_ready", "m_l_ready")]
    fin_ready, fin_t, fin_copied, out_stored = [sem(n) for n in ("fin_ready", "fin_t", "fin_copied", "out_stored")]

    def update_index(l, sub):
        return 1 + 3 * l + sub

    def tokens(l, sub):
        return LAT if (l, sub) == (DEPTH - 1, 2) else TOK

    def query_tokens(l):
        return TOK if l < DEPTH - 1 else LAT

    def halves(n):
        return [(0, slice(0, LAT)), (1, slice(LAT, TOK))][:n // LAT]

    units = [attention_units(l) for l in range(DEPTH)]
    unit0 = [0, len(units[0])]
    comp_at, n_comps = {}, 0
    for l in range(DEPTH):
        for n, u in enumerate(units[l]):
            k = 2 if u[0] == DIFF_BR else 1
            comp_at[l, n] = list(range(n_comps, n_comps + k))
            n_comps += k
    unit_of_comp = {cc: unit0[l] + n for (l, n), v in comp_at.items() for cc in v}
    na_before = {}
    seen = 0
    for l in range(DEPTH):
        for n, u in enumerate(units[l]):
            na_before[l, n] = seen
            seen += u[0] == NA_BR and not u[3]

    ada_counts = {(l, sub): ADA_GROUPS + 3 * l + sub for l in range(DEPTH) for sub in range(3)}

    stages = mixing_stages()
    stage_units = [[[n for n, u in enumerate(units[l]) if u[0] == br] for br, _ in stages] for l in range(DEPTH)]
    PROJ_ALL = PROJ_SLOTS + len(PROJ_NA)

    def stage_events(l, k):
        items = stages[k][1]
        slot = base[l, 1, "mix"] + sum(len(it) for _, it in stages[:k])
        us = stage_units[l][k]
        done = 0
        events = []
        for n in range(len(us) + 1):
            upto = (n + 1) * len(items) // (len(us) + 1)
            if n < len(us):
                events.append(("unit", us[n]))
            for m in range(done, upto):
                events.append(("item", slot + m, items[m]))
            done = upto
        if us:
            events.append(("close",))
        first_item = next(m for m, e in enumerate(events) if e[0] == "item")
        if k == 0:
            events[first_item + 1:first_item + 1] = [("pool_y",)]
        elif k == 1:
            events[first_item + 1:first_item + 1] = [("subnorm",), ("split",)]
        elif k > 1:
            events[first_item:first_item] = [("split",)]
        return events

    def bank_uses(l):
        uses, tanhs, gates, projs = {}, 32 * l, 32 * l, PROJ_ALL * l + PROJ_SLOTS
        order = 0
        for k in range(len(stages)):
            for e in stage_events(l, k):
                if e[0] == "pool_y":
                    for p in range(2):
                        uses["pool_y", p] = (order, y_pool_ready, l + 1)
                        order += 1
                elif e[0] == "subnorm":
                    for p in range(2):
                        uses["subnorm", p] = (order, dstd_ready, 2 * l + p + 1)
                        order += 1
                elif e[0] == "item" and e[2][0] == "gate":
                    tanhs += 1
                    uses[e[2]] = (order, tanh_ready, tanhs)
                    order += 1
                elif e[0] == "item" and e[2][0] == "proj":
                    projs += 1
                    uses[e[2]] = (order, proj_ready, projs)
                    order += 1
                elif e[0] == "item" and e[2][0] == "branch":
                    for n in range(4):
                        gates += 1
                        uses["branch", e[2][1], 4 * e[2][2] + n] = (order, gated, gates)
                        order += 1
        return uses

    branch_order = [POOL_BR] + [br for br, _ in stages[:3]]
    uses = [bank_uses(l) for l in range(DEPTH)]
    use_at = [{v[0]: v for v in uses[l].values()} for l in range(DEPTH)]

    def stream_bank(l, key):
        return 6 + uses[l][key][0] % 2

    def bank_free(eng, l, key):
        order = uses[l][key][0]
        if order >= 2:
            _, reader, count = use_at[l][order - 2]
            eng.wait_ge(reader, count)

    def steps(eng, iters, body_slots, body, peel=False):
        if peel:
            for i in range(iters):
                body(i)
        else:
            with eng.Fori(0, iters) as i:
                body(i)

    rotary_slots = {base[l, 1, "proj"] + [what for what, _, _ in PROJ].index("kr") for l in range(DEPTH)}

    def rotary_slot(b, i, s):
        return isinstance(i, int) and b + s + AHEAD in rotary_slots

    def wide(w, at, kt):
        return w[:, at].rearrange("p (k a) n -> p k (a n)", k=kt)

    def four(w, at):
        return w[:, at].rearrange("p k (a n) -> p k a n", n=ROT)

    def four_of(w, at):
        return w[:, at, :, 0:ROT].unsqueeze(2).to_broadcast([P, KT, P // ROT, ROT])

    block = stack.enter_context(nc.Block())

    @block.sync
    def _(sp):
        sp.dma_start(x_tok[:, 0:2, :], t["x"][0].rearrange("(t p) n -> p t n", p=P)).then_inc(in_loaded, 16)
        sp.dma_start(x_tok[:, 2:4, :], t["ctx"][0].rearrange("(t p) n -> p t n", p=P)).then_inc(in_loaded, 16)

        def repeat(first, last, body):
            with sp.Fori(first + 1, last + 1) as r:
                body(lambda m, c: r * m + (c - m))

        def fixed(i):
            return lambda m, c: i * m + c

        def load(b, i, body_slots, s, src, col, kt=KT, shape=None):
            at = (b + s) % RING
            freed = i(body_slots, b + s - RING + 1)
            if not isinstance(freed, int) or freed > 0:
                sp.wait_ge(w_lo_ready, freed)
            dst = wide(raw, at, shape) if shape else raw[:, at, 0:kt, :]
            sp.dma_start(dst, src(col)).then_inc(w_loaded[at], 16)

        def load_ada0(first, last):
            ada = t["ada_w"][0].rearrange("(k p) n -> p k n", p=P)
            for m in range(first, last):
                if m >= ADA0_PLACES:
                    sp.wait_ge(ada0_used, m - ADA0_PLACES + 1)
                sp.dma_start(ada0[:, m % ADA0_PLACES], ada[:, :, m * ADA_GROUP:(m + 1) * ADA_GROUP]).then_inc(ada0_loaded[m % ADA0_PLACES], 16)

        for l in range(DEPTH):
            for sub in range(3):
                nl, nsub = (l, sub + 1) if sub < 2 else (l + 1, 0)
                ada = t["ada_w"][min(nl, DEPTH - 1)].rearrange("(k p) n -> p k n", p=P)
                ada_col = nsub * 3 * D
                if sub != 1:
                    w_in = t["ffn_w_in"][l, sub // 2].rearrange("(k p) n -> p k n", p=P)
                    w_out = t["ffn_w_out"][l, sub // 2].rearrange("(k p) n -> p k n", p=P)
                    b = base[l, sub, "in"]

                    def load_in(i, b=b, w_in=w_in):
                        for s in range(4):
                            load(b, i, 4, s, lambda col: w_in[:, :, bass.ds(col, P)], i(2 * P, s // 2 * P + s % 2 * FFN))
                    if b == 0:
                        load_ada0(0, ADA0_FIRST)
                        load_in(fixed(0))
                        load_ada0(ADA0_FIRST, ADA_GROUPS)
                        repeat(1, HT // 2, load_in)
                    else:
                        repeat(0, HT // 2, load_in)
                    b = base[l, sub, "out"]
                    per = out_slots(l, sub)

                    def load_out(i, b=b, w_out=w_out, ada=ada, per=per, ada_col=ada_col):
                        for c in range(4):
                            for part, (k0, kn) in enumerate(OUT_PARTS):
                                s = per * c + part * (per // 3)
                                if per == 6:
                                    group, k4 = (3 * c + part) // 2, (3 * c + part) % 2 * 4
                                    load(b, i, 24, s, lambda col: ada[:, k4:k4 + 4, bass.ds(col, ADA_GROUP)],
                                         i(6 * ADA_GROUP, ada_col + group * ADA_GROUP), shape=4)
                                    s += 1
                                load(b, i, 4 * per, s, lambda col: w_out[:, k0:k0 + kn, bass.ds(col, P)],
                                     i(4 * P, c * P), kn)
                    repeat(0, 2, load_out)
                else:
                    w_mix = t["mix_w_in"][l].rearrange("(k p) n -> p k n", p=P)
                    whole = lambda w: lambda c: w[:, :, c:c + P]
                    b = base[l, sub, "proj"]
                    for s, (_, _, col) in enumerate(PROJ):
                        load(b, fixed(0), 0, s, whole(w_mix), col)
                    s = base[l, sub, "mix"]
                    for _, items in stages:
                        for item in items:
                            if item[0] == "proj":
                                load(s, fixed(0), 0, 0, whole(w_mix), PROJ_NA[item[1]][2])
                            elif item[0] == "gate":
                                load(s, fixed(0), 0, 0, whole(w_mix), GATE_COL + item[1] * D + item[2] * P)
                            elif item[0] == "ada":
                                k4 = item[1] % 2 * 4
                                load(s, fixed(0), 0, 0, lambda col: ada[:, k4:k4 + 4, col:col + ADA_GROUP],
                                     ada_col + item[1] // 2 * ADA_GROUP, shape=4)
                            else:
                                w_branch = t["branch_w_out"][l, item[1]].rearrange("(k p) n -> p k n", p=P)
                                load(s, fixed(0), 0, 0, lambda col: w_branch[:, :, col:col + 4 * P], item[2] * 4 * P, shape=2)
                            s += 1
                    w_mo = t["mix_w_out"][l].rearrange("(k p) n -> p k n", p=P)
                    b = base[l, sub, "mixout"]

                    def load_mo(i, b=b, w_mo=w_mo):
                        for s in range(4):
                            load(b, i, 4, s, lambda col: w_mo[:, :, bass.ds(col, P)], i(4 * P, s * P))
                    repeat(0, 2, load_mo)
        for tt in range(2):
            sp.wait_ge(fin_copied, 2 * (tt + 1))
            sp.dma_start(t["out"][0, tt * P:(tt + 1) * P, :], out_tok[:, tt, :]).then_inc(out_stored, 16)
        sp.wait_ge(out_stored, 32)

    @block.gpsimd
    def _(pool):
        def load_rows(r0, n, a, src):
            pool.dma_start(rows[r0:r0 + n, a, :], src).then_inc(rows_loaded, 16)

        ada_rows = t["ada_b"].rearrange("l (r n) -> l r n", n=P)
        load_rows(0, 72, 0, ada_rows[0])
        load_rows(72, 48, 0, t["norm_g"].rearrange("l s (k n) -> (l s k) n", n=P))
        load_rows(120, 8, 0, t["final_norm_g"].rearrange("(k n) -> k n", n=P))
        load_rows(0, 72, 1, ada_rows[1])
        load_rows(72, 8, 1, t["c"].rearrange("b (k n) -> (b k) n", n=P))
        load_rows(80, 8, 1, t["c_ctx"].rearrange("(k n) -> k n", n=P))
        load_rows(88, 4, 1, t["pool_scale"].rearrange("l (k n) -> (l k) n", n=P))
        load_rows(92, 4, 1, t["mla_q_norm_g"].rearrange("l (k n) -> (l k) n", n=P))
        load_rows(96, 2, 1, t["mla_kv_norm_g"])
        for half in range(2):
            pool.dma_start(rows[98:100, 1, half * 64:half * 64 + 64], t["diff_subln_g"]).then_inc(rows_loaded, 16)
        pool.dma_start(tab[:, :], t["tables"]).then_inc(tab_loaded, 16)
        pool.dma_start(lam_row[:, 0:256], t["diff_lambda"].rearrange("l q d -> (l q d)").rearrange("(a n) -> a n", a=1)).then_inc(lam_loaded, 16)

        for l in range(DEPTH):
            for hd in range(4):
                first = NA_ROWS - GRID_ROWS
                src = t["na_rpb"][l, hd, first:first + RPB_USED, :].unsqueeze(1).to_broadcast([RPB_USED, GRID_W, RPB_COLS])
                pool.dma_start(rpb_rows[l, hd], src).then_inc(rpb_stored, 16)
        pool.wait_ge(rpb_stored, 16 * 4 * DEPTH)

        def norm(q, n):
            pool.wait_ge(mods_ready, q + 1)
            pool.wait_ge(rstd_ready, q + 1)
            for j, k in enumerate(POOL_TILES):
                if k >= 4:
                    pool.wait_ge(xl_ready, q * KT + k - 3)
                tmp = norm_tmp[k % 4]
                pool.tensor_tensor(tmp[:, 0:n], h[:, k, 0:n], rstd[:, 0:n], ALU.mult).then_inc(pool_step, 1)
                pool.wait_ge(pool_step, q * len(POOL_TILES) + j + 1)
                for w, cols_of in halves(n):
                    last = pool.tensor_scalar(tmp[:, cols_of], tmp[:, cols_of], mods[:, q % 2, 8 + k, w:w + 1], None, ALU.mult)
                last.then_inc(pool_scaled, 1)

        for l in range(DEPTH):
            norm(3 * l, tokens(l, 0))
            norm(3 * l + 1, tokens(l, 1))
            pool.dma_start(w_qb, t["mla_w_qb"][l].rearrange("(k p) n -> p k n", p=P)).then_inc(mix_loaded, 16)
            pool.dma_start(w_kvb, t["mla_w_kvb"][l]).then_inc(mix_loaded, 16)
            pool.memset(w_pool, 0.0).then_inc(consts_set, 1)
            pool.wait_ge(consts_set, l + 1)
            for g in range(4):
                r = g % 2 * 64
                pool.dma_start(w_pool[r:r + 64, g // 2, r:r + 64], t["pool_w"][l, g]).then_inc(pool_loaded, 16)
            pool.dma_start(pool_mat, t["pool_mats"]).then_inc(pool_loaded, 16)
            pool.wait_ge(pool_y_t, l + 1)
            for hd in range(4):
                for r in range(GRID_ROWS):
                    src = bass.AP(tensor=rpb_rows.tensor,
                                  offset=(l * 4 + hd) * RPB_USED * GRID_W * RPB_COLS
                                  + (GRID_ROWS - 1 - r) * GRID_W * RPB_COLS + NA_COLS - 1,
                                  ap=[[RPB_COLS - 1, GRID_W], [GRID_W * RPB_COLS, GRID_ROWS], [1, GRID_W]])
                    pool.dma_start(bias[r % 2 * 64:r % 2 * 64 + 64, hd, r // 2], src).then_inc(bias_loaded, 16)
            pool.wait_ge(bias_loaded, 16 * 16 * (l + 1))
            for hd in range(4):
                for b in range(2):
                    pool.tensor_tensor(bias[:, hd, b], bias[:, hd, b],
                                       mask.unsqueeze(1).to_broadcast([P, GRID_ROWS, GRID_W]), ALU.add).then_inc(bias_ready, 1)
            n = query_tokens(l)
            for br in range(1, 4):
                for c in range(KT):
                    pool.wait_ge(gated, 32 * l + 8 * br + c + 1)
                    if br > 1:
                        pool.wait_ge(macc_ready, 24 * l + 8 * (br - 2) + c + 1)
                    acc = unit(U_MACC + c)[:, 0:n]
                    pool.tensor_tensor(acc, acc, mtmp[c % 2][:, 0:n], ALU.add).then_inc(macc_ready, 1)
            norm(3 * l + 2, tokens(l, 2))

    @block.tensor
    def _(pe):
        pe.wait_ge(tab_loaded, 16)
        pe.wait_ge(rows_loaded, 16 * 11)
        pe.transpose(ps[:, 6, 0:P], rows[:, 0, :], ident)
        pe.transpose(ps[:, 6, P:P + 100], rows[0:100, 1, :], ident[0:100, 0:100]).then_inc(cols_t_ready, 1)
        pe.wait_ge(in_loaded, 32)
        for k in range(KT):
            if k >= 4:
                pe.wait_ge(xt_copied, k - 3)
            for tt in range(4):
                last = pe.transpose(ps[:, k % 4, tt * P:(tt + 1) * P], x_tok[:, tt, k * P:(k + 1) * P], ident)
            last.then_inc(xt_ready, 1)
        pe.wait_ge(lam_step, 3)
        pe.matmul(ps[:, 5, 0:2], ones[0:1, :], lam_row[:, 400:402], start=True, stop=True).then_inc(lam_bc, 1)

        def three_passes(dst, hi, lo, mh, ml, first, last):
            pe.matmul(dst, lo, mh, start=first, stop=False)
            pe.matmul(dst, hi, ml, start=False, stop=False)
            return pe.matmul(dst, hi, mh, start=False, stop=last)

        def slot_products(b, i, body_slots, s, dst, mh, ml, kt=KT, first=True, last=True):
            at = (b + s) % RING
            pe.wait_ge(w_lo_ready, i * body_slots + (b + s + 1))
            for k in range(kt):
                mm = three_passes(dst, w_hi[:, at, k, :], w_lo[:, at, k, :], mh(k), ml(k),
                                  first and k == 0, last and k == kt - 1)
            mm.then_inc(w_used, 1)

        def ada_slot(b, i, body_slots, s, bank, part):
            at = (b + s) % RING
            pe.wait_ge(w_lo_ready, i * body_slots + (b + s + 1))
            hi, lo = wide(w_hi, at, 4), wide(w_lo, at, 4)
            for k in range(4):
                pe.matmul(ps[0:ADA_ROWS, bank, 0:ADA_GROUP], s4[:, 4 * part + k, :], lo[:, k, :], start=(part == 0 and k == 0), stop=False)
                mm = pe.matmul(ps[0:ADA_ROWS, bank, 0:ADA_GROUP], s4[:, 4 * part + k, :], hi[:, k, :], start=False, stop=(part == 1 and k == 3))
            mm.then_inc(w_used, 1)

        def ada_columns(q, i, group, bank):
            pe.wait_ge(ada_rows_copied, i * 6 + (q * ADA_GROUPS + group + 1))
            for n in range(2):
                mm = pe.matmul(ps[:, bank, bass.ds(i * 24 + (ADA_GROUP + 4 * group + 2 * n), 2)],
                               ada_rows[:, n * P:(n + 1) * P], pair, start=True, stop=True)
            return mm

        def first_ada(first, last):
            def columns(m):
                pe.wait_ge(ada_rows_copied, m + 1)
                for n in range(2):
                    mm = pe.matmul(ps[:, 0, ADA_GROUP + 4 * m + 2 * n:ADA_GROUP + 4 * m + 2 * n + 2],
                                   ada0_rows[m % 2][:, n * P:(n + 1) * P], pair[0:2, :], start=True, stop=True)
                mm.then_inc(ada_cols_ready, 1)

            for m in range(first, last):
                place = m % ADA0_PLACES
                pe.wait_ge(ada0_loaded[place], 16 * (m // ADA0_PLACES + 1))
                if m >= 2:
                    pe.wait_ge(ada_rows_copied, m - 1)
                for k in range(KT):
                    mm = pe.matmul(ps[0:2, ADA0_BANKS[m % 2], 0:ADA_GROUP], sc[:, :, k], ada0[:, place, k, :],
                                   start=(k == 0), stop=(k == KT - 1))
                mm.then_inc(ada0_used, 1)
                if m > first:
                    columns(m - 1)
            columns(last - 1)

        def norm_sum(q, n):
            pe.wait_ge(ssq_ready, KT * (q + 1))
            pe.matmul(ps[:, SUM_BANK, 0:n], ones, ssq[:, 0:n], start=True, stop=True).then_inc(sums_ready, 1)

        def first_slots(q, b, banks, n):
            for k in range(KT):
                pe.wait_ge(xl_ready, q * KT + k + 1)
                for s in range(2):
                    if k == 0:
                        pe.wait_ge(w_lo_ready, b + s + 1)
                    at = (b + s) % RING
                    mm = three_passes(ps[:, banks[s], 0:n], w_hi[:, at, k, :], w_lo[:, at, k, :],
                                      xh[:, k, 0:n], xl[:, k, 0:n], k == 0, k == KT - 1)
                    if k == KT - 1:
                        mm.then_inc(w_used, 1)

        def ffn_phase(l, sub, f):
            n = tokens(l, sub)
            q = update_index(l, sub) - 1
            b = base[l, sub, "in"]

            def pair(i, p):
                for s in (2 * p, 2 * p + 1):
                    slot_products(b, i, 4, s, ps[:, s, 0:n], lambda k: xh[:, k, 0:n], lambda k: xl[:, k, 0:n])

            def body(i):
                for p in range(2):
                    if not isinstance(i, int):
                        pe.wait_ge(prod_ready, i * 2 + (f * HT + p - 1))
                    pair(i, p)
            first_slots(q, b, (0, 1), n)
            pair(0, 1)
            with pe.Fori(1, HT // 2) as i:
                body(i)

            b = base[l, sub, "out"]
            u = update_index(l, sub)

            per = out_slots(l, sub)

            def out_body(i):
                for c in range(4):
                    if not (isinstance(i, int) and i == 0):
                        pe.wait_ge(h_ready, i * 4 + ((u - 1) * KT + c - 3))
                    for part, (k0, kn) in enumerate(OUT_PARTS):
                        s = per * c + part * (per // 3)
                        if per == 6:
                            if isinstance(i, int) and i == 0 and c == 0 and part == 0:
                                pe.wait_ge(prod_ready, (f + 1) * HT - 1)
                            j = 3 * c + part
                            if j % 2 == 0 and j > 0:
                                ada_columns(3 * l + sub + 1, i, j // 2 - 1, 0)
                            ada_slot(b, i, 24, s, 0, j % 2)
                            s += 1
                        if isinstance(i, int) and i == 0 and c == 0:
                            pe.wait_ge(hid_l_ready, f * HT + k0 + kn)
                        slot_products(b, i, 4 * per, s, ps[:, 4 + c, 0:n],
                                      lambda k: hid_h[:, k0 + k, 0:n], lambda k: hid_l[:, k0 + k, 0:n],
                                      kn, part == 0, part == 2)
                if per == 6 and c == 3:
                    mm = ada_columns(3 * l + sub + 1, i, 5, 0)
                    if i == 1:
                        mm.then_inc(ada_cols_ready, 1)
            for i in range(2):
                out_body(i)

        def project(l, slot, what, banks):
            n = query_tokens(l) if what in QUERY_ONLY else TOK
            if what not in TOKEN_MAJOR:
                slot_products(slot, 0, 0, 0, ps[:, banks[0], 0:n], lambda k: xh[:, k, 0:n], lambda k: xl[:, k, 0:n])
                return
            at = (slot - 1) % RING
            pe.wait_ge(w_lo_ready, slot + 1)
            per = n // P // 2
            for tt in range(n // P):
                dst, tokens_of = ps[:, banks[tt // per], tt % per * 256:(tt % per + 1) * 256], slice(tt * P, (tt + 1) * P)
                for k in range(KT):
                    mm = three_passes(dst, xh[:, k, tokens_of], xl[:, k, tokens_of],
                                      w_hi[:, at:at + 2, k, :], w_lo[:, at:at + 2, k, :], k == 0, k == KT - 1)
            mm.then_inc(w_used, 2)

        def proj_phase(l):
            b = base[l, 1, "proj"]
            n = query_tokens(l)
            first_slots(3 * l + 1, b, (6, 7), n)
            for s, (what, c, _) in enumerate(PROJ):
                if s < 2 or (what in TOKEN_MAJOR and c == 0):
                    continue
                pe.wait_ge(proj_ready, l * PROJ_ALL + s - 1)
                project(l, b + s, what, (6, 7) if what in TOKEN_MAJOR else (6 + s % 2,))
                if s == 3:
                    latent_sums(l, n)
                elif s == 6:
                    latent_queries(l, n)
                elif s == 7:
                    latent_keys_values(l)
                elif s == 9:
                    rotations(l)
            pooled_sums(l, n)

        def latent_sums(l, n):
            pe.wait_ge(msq_ready, 3 * l + 3)
            pe.matmul(ps[:, 0, 0:n], ones, unit(U_P)[:, 0:n], start=True, stop=False)
            pe.matmul(ps[:, 0, 0:n], ones, unit(U_P + 1)[:, 0:n], start=False, stop=True)
            pe.matmul(ps[:, 1, :], ones, unit(U_P + 2), start=True, stop=True).then_inc(msum_ready, 1)

        def latent_queries(l, n):
            pe.wait_ge(mnorm_ready, l + 1)
            pe.wait_ge(mix_loaded, 32 * (l + 1))
            for hd in range(4):
                for k in range(2):
                    mm = pe.matmul(ps[0:96, 2 + hd, 0:n], w_qb[:, k, hd * 96:(hd + 1) * 96],
                                   unit(feat["qa", k])[:, 0:n], start=(k == 0), stop=(k == 1))
                mm.then_inc(mla_t, 1)

        def latent_keys_values(l):
            for hd in range(4):
                if hd >= 2:
                    pe.wait_ge(mla_ready, 10 * l + hd - 1)
                pe.matmul(ps[0:64, hd, :], w_kvb[:, hd * P:hd * P + 64], unit(feat["kva", 0]),
                          start=True, stop=True).then_inc(mla_t, 1)
            w_v = w_kvb.rearrange("p (h c) -> p h c", h=4)[:, :, 64:P]
            for tt in range(4):
                if tt % 2 == 0:
                    pe.wait_ge(mla_ready, 10 * l + 3 + tt // 2)
                mm = pe.matmul(ps[:, 4 + tt // 2, tt % 2 * 256:tt % 2 * 256 + 256],
                               unit(feat["kva", 0])[:, tt * P:(tt + 1) * P], w_v, start=True, stop=True)
                if tt % 2:
                    mm.then_inc(mla_t, 1)

        def rotations(l):
            pe.wait_ge(mla_ready, 10 * (l + 1))
            for n, key in enumerate(ROTATED):
                mm = pe.matmul(ps[:, n // 2, n % 2 * LAT:(n % 2 + 1) * LAT], perm, unit(feat[key])[:, 0:LAT], start=True, stop=True)
                if n % 2 or n == 4:
                    mm.then_inc(rot_ready, 1)
            for hd in range(4):
                mm = pe.matmul(ps[64:96, 3 + hd // 2, hd % 2 * LAT:(hd % 2 + 1) * LAT], perm[64:96, 64:96],
                               unit(MQ + hd)[64:96, 0:LAT], start=True, stop=True)
                if hd % 2:
                    mm.then_inc(mrot_ready, 1)

        def pooled_sums(l, n):
            pe.wait_ge(pool_loaded, 16 * 5 * (l + 1))
            pe.wait_ge(rope_step, (l + 1) * ROPE_STEPS)
            u = token_major("pool")
            for g in range(4):
                r = g % 2 * 64
                for half in range(n // LAT):
                    for tt in range(2):
                        mm = pe.matmul(ps[r:r + 64, (5, 3)[g // 2], half * LAT:(half + 1) * LAT],
                                       u[:, 2 * half + tt, g * 64:(g + 1) * 64], pool_mat[:, g, tt, :],
                                       start=(tt == 0), stop=(tt == 1))
            mm.then_inc(pooled_t, 1)

        def mixing_phase(l):
            us = units[l]
            pe.wait_ge(kr_spread, l + 1)
            pe.wait_ge(proj_ready, l * PROJ_ALL + PROJ_SLOTS)

            def scores(n):
                br, hd, b, is_ctx = us[n]
                q0 = (LAT if is_ctx else 0) + b * P
                k0 = LAT if is_ctx else 0
                for j, cc in enumerate(comp_at[l, n]):
                    if cc >= S_BANKS:
                        pe.wait_ge(exp_ready, cc - S_BANKS + 1)
                    if br == DIFF_BR:
                        r, rn, qt, kt = hd % 2 * 64 + j * 32, 32, feat["dq", hd // 2], feat["dk", hd // 2]
                    elif br == NA_BR:
                        r, rn, qt, kt = hd % 2 * 64, 64, feat["nq", hd // 2], feat["nk", hd // 2]
                    else:
                        r, rn, qt, kt = 0, 96, MQ + hd, MK + hd
                    pe.matmul(ps[:, cc % S_BANKS, 0:TOK - k0], unit(qt)[r:r + rn, q0:q0 + P],
                              unit(kt)[r:r + rn, k0:TOK], start=True, stop=True).then_inc(score_ready, 1)

            def transposes(n):
                u = unit0[l] + n
                _, _, _, is_ctx = us[n]
                pe.wait_ge(probs_ready, u + 1)
                if u >= 1:
                    pe.wait_ge(probs_t_copied, u)
                src = unit(U_P + comp_at[l, n][0] % 4)
                for kt in range(2 if is_ctx else 4):
                    mm = pe.transpose(ps[:, PT_BANK, kt * P:(kt + 1) * P], src[:, kt * P:(kt + 1) * P], ident)
                mm.then_inc(probs_t, 1)

            def values(n):
                br, hd, _, is_ctx = us[n]
                v = (unit0[l] + n) // 2
                pe.wait_ge(probs_t_copied, unit0[l] + n + 1)
                if v >= 1:
                    pe.wait_ge(attn_ready, v)
                vals = token_major({DIFF_BR: "dv", NA_BR: "nv", MLA_BR: "mv"}[br])
                pt = arena[:, U_PT + v % 2 * 2:U_PT + v % 2 * 2 + 2, :].rearrange("p a (t q) -> p (a t) q", q=256)
                r, kts = hd % 2 * 64, 2 if is_ctx else 4
                for kt in range(kts):
                    mm = pe.matmul(ps[r:r + 64, O_BANK, 0:256],
                                   vals[:, (2 if is_ctx else 0) + kt, hd * 64:(hd + 1) * 64], pt[:, kt, :],
                                   start=(kt == 0), stop=(kt == kts - 1))
                mm.then_inc(attn_t, 1)

            nt = query_tokens(l)

            def item(slot, it):
                if it[0] == "ada":
                    if it[1] % 2 == 0 and it[1] > 0:
                        ada_columns(3 * l + 2, 0, it[1] // 2 - 1, ada_bank(1))
                    ada_slot(slot, 0, 0, 0, ada_bank(1), it[1] % 2)
                elif it[0] == "branch":
                    at, br = slot % RING, it[1]
                    pe.wait_ge(w_lo_ready, slot + 1)
                    pe.wait_ge(y_l_ready, 4 * l + branch_order.index(br) + 1)
                    for c in range(4):
                        key = ("branch", br, 4 * it[2] + c)
                        bank_free(pe, l, key)
                        for k in range(2):
                            mm = three_passes(ps[:, stream_bank(l, key), 0:nt], w_hi[:, at, 4 * k + c, :], w_lo[:, at, 4 * k + c, :],
                                              y_h[:, k, 0:nt], y_l[:, k, 0:nt], k == 0, k == 1)
                        mm.then_inc(branch_t if c < 3 else w_used, 1)
                else:
                    bank_free(pe, l, it)
                    if it[0] == "proj":
                        what, c, _ = PROJ_NA[it[1]]
                        if what not in TOKEN_MAJOR:
                            project(l, slot, what, (stream_bank(l, it),))
                        elif c == 1:
                            project(l, slot, what, (stream_bank(l, ("proj", it[1] - 1)), stream_bank(l, it)))
                    else:
                        slot_products(slot, 0, 0, 0, ps[:, stream_bank(l, it), 0:nt], lambda k: xh[:, k, 0:nt], lambda k: xl[:, k, 0:nt])

            nt = query_tokens(l)

            for k in range(len(stages)):
                mine = stage_units[l][k]
                if mine:
                    scores(mine[0])
                if k == 0:
                    pe.wait_ge(pooled_ready, l + 1)
                for e in stage_events(l, k):
                    if e[0] == "unit":
                        n = e[1]
                        if n + 1 in mine:
                            scores(n + 1)
                        transposes(n)
                        if n % 2 == 0 and n > mine[0]:
                            values(n - 1)
                    elif e[0] == "item":
                        item(e[1], e[2])
                    elif e[0] == "close":
                        values(mine[-1])
                    elif e[0] == "pool_y":
                        for p in range(2):
                            bank_free(pe, l, ("pool_y", p))
                            mm = pe.matmul(ps[:, stream_bank(l, ("pool_y", p)), 0:nt], w_pool[:, p, :], pooled[:, p, 0:nt], start=True, stop=True)
                        mm.then_inc(pool_y_t, 1)
                    elif e[0] == "subnorm":
                        for p in range(2):
                            bank_free(pe, l, ("subnorm", p))
                            pe.wait_ge(dsq_ready, 2 * l + p + 1)
                            pe.matmul(ps[:, stream_bank(l, ("subnorm", p)), 0:nt], blocks, sq[:, p, 0:nt],
                                      start=True, stop=True).then_inc(dsum_ready, 1)

            ada_columns(3 * l + 2, 0, ADA_GROUPS - 1, ada_bank(1)).then_inc(ada_cols_ready, 1)
            b = base[l, 1, "mixout"]
            u = update_index(l, 1)
            for i in range(2):
                for s in range(4):
                    at = (b + s) % RING
                    if i > 0:
                        pe.wait_ge(h_ready, (u - 1) * KT + i * 4 + s - 3)
                    else:
                        pe.wait_ge(gated, 32 * (l + 1))
                    pe.wait_ge(w_lo_ready, b + 4 * i + s + 1)
                    for k in range(KT):
                        if i == 0 and s == 0:
                            pe.wait_ge(m_l_ready, l * KT + k + 1)
                        mm = three_passes(ps[:, 4 + s, 0:nt], w_hi[:, at, k, :], w_lo[:, at, k, :],
                                          m_h[:, k, 0:nt], m_l[:, k, 0:nt], k == 0, k == KT - 1)
                    mm.then_inc(w_used, 1)

        pe.wait_ge(cond_ready, 1)
        pe.wait_ge(xt_copied, KT)
        first_ada(0, ADA0_FIRST)
        for l in range(DEPTH):
            for sub in range(3):
                norm_sum(3 * l + sub, tokens(l, sub))
                if (l, sub) == (0, 0):
                    pe.wait_ge(mods_ready, 1)
                    first_ada(ADA0_FIRST, ADA_GROUPS)
                    pe.wait_ge(gates_ready, 1)
                if sub != 1:
                    ffn_phase(l, sub, 2 * l + sub // 2)
                else:
                    proj_phase(l)
                    mixing_phase(l)
        norm_sum(3 * DEPTH, LAT)
        for tt in range(2):
            for k in range(KT):
                pe.wait_ge(fin_ready, k + 1)
                mm = pe.transpose(ps[:, 2 * tt + k // 4, k % 4 * P:(k % 4 + 1) * P], norm_tmp_final(k)[:, tt * P:(tt + 1) * P], ident)
                if k % 4 == 3:
                    mm.then_inc(fin_t, 1)

    @block.scalar
    def _(act):
        def split(b, i, body_slots, s):
            at = (b + s + AHEAD) % RING
            act.wait_ge(w_loaded[at], i * (body_slots // RING * 16) + 16 * ((b + s + AHEAD) // RING + 1))
            if not (isinstance(i, int) and i * body_slots + b + s + AHEAD < RING):
                act.wait_ge(w_used, i * body_slots + (b + s + AHEAD - RING + 1))
            if rotary_slot(b, i, s):
                act.copy(four(w_hi, at), four_of(raw, at)).then_inc(w_hi_ready, 1)
                return
            act.copy(w_hi[:, at], raw[:, at]).then_inc(w_hi_ready, 1)

        def maybe_split(b, i, body_slots, s):
            if not isinstance(i, int) or i * body_slots + b + s + AHEAD < total_slots:
                split(b, i, body_slots, s)

        def squares(u, i, step, c, n):
            tile = i * step + c
            act.wait_ge(h_ready, i * step + ((u - 1) * KT + c + 1))
            act.wait_ge(ssq_ready, i * step + (u * KT + c - 1))
            act.activation(sq[:, c % 2, 0:n], h[:, bass.ds(tile, 1), 0:n].rearrange("p a n -> p (a n)"),
                           ACT.Square).then_inc(sq_ready, 1)

        act.wait_ge(cols_ready, 1)
        act.activation(sc[:, :, :].rearrange("p w k -> p (w k)"), cond_cols, ACT.Silu).then_inc(cond_ready, 1)
        act.wait_ge(cond_ready, 1)
        act.copy(s4[:, :, 0:2].rearrange("p k w -> p w k"), sc[:, :, :]).then_inc(s4_ready, 1)
        for k in range(KT):
            act.wait_ge(xt_ready, k + 1)
            act.copy(h[:, k, :], ps[:, k % 4, :]).then_inc(xt_copied, 1)
            act.wait_ge(xt_copied, k + 1)
            if k >= 2:
                act.wait_ge(ssq_ready, k - 1)
            act.activation(sq[:, k % 2, :], h[:, k, :], ACT.Square).then_inc(sq_ready, 1)
        act.wait_ge(lam_step, 2)
        act.activation(lam_row[:, 392:396], lam_row[:, 384:388], ACT.Exp).then_inc(lam_exp, 1)

        def first_ada(first, last):
            for m in range(first, last):
                act.wait_ge(ada0_used, m + 1)
                if m >= 2:
                    act.wait_ge(ada_cols_ready, m - 1)
                act.copy(ada0_rows[m % 2], ps[0:2, ADA0_BANKS[m % 2], 0:ADA_GROUP]).then_inc(ada_rows_copied, 1)

        first_ada(0, ADA0_FIRST)

        def copy_ada_rows(used, bank):
            act.wait_ge(w_used, used)
            act.copy(ada_rows, ps[0:ADA_ROWS, bank, 0:ADA_GROUP]).then_inc(ada_rows_copied, 1)

        def root(dst, src, width):
            return act.activation(dst, src, ACT.Sqrt, bias=eps_col, scale=1.0 / width)

        def norm(q, n):
            if q == 0:
                act.wait_ge(eps_set, 1)
                act.wait_ge(mods_ready, 1)
            act.wait_ge(sums_ready, q + 1)
            root(rstd[:, 0:n], ps[:, SUM_BANK, 0:n], D).then_inc(std_ready, 1)
            if q == 3 * DEPTH:
                return
            if q == 0:
                for m in range(AHEAD):
                    split(-AHEAD, 0, 0, m)
            for k in range(KT):
                scaled_ready(act, q, k)
                for w, cols_of in halves(n):
                    last = act.activation(xh[:, k, cols_of], norm_tmp[k % 4][:, cols_of], ACT.Identity, bias=mods[:, q % 2, k, w:w + 1])
                last.then_inc(xh_ready, 1)

        def ffn_phase(l, sub, f):
            n = tokens(l, sub)
            b = base[l, sub, "in"]

            def body(i):
                for p in range(2):
                    split(b, i, 4, 2 * p)
                    act.wait_ge(w_used, i * 4 + (b + 2 * p + 1))
                    if f * HT + p >= 2 or not isinstance(i, int):
                        act.wait_ge(prod_ready, i * 2 + (f * HT + p - 1))
                    act.activation(silu[:, p, 0:n], ps[:, 2 * p, 0:n], ACT.Silu).then_inc(silu_ready, 1)
                    split(b, i, 4, 2 * p + 1)
                    act.wait_ge(prod_ready, i * 2 + (f * HT + p + 1))
                    act.copy(hid_h[:, bass.ds(i * 2 + p, 1), 0:n].rearrange("p a n -> p (a n)"), prod[:, p, 0:n]).then_inc(hid_h_ready, 1)
            body(0)
            with act.Fori(1, HT // 2) as i:
                body(i)
            b = base[l, sub, "out"]
            u = update_index(l, sub)

            per = out_slots(l, sub)

            def out_body(i):
                for c in range(4):
                    for part in range(per):
                        maybe_split(b, i, 4 * per, per * c + part)
                        if per == 6 and part % 2 == 1 and (3 * c + part // 2) % 2 == 1:
                            copy_ada_rows(i * 24 + (b + per * c + part), 0)
                    squares(u, i, 4, c, n)
            steps(act, 2, 12, out_body, peel=(l, sub) == (DEPTH - 1, 2))

        def mix_phase(l):
            n = query_tokens(l)
            b = base[l, 1, "proj"]
            def projected(slot, what, c, banks):
                m = n if what in QUERY_ONLY else TOK
                if what in TOKEN_MAJOR:
                    if c == 0:
                        return
                    act.wait_ge(w_used, slot + 1)
                    per = m // P // 2
                    for j, bank in enumerate(banks):
                        act.copy(token_major(what)[:, j * per:(j + 1) * per, :],
                                 ps[:, bank, 0:per * 256].rearrange("p (t n) -> p t n", n=256)).then_inc(proj_ready, 1)
                    return
                act.wait_ge(w_used, slot + 1)
                bank = banks[0]
                if what in ("qa", "kva"):
                    j = c if what == "qa" else 2
                    act.activation(unit(U_P + j)[:, 0:m], ps[:, bank, 0:m], ACT.Square).then_inc(msq_ready, 1)
                if what == "nq":
                    act.mul(unit(feat[what, c])[:, 0:m], ps[:, bank, 0:m], 0.125).then_inc(proj_ready, 1)
                else:
                    act.copy(unit(feat[what, c])[:, 0:m], ps[:, bank, 0:m]).then_inc(proj_ready, 1)

            def mla_copies(first, last):
                for j in range(first, last):
                    act.wait_ge(mla_t, 10 * l + j + 1)
                    if j < 4:
                        act.copy(unit(MQ + j)[0:96, 0:n], ps[0:96, 2 + j, 0:n]).then_inc(mla_ready, 1)
                    elif j < 8:
                        act.copy(unit(MK + j - 4)[0:64, :], ps[0:64, j - 4, :]).then_inc(mla_ready, 1)
                    else:
                        act.copy(token_major("mv")[:, 2 * (j - 8):2 * (j - 8) + 2, :],
                                 ps[:, j - 4, :].rearrange("p (t n) -> p t n", t=2)).then_inc(mla_ready, 1)

            for s, (what, c, _) in enumerate(PROJ):
                split(b, 0, 0, s)
                projected(b + s, what, c, (6, 7) if what in TOKEN_MAJOR else (6 + s % 2,))
                if s == 3:
                    act.wait_ge(msum_ready, l + 1)
                    root(unit(U_P)[:, 0:n], ps[:, 0, 0:n], 256)
                    root(unit(U_P + 2), ps[:, 1, :], 128).then_inc(mstd_ready, 1)
                elif s == 6:
                    mla_copies(0, 4)
                elif s == 7:
                    mla_copies(4, 10)
            act.wait_ge(pooled_t, l + 1)
            act.copy(pooled[:, 0, 0:n], ps[:, 5, 0:n])
            act.copy(pooled[:, 1, 0:n], ps[:, 3, 0:n]).then_inc(pooled_ready, 1)
            us = units[l]

            def exps(m):
                br, _, _, is_ctx = us[m]
                width = CTX if is_ctx else TOK
                scale = {DIFF_BR: 32 ** -0.5, MLA_BR: 96 ** -0.5, NA_BR: 1.0}[br]
                for cc in comp_at[l, m]:
                    act.wait_ge(max_ready, cc + 1)
                    if cc >= 4:
                        act.wait_ge(probs_t, unit_of_comp[cc - 4] + 1)
                    act.activation(unit(U_P + cc % 4)[:, 0:width], ps[:, cc % S_BANKS, 0:width], ACT.Exp,
                                   bias=exp_bias(cc), scale=scale, accum_out=exp_sum(cc)).then_inc(exp_ready, 1)

            def copy_t(m):
                u = unit0[l] + m
                _, _, qb, is_ctx = us[m]
                v = u // 2
                act.wait_ge(probs_t, u + 1)
                if v >= 2:
                    act.wait_ge(attn_t, v - 1)
                kts = 2 if is_ctx else 4
                pt = arena[:, U_PT + v % 2 * 2:U_PT + v % 2 * 2 + 2, :].rearrange("p a (t q) -> p (a t) q", q=256)
                act.copy(pt[:, 0:kts, qb * P:(qb + 1) * P],
                         ps[:, PT_BANK, 0:kts * P].rearrange("p (t q) -> p t q", q=P)).then_inc(probs_t_copied, 1)

            def copy_out(m):
                br, hd, _, is_ctx = us[m]
                v = (unit0[l] + m) // 2
                act.wait_ge(attn_t, v + 1)
                r, q0 = hd % 2 * 64, LAT if is_ctx else 0
                act.wait_ge(y_l_ready, 4 * l + branch_order.index(br))
                act.copy(y[r:r + 64, hd // 2, q0:q0 + LAT], ps[r:r + 64, O_BANK, 0:LAT]).then_inc(attn_ready, 1)

            def item(slot, it):
                split(slot, 0, 0, 0)
                if it[0] == "ada" and it[1] % 2 == 1:
                    copy_ada_rows(slot + 1, ada_bank(1))
                elif it[0] == "proj":
                    what, c, _ = PROJ_NA[it[1]]
                    banks = (stream_bank(l, ("proj", it[1] - 1)), stream_bank(l, it)) if what in TOKEN_MAJOR and c == 1 else (stream_bank(l, it),)
                    projected(slot, what, c, banks)
                elif it[0] == "gate":
                    _, _, count = uses[l][it]
                    act.wait_ge(w_used, slot + 1)
                    if count > 4:
                        act.wait_ge(gated, (count - 1) // 4 * 4)
                    act.activation(tanh_buf[it[2] % 4][:, 0:n], ps[:, stream_bank(l, it), 0:n], ACT.Tanh, scale=0.5).then_inc(tanh_ready, 1)

            for k in range(len(stages)):
                mine = stage_units[l][k]
                if mine:
                    exps(mine[0])
                for e in stage_events(l, k):
                    if e[0] == "unit":
                        m = e[1]
                        if m + 1 in mine:
                            exps(m + 1)
                        copy_t(m)
                        if m % 2 == 0 and m > mine[0]:
                            copy_out(m - 1)
                    elif e[0] == "item":
                        item(e[1], e[2])
                    elif e[0] == "close":
                        copy_out(mine[-1])
                        if k == 0:
                            act.wait_ge(attn_ready, (unit0[l] + mine[-1] + 1) // 2)
                            for p in range(2):
                                act.activation(sq[:, p, 0:n], y[:, p, 0:n], ACT.Square).then_inc(dsq_ready, 1)
                    elif e[0] == "pool_y":
                        act.wait_ge(pool_y_t, l + 1)
                        for p in range(2):
                            last = act.activation(y[:, p, 0:n], ps[:, stream_bank(l, ("pool_y", p)), 0:n], ACT.Copy, scale=pool_scale_col(l, p))
                        last.then_inc(y_pool_ready, 1)
                        act.wait_ge(y_pool_ready, l + 1)
                        act.copy(y_h[:, :, 0:n], y[:, :, 0:n]).then_inc(y_h_ready, 1)
                    elif e[0] == "subnorm":
                        for p in range(2):
                            act.wait_ge(dsum_ready, 2 * l + p + 1)
                            root(sq[:, p, 0:n], ps[:, stream_bank(l, ("subnorm", p)), 0:n], 64).then_inc(dstd_ready, 1)
                    elif e[0] == "split":
                        if k == 1:
                            act.wait_ge(dnorm_ready, 2 * (l + 1))
                        else:
                            act.wait_ge(attn_ready, (unit0[l] + stage_units[l][k - 1][-1] + 1) // 2)
                        act.wait_ge(w_used, base[l, 1, "mix"] + sum(len(items) for _, items in stages[:k]))
                        act.copy(y_h[:, :, 0:n], y[:, :, 0:n]).then_inc(y_h_ready, 1)
            for c in range(KT):
                act.wait_ge(macc_ready, 24 * l + 16 + c + 1)
                act.copy(m_h[:, c, 0:n], unit(U_MACC + c)[:, 0:n]).then_inc(m_h_ready, 1)
            b = base[l, 1, "mixout"]
            u = update_index(l, 1)

            def out_body(i):
                for c in range(4):
                    split(b, i, 4, c)
                    squares(u, i, 4, c, n)
            steps(act, 2, 4, out_body)

        for l in range(DEPTH):
            for sub in range(3):
                norm(3 * l + sub, tokens(l, sub))
                if (l, sub) == (0, 0):
                    first_ada(ADA0_FIRST, ADA_GROUPS)
                if sub != 1:
                    ffn_phase(l, sub, 2 * l + sub // 2)
                else:
                    mix_phase(l)
        norm(3 * DEPTH, LAT)
        for tt in range(2):
            for a in range(2):
                act.wait_ge(fin_t, 2 * tt + a + 1)
                act.copy(out_tok[:, tt, a * 512:(a + 1) * 512], ps[:, 2 * tt + a, :]).then_inc(fin_copied, 1)

    @block.vector
    def _(dve):
        def split(b, i, body_slots, s):
            at = (b + s + AHEAD) % RING
            dve.wait_ge(w_hi_ready, i * body_slots + (b + s + AHEAD + 1))
            if rotary_slot(b, i, s):
                dve.tensor_tensor(four(w_lo, at), four_of(raw, at), four(w_hi, at), ALU.subtract).then_inc(w_lo_ready, 1)
                return
            dve.tensor_tensor(w_lo[:, at], raw[:, at], w_hi[:, at], ALU.subtract).then_inc(w_lo_ready, 1)

        def maybe_split(b, i, body_slots, s):
            if not isinstance(i, int) or i * body_slots + b + s + AHEAD < total_slots:
                split(b, i, body_slots, s)

        def add_squares(u, i, step, c, n):
            dve.wait_ge(sq_ready, i * step + (u * KT + c + 1))
            dve.wait_ge(ssq_ready, i * step + (u * KT + c))
            dve.tensor_tensor(ssq[:, 0:n], ssq[:, 0:n], sq[:, c % 2, 0:n], ALU.add).then_inc(ssq_ready, 1)

        dve.memset(eps_col, EPS).then_inc(eps_set, 1)
        dve.wait_ge(cols_t_ready, 1)
        dve.tensor_copy(cols[:, 0:P + 100], ps[:, 6, 0:P + 100]).then_inc(cols_ready, 1)
        dve.wait_ge(cols_ready, 1)
        for l in range(DEPTH):
            dve.tensor_scalar(subln_g[l], subln_col(l), 1.0 - LAM_INIT[l], None, ALU.mult).then_inc(cols_ready, 1)
        dve.wait_ge(s4_ready, 1)
        dve.tensor_tensor(s4[:, :, 2:4].rearrange("p k w -> p w k"), sc[:, :, :],
                          s4[:, :, 0:2].rearrange("p k w -> p w k"), ALU.subtract).then_inc(s4_ready, 1)
        dve.wait_ge(lam_loaded, 16)
        dl = lam_row[:, 0:256].rearrange("o (a b d) -> o a b d", a=4, b=2)
        dve.tensor_tensor(lam_row[:, 256:384].rearrange("o (a d) -> o a d", a=4), dl[:, :, 0, :], dl[:, :, 1, :], ALU.mult).then_inc(lam_step, 1)
        dve.wait_ge(lam_step, 1)
        dve.reduce_sum(lam_row[:, 384:388], lam_row[:, 256:384].rearrange("o (a d) -> o a d", a=4), AX_X).then_inc(lam_step, 1)
        for k in range(KT):
            dve.wait_ge(sq_ready, k + 1)
            if k == 0:
                dve.tensor_copy(ssq[:, :], sq[:, 0, :]).then_inc(ssq_ready, 1)
            else:
                dve.wait_ge(ssq_ready, k)
                dve.tensor_tensor(ssq[:, :], ssq[:, :], sq[:, k % 2, :], ALU.add).then_inc(ssq_ready, 1)
        dve.wait_ge(lam_exp, 1)
        e = lam_row[:, 392:396].rearrange("o (l a) -> o l a", l=2)
        dve.tensor_tensor(lam_row[:, 400:402], e[:, :, 1], e[:, :, 0], ALU.subtract).then_inc(lam_step, 1)
        dve.wait_ge(lam_bc, 1)
        for l in range(DEPTH):
            dve.tensor_scalar(neg_lam[l], ps[:, 5, l:l + 1], -LAM_INIT[l], None, ALU.add).then_inc(lam_ready, 1)

        def modulation(l, sub, bank, count, first, last):
            m = mods[:, (3 * l + sub) % 2]
            acc = ps[:, bank, ADA_GROUP:ADA_GROUP + 6 * KT].rearrange("p (n c) -> p n c", c=2)
            dve.wait_ge(ada_cols_ready, count)
            dve.tensor_tensor(m[:, first:last, :], acc[:, first:last, :],
                              ada_b_cols(l, sub)[:, first:last].unsqueeze(2).to_broadcast([P, last - first, 2]), ALU.add).then_inc(mod_step, 1)
            steps_done[0] += 1
            dve.wait_ge(mod_step, steps_done[0])
            if first == 0:
                dve.scalar_tensor_tensor(out=m[:, 8:16, :], in0=m[:, 8:16, :], scalar=1.0,
                                         in1=norm_g_cols(l, sub).unsqueeze(2).to_broadcast([P, KT, 2]), op0=ALU.add, op1=ALU.mult).then_inc(mods_ready, 1)
            if last == 3 * KT:
                dve.tensor_scalar(m[:, 16:24, :], m[:, 16:24, :], 0.5, None, ALU.mult).then_inc(gates_ready, 1)

        steps_done = [0]

        def norm(l, sub):
            q, n = 3 * l + sub, tokens(l, sub)
            m = mods[:, q % 2]
            dve.wait_ge(mods_ready, q + 1)
            dve.wait_ge(std_ready, q + 1)
            dve.reciprocal(rstd[:, 0:n], rstd[:, 0:n]).then_inc(rstd_ready, 1)
            if q == 0:
                for s in range(AHEAD):
                    split(-AHEAD, 0, 0, s)

            dve.wait_ge(rstd_ready, q + 1)
            mine = [k for k in range(KT) if k not in POOL_TILES]

            def scale_upto(last):
                while mine and mine[0] <= last:
                    k = mine.pop(0)
                    if k >= 4:
                        dve.wait_ge(xl_ready, q * KT + k - 3)
                    for w, cols_of in halves(n):
                        done = dve.scalar_tensor_tensor(out=norm_tmp[k % 4][:, cols_of], in0=h[:, k, cols_of],
                                                        scalar=m[:, 8 + k, w:w + 1], in1=rstd[:, cols_of], op0=ALU.mult, op1=ALU.mult)
                    done.then_inc(dve_scaled, 1)

            for k in range(KT):
                scale_upto(k + 1)
                scaled_ready(dve, q, k)
                dve.wait_ge(xh_ready, q * KT + k + 1)
                for w, cols_of in halves(n):
                    last = dve.scalar_tensor_tensor(out=xl[:, k, cols_of], in0=norm_tmp[k % 4][:, cols_of], scalar=m[:, k, w:w + 1],
                                                    in1=xh[:, k, cols_of], op0=ALU.add, op1=ALU.subtract)
                last.then_inc(xl_ready, 1)

        def update(l, sub, i, c, bank, n, used):
            u = update_index(l, sub)
            m = mods[:, (3 * l + sub) % 2]
            tile = i * 4 + c
            dve.wait_ge(w_used, used)
            hk = h[:, bass.ds(tile, 1), :].rearrange("p a n -> p (a n)")
            for w, cols_of in halves(n):
                gate = m[:, bass.ds(tile + 16, 1), w:w + 1].rearrange("p a n -> p (a n)")
                last = dve.scalar_tensor_tensor(out=hk[:, cols_of], in0=ps[:, bank, cols_of], scalar=gate,
                                                in1=hk[:, cols_of], op0=ALU.mult, op1=ALU.add)
            last.then_inc(h_ready, 1)

        def reset_squares(l, sub, n):
            dve.wait_ge(gates_ready, 3 * l + sub + 1)
            dve.memset(ssq[:, 0:n], 0.0).then_inc(ssq_reset, 1)
            dve.wait_ge(ssq_reset, update_index(l, sub))

        def ffn_phase(l, sub, f):
            n = tokens(l, sub)
            b = base[l, sub, "in"]

            def body(i):
                for p in range(2):
                    split(b, i, 4, 2 * p)
                    split(b, i, 4, 2 * p + 1)
                    dve.wait_ge(w_used, i * 4 + (b + 2 * p + 2))
                    dve.wait_ge(silu_ready, i * 2 + (f * HT + p + 1))
                    if f * HT + p >= 2 or not isinstance(i, int):
                        dve.wait_ge(hid_l_ready, i * 2 + (f * HT + p - 1))
                    dve.tensor_tensor(prod[:, p, 0:n], silu[:, p, 0:n], ps[:, 2 * p + 1, 0:n], ALU.mult).then_inc(prod_ready, 1)
                    dve.wait_ge(hid_h_ready, i * 2 + (f * HT + p + 1))
                    tile = bass.ds(i * 2 + p, 1)
                    dve.tensor_tensor(hid_l[:, tile, 0:n].rearrange("p a n -> p (a n)"), prod[:, p, 0:n],
                                      hid_h[:, tile, 0:n].rearrange("p a n -> p (a n)"), ALU.subtract).then_inc(hid_l_ready, 1)
            body(0)
            with dve.Fori(1, HT // 2) as i:
                body(i)
            b = base[l, sub, "out"]
            reset_squares(l, sub, n)

            per = out_slots(l, sub)

            def out_body(i):
                for c in range(4):
                    for part in range(per):
                        maybe_split(b, i, 4 * per, per * c + part)
                    update(l, sub, i, c, 4 + c, n, i * (4 * per) + (b + per * (c + 1)))
                    add_squares(update_index(l, sub), i, 4, c, n)
            steps(dve, 2, 12, out_body, peel=(l, sub) == (DEPTH - 1, 2))
            if per == 6:
                nl, nsub = (l, 1) if sub == 0 else (l + 1, 0)
                modulation(nl, nsub, 0, ada_counts[nl, nsub], 0, 3 * KT)

        rope = [0]

        def rotate(dst, partner, rows_of):
            a, c = sq[rows_of, 0, 0:LAT], sq[rows_of, 1, 0:LAT]
            dve.tensor_tensor(a, partner, sin[rows_of, :], ALU.mult).then_inc(rope_step, 1)
            dve.tensor_tensor(c, dst, cos[rows_of, :], ALU.mult).then_inc(rope_step, 1)
            rope[0] += 2
            dve.wait_ge(rope_step, rope[0])
            rope[0] += 1
            return dve.tensor_tensor(dst, a, c, ALU.add).then_inc(rope_step, 1)

        def mix_phase(l):
            n = query_tokens(l)
            b = base[l, 1, "proj"]
            for s in range(PROJ_SLOTS):
                split(b, 0, 0, s)
                if s == 4:
                    dve.wait_ge(mstd_ready, l + 1)
                    dve.reciprocal(unit(U_P + 1)[:, 0:n], unit(U_P)[:, 0:n]).then_inc(mrstd_ready, 1)
                elif s == 5:
                    dve.reciprocal(unit(U_P + 3), unit(U_P + 2)).then_inc(mrstd_ready, 1)
                    dve.wait_ge(mrstd_ready, 2 * (l + 1))
                    for p in range(2):
                        qa = unit(feat["qa", p])[:, 0:n]
                        dve.scalar_tensor_tensor(out=qa, in0=qa, scalar=q_g_col(l, p), in1=unit(U_P + 1)[:, 0:n], op0=ALU.mult, op1=ALU.mult)
                    kva = unit(feat["kva", 0])
                    dve.scalar_tensor_tensor(out=kva, in0=kva, scalar=kv_g_col(l), in1=unit(U_P + 3), op0=ALU.mult, op1=ALU.mult).then_inc(mnorm_ready, 1)
                elif s == 10:
                    for j, key in enumerate(ROTATED):
                        dve.wait_ge(rot_ready, 3 * l + j // 2 + 1)
                        if j:
                            dve.wait_ge(rope_step, rope[0])
                        rotate(unit(feat[key])[:, 0:LAT], ps[:, j // 2, j % 2 * LAT:(j % 2 + 1) * LAT], slice(0, P))
                    dve.wait_ge(rope_step, rope[0])
                    for hd in range(4):
                        last = dve.tensor_copy(unit(MK + hd)[64:96, :], unit(feat["kr", 0])[64:96, :])
                    last.then_inc(kr_spread, 1)
                    rows_of = slice(64, 96)
                    for hd in range(4):
                        dve.wait_ge(mrot_ready, 2 * l + hd // 2 + 1)
                        dve.wait_ge(rope_step, rope[0])
                        rotate(unit(MQ + hd)[rows_of, 0:LAT], ps[rows_of, 3 + hd // 2, hd % 2 * LAT:(hd % 2 + 1) * LAT], rows_of)
            us = units[l]

            def maxima(m):
                br, hd, qb, is_ctx = us[m]
                width = CTX if is_ctx else TOK
                for cc in comp_at[l, m]:
                    bank = ps[:, cc % S_BANKS, 0:width]
                    dve.wait_ge(score_ready, cc + 1)
                    if br == NA_BR and not is_ctx:
                        dve.wait_ge(bias_ready, 8 * (l + 1))
                        dve.tensor_tensor(bank[:, 0:LAT], bank[:, 0:LAT],
                                          bias[:, hd, qb].rearrange("p i k -> p (i k)"), ALU.add).then_inc(biased, 1)
                        dve.wait_ge(biased, na_before[l, m] + 1)
                    if cc >= 8:
                        dve.wait_ge(exp_ready, cc - 7)
                    dve.tensor_reduce(neg_max(cc), bank, AX_X, ALU.max, negate=True).then_inc(max_step, 1)
                    dve.wait_ge(max_step, cc + 1)
                    scale = {DIFF_BR: 32 ** -0.5, MLA_BR: 96 ** -0.5, NA_BR: 1.0}[br]
                    dve.tensor_scalar(exp_bias(cc), neg_max(cc), scale, None, ALU.mult).then_inc(max_ready, 1)

            def normalise(m):
                br, _, _, is_ctx = us[m]
                width = CTX if is_ctx else TOK
                cs = comp_at[l, m]
                for cc in cs:
                    dve.wait_ge(exp_ready, cc + 1)
                    dve.reciprocal(exp_inv(cc), exp_sum(cc)).then_inc(inv_step, 1)
                dve.wait_ge(inv_step, inv_count(l, m) - (br == DIFF_BR) * 2)
                first = unit(U_P + cs[0] % 4)[:, 0:width]
                if br == DIFF_BR:
                    second = unit(U_P + cs[1] % 4)[:, 0:width]
                    dve.tensor_tensor(exp_inv2(cs[0]), exp_inv(cs[1]), neg_lam[l], ALU.mult).then_inc(inv_step, 1)
                    dve.tensor_scalar(first, first, exp_inv(cs[0]), None, ALU.mult).then_inc(inv_step, 1)
                    dve.wait_ge(inv_step, inv_count(l, m))
                    dve.scalar_tensor_tensor(out=first, in0=second, scalar=exp_inv2(cs[0]), in1=first,
                                             op0=ALU.mult, op1=ALU.add).then_inc(probs_ready, 1)
                else:
                    dve.tensor_scalar(first, first, exp_inv(cs[0]), None, ALU.mult).then_inc(probs_ready, 1)

            if l == 0:
                dve.wait_ge(lam_ready, 2)
            def item(slot, it):
                split(slot, 0, 0, 0)
                if it[0] != "branch":
                    return
                for c in range(4 * it[2], 4 * it[2] + 4):
                    _, _, count = uses[l]["branch", it[1], c]
                    if c % 4 < 3:
                        dve.wait_ge(branch_t, (count - 1) // 4 * 3 + c % 4 + 1)
                    else:
                        dve.wait_ge(w_used, slot + 1)
                    dve.wait_ge(tanh_ready, count)
                    if it[1] == branch_order[0]:
                        dst = unit(U_MACC + c)[:, 0:n]
                    else:
                        dst = mtmp[c % 2][:, 0:n]
                        done = count - 8 * (l + 1)
                        if done > 2:
                            dve.wait_ge(macc_ready, done - 2)
                    dve.scalar_tensor_tensor(out=dst, in0=tanh_buf[c % 4][:, 0:n], scalar=1.0,
                                             in1=ps[:, stream_bank(l, ("branch", it[1], c)), 0:n],
                                             op0=ALU.add, op1=ALU.mult).then_inc(gated, 1)

            for k in range(len(stages)):
                mine = stage_units[l][k]
                if mine:
                    maxima(mine[0])
                    normalise(mine[0])
                for e in stage_events(l, k):
                    if e[0] == "unit":
                        if e[1] + 1 in mine:
                            maxima(e[1] + 1)
                            normalise(e[1] + 1)
                    elif e[0] == "item":
                        item(e[1], e[2])
                    elif e[0] == "subnorm":
                        for p in range(2):
                            dve.wait_ge(dstd_ready, 2 * l + p + 1)
                            dve.reciprocal(sq[:, p, 0:n], sq[:, p, 0:n]).then_inc(dinv_ready, 1)
                            dve.wait_ge(dinv_ready, 2 * l + p + 1)
                            yd = y[:, p, 0:n]
                            dve.scalar_tensor_tensor(out=yd, in0=yd, scalar=subln_g[l], in1=sq[:, p, 0:n], op0=ALU.mult, op1=ALU.mult).then_inc(dnorm_ready, 1)
                    elif e[0] in ("split", "pool_y"):
                        dve.wait_ge(y_h_ready, 4 * l + k + 1)
                        dve.tensor_tensor(y_l[:, :, 0:n], y[:, :, 0:n], y_h[:, :, 0:n], ALU.subtract).then_inc(y_l_ready, 1)
            for c in range(KT):
                dve.wait_ge(m_h_ready, l * KT + c + 1)
                dve.tensor_tensor(m_l[:, c, 0:n], unit(U_MACC + c)[:, 0:n], m_h[:, c, 0:n], ALU.subtract).then_inc(m_l_ready, 1)
            modulation(l, 2, ada_bank(1), ada_counts[l, 2], 0, 3 * KT)
            b = base[l, 1, "mixout"]
            reset_squares(l, 1, n)

            def out_body(i):
                for c in range(4):
                    split(b, i, 4, c)
                    update(l, 1, i, c, 4 + c, n, i * 4 + (b + c + 1))
                    add_squares(update_index(l, 1), i, 4, c, n)
            steps(dve, 2, 4, out_body)

        def inv_count(l, m):
            total = 0
            for ll in range(l + 1):
                for mm, u in enumerate(units[ll]):
                    if (ll, mm) > (l, m):
                        break
                    total += 4 if u[0] == DIFF_BR else 1
            return total

        modulation(0, 0, 0, ADA0_FIRST, 0, 2 * KT)
        for l in range(DEPTH):
            for sub in range(3):
                norm(l, sub)
                if (l, sub) == (0, 0):
                    modulation(0, 0, 0, ADA_GROUPS, 2 * KT, 3 * KT)
                if sub != 1:
                    ffn_phase(l, sub, 2 * l + sub // 2)
                else:
                    mix_phase(l)
        q = 3 * DEPTH
        dve.wait_ge(std_ready, q + 1)
        dve.reciprocal(rstd[:, 0:LAT], rstd[:, 0:LAT]).then_inc(rstd_ready, 1)
        dve.wait_ge(rstd_ready, q + 1)
        for k in range(KT):
            dve.scalar_tensor_tensor(out=norm_tmp_final(k), in0=h[:, k, 0:LAT], scalar=final_g[:, k:k + 1],
                                     in1=rstd[:, 0:LAT], op0=ALU.mult, op1=ALU.mult).then_inc(fin_ready, 1)


def arena_offset(nc, arena):
    return nc.lookup_mloc(arena).addr


_INPUTS = ["x", "c", "ctx", "c_ctx", "ada_w", "ada_b", "norm_g", "ffn_w_in", "ffn_w_out", "mix_w_in",
           "pool_w", "pool_scale", "na_rpb", "diff_lambda", "diff_subln_g", "mla_q_norm_g",
           "mla_kv_norm_g", "mla_w_qb", "mla_w_kvb", "branch_w_out", "mix_w_out", "final_norm_g"]


def kernel(**inputs):
    import concourse.bacc as bacc
    from concourse.bass_utils import run_bass_kernel_spmd

    nc = bacc.Bacc("TRN2", target_bir_lowering=False, num_devices=1)
    arrays = {name: np.ascontiguousarray(inputs[name]) for name in _INPUTS}
    arrays["tables"] = host_constants()
    arrays["pool_mats"] = pool_matrices()
    aps = {name: nc.dram_tensor(f"in_{name}", a.shape, mybir.dt.from_np(a.dtype), kind="ExternalInput").ap()
           for name, a in arrays.items()}
    aps["out"] = nc.dram_tensor("out", (1, LAT, D), F32, kind="ExternalOutput").ap()
    backbone(nc, **aps)
    r = run_bass_kernel_spmd(nc, [{f"in_{name}": a for name, a in arrays.items()}], core_ids=[0])
    return r.results[0]["out"]
```

```python
from contextlib import ExitStack

import numpy as np

import concourse.bass as bass
from concourse import mybir

F32 = mybir.dt.float32
F32R = mybir.dt.float32r
ALU = mybir.AluOpType
ACT = mybir.ActivationFunctionType
AX_X = mybir.AxisListType.X

P = 128
D = 1024
KT = D // P
LAT = 256
CTX = 256
TOK = LAT + CTX
DEPTH = 2
FFN = 2816
HT = FFN // P
EPS = 1e-6
GRID_W = 64
NA_ROWS, NA_COLS = 8, 16
RPB_ROWS, RPB_COLS = 2 * NA_ROWS - 1, 2 * NA_COLS - 1
GRID_ROWS = LAT // GRID_W
RPB_USED = 2 * GRID_ROWS - 1
POOL_WINDOWS = (2, 4, 8, 16)
ROT = 32
ROPE_STEPS = 3 * (5 + 4)
POOL_TILES = (2, 5, 7)
LAM_INIT = [0.8 - 0.6 * float(np.exp(-0.3 * l)) for l in range(DEPTH)]

RING = 4
AHEAD = 3

PROJ = (
    [("qa", c, 1792 + c * P) for c in range(2)]
    + [("kva", 0, 2048), ("kr", 0, 2176)]
    + [("dq", c, 1024 + c * P) for c in range(2)]
    + [("dk", c, 1280 + c * P) for c in range(2)]
    + [("pool", c, c * P) for c in range(2)]
    + [("dv", c, 1536 + c * P) for c in range(2)]
)
PROJ_NA = (
    [("nq", c, 256 + c * P) for c in range(2)]
    + [("nk", c, 512 + c * P) for c in range(2)]
    + [("nv", c, 768 + c * P) for c in range(2)]
)
PROJ_SLOTS = len(PROJ)
ROW_LOADS = 11
ROTATED = [("dq", 0), ("dq", 1), ("dk", 0), ("dk", 1), ("kr", 0)]
GATE_COL = 2208
TOKEN_MAJOR = ("pool", "dv", "nv")
QUERY_ONLY = ("pool", "qa", "dq", "nq")
POOL_BR, NA_BR, DIFF_BR, MLA_BR = range(4)

OUT_PARTS = ((0, 8), (8, 8), (16, 6))
ADA_GROUP = 256
ADA_GROUPS = 3 * D // ADA_GROUP
ADA_SLOTS = 2 * ADA_GROUPS
ADA_ROWS = 4


def mixing_stages():
    def gates(br, half):
        return [("gate", br, 4 * half + n) for n in range(4)]

    def proj(first, last):
        return [("proj", n) for n in range(first, last)]

    def ada(first, last):
        return [("ada", n) for n in range(first, last)]

    def woven(a, b):
        out, used = [], 0
        for n, x in enumerate(a):
            out += [x]
            if x[0] == "proj" and PROJ_NA[x[1]][:2] == ("nv", 0):
                continue
            upto = (n + 1) * len(b) // len(a)
            out += b[used:upto]
            used = upto
        return out

    def rest(br):
        return [("branch", br, 0)] + gates(br, 1) + [("branch", br, 1)]

    return [
        (DIFF_BR, woven(gates(POOL_BR, 0) + rest(POOL_BR) + gates(DIFF_BR, 0), ada(0, 12))),
        (MLA_BR, woven(proj(0, 4) + rest(DIFF_BR) + proj(4, 6) + gates(MLA_BR, 0), ada(12, 16))),
        (NA_BR, woven(rest(MLA_BR) + gates(NA_BR, 0), ada(16, 22))),
        (None, ada(22, 24) + rest(NA_BR)),
    ]


def out_slots(l, sub):
    return 3 if (l, sub) == (DEPTH - 1, 2) else 6


def slot_bases():
    base, at = {(0, 0, "ada"): 0}, ADA_SLOTS
    for l in range(DEPTH):
        for sub in range(3):
            phases = ([("proj", PROJ_SLOTS), ("mix", sum(len(items) for _, items in mixing_stages())), ("mixout", KT)]
                      if sub == 1 else [("in", 2 * HT), ("out", out_slots(l, sub) * KT)])
            for name, n in phases:
                base[l, sub, name] = at
                at += n
    return base, at


def attention_units(l):
    units = []
    for br in (DIFF_BR, MLA_BR, NA_BR):
        for ctx in ((False, True) if l < DEPTH - 1 else (False,)):
            for h in range(4):
                units += [(br, h, b, ctx) for b in range(2)]
    return units


def host_constants():
    t = np.arange(LAT)
    pos = np.stack([t // GRID_W, t % GRID_W]).astype(np.float32)
    half, quarter = ROT // 2, ROT // 4
    inv = (np.float32(10000.0) ** (-np.arange(0, half, 2, dtype=np.float32) / np.float32(half))).astype(np.float32)
    cos = np.zeros((P, LAT), np.float32)
    sin = np.zeros((P, LAT), np.float32)
    perm = np.zeros((P, P), np.float32)
    for f in range(P):
        a, r = (f % ROT) // half, f % half
        ang = pos[a] * inv[r % quarter]
        cos[f], sin[f] = np.cos(ang), np.sin(ang)
        if r < quarter:
            perm[f + quarter, f] = -1.0
        else:
            perm[f - quarter, f] = 1.0
    ident = np.eye(P, dtype=np.float32)
    blocks = np.kron(np.eye(2), np.ones((64, 64))).astype(np.float32)
    ones = np.ones((P, P), np.float32)
    j = np.arange(P) % GRID_W
    start = np.clip(j - NA_COLS // 2, 0, GRID_W - NA_COLS)[:, None]
    key = np.arange(GRID_W)[None, :]
    mask = np.where((key >= start) & (key < start + NA_COLS), 0.0, -1e30).astype(np.float32)
    pair = np.tile(np.eye(2, dtype=np.float32), (P // 2, 1))
    return np.concatenate([cos, sin, perm, ident, blocks, ones, mask, pair], axis=1)


def pool_matrices():
    out = np.zeros((LAT, 4, LAT), np.float32)
    for g, w in enumerate(POOL_WINDOWS):
        for i in range(LAT):
            lo, hi = max(i - w // 2, 0), min(i - w // 2 + w, LAT)
            out[lo:hi, g, i] += np.float32(1.0) / np.float32(hi - lo)
            out[i, g, i] -= 1.0
    return np.ascontiguousarray(out.reshape(2, P, 4, LAT).transpose(1, 2, 0, 3))


def backbone(nc, x, c, ctx, c_ctx, ada_w, ada_b, norm_g, ffn_w_in, ffn_w_out, mix_w_in, pool_w,
             pool_scale, na_rpb, diff_lambda, diff_subln_g, mla_q_norm_g, mla_kv_norm_g, mla_w_qb,
             mla_w_kvb, branch_w_out, mix_w_out, final_norm_g, tables, pool_mats, out):
    with ExitStack() as stack:
        build(nc, stack, locals())


def build(nc, stack, t):
    base, total_slots = slot_bases()

    def sb(name, shape, dt=F32):
        return stack.enter_context(nc.sbuf_tensor(name, shape, dt))

    def sem(name):
        return stack.enter_context(nc.semaphore(name))

    raw = sb("w_raw", [P, RING, KT, P])
    w_hi = sb("w_hi", [P, RING, KT, P], F32R)
    w_lo = sb("w_lo", [P, RING, KT, P], F32R)
    h = sb("h", [P, KT, TOK])
    xh = sb("xh", [P, KT, TOK], F32R)
    xl = sb("xl", [P, KT, TOK], F32R)
    work = sb("work", [P, 4, TOK])
    silu, prod = work[:, 0:2, :], work[:, 2:4, :]
    bias = work[:, :, :].rearrange("p h (b i k) -> p h b i k", b=2, i=GRID_ROWS)
    ssq = sb("ssq", [P, TOK])
    sq = sb("sq", [P, 2, TOK])
    rstd = sb("rstd", [P, TOK])
    tab = sb("tab", [P, 2 * LAT + 4 * P + GRID_W + 2])
    cos, sin = tab[:, 0:LAT], tab[:, LAT:2 * LAT]
    perm, ident, blocks, ones = [tab[:, 2 * LAT + n * P:2 * LAT + (n + 1) * P] for n in range(4)]
    mask = tab[:, 2 * LAT + 4 * P:2 * LAT + 4 * P + GRID_W]
    pair = tab[0:ADA_ROWS, 2 * LAT + 4 * P + GRID_W:]
    cols = sb("cols", [P, 2 * P])
    s4 = sb("s4", [P, KT, 4], F32R)
    sc = sb("sc", [P, 2, KT])
    mods = sb("mods", [P, 2, 24, 2])
    small = sb("small", [P, 96])
    UNITS = 2 * HT
    arena = sb("arena", [P, UNITS, TOK])
    start_of_arena = arena_offset(nc, arena)

    def view(name, unit, n, dt=F32):
        return nc.alloc_sbuf_tensor_at(name, [P, n, TOK], dt, offset=start_of_arena + unit * TOK * 4)

    hid_h = view("hid_h", 0, HT, F32R)
    hid_l = view("hid_l", HT, HT, F32R)
    feat = {("dq", 0): 0, ("dq", 1): 1, ("dk", 0): 2, ("dk", 1): 3,
            ("nq", 0): 0, ("nq", 1): 1, ("nk", 0): 2, ("nk", 1): 3,
            ("qa", 0): 16, ("qa", 1): 17, ("kva", 0): 18, ("kr", 0): 19}
    tok_unit = {"dv": 4, "nv": 4, "mv": 14, "pool": 30}
    MQ, MK, U_PT, U_P, U_Y, U_MACC = 6, 10, 16, 20, 24, 30
    y_h = view("y_h", 26, 2, F32R)
    y_l = view("y_l", 28, 2, F32R)
    m_h = view("m_h", 0, 8, F32R)
    m_l = view("m_l", 8, 8, F32R)

    def unit(n):
        return arena[:, n, :]

    def token_major(what):
        u = tok_unit[what]
        return arena[:, u:u + 2, :].rearrange("p a (t c) -> p (a t) c", c=256)

    x_tok = arena[:, 0:8, :].rearrange("p (t a) n -> p t (a n)", t=4)
    out_tok = arena[:, 0:4, :].rearrange("p (t a) n -> p t (a n)", t=2)
    rows = arena[:, 8, :].rearrange("p (a n) -> p a n", a=4)
    lam_row = arena[0:1, 9, :]
    norm_tmp = [unit(40 + n) for n in range(4)]
    pool_mat = arena[:, 32:36, :].rearrange("p g (t n) -> p g t n", t=2)
    pooled = arena[:, 36:38, :]
    y = arena[:, U_Y:U_Y + 2, :]
    tanh_buf = [unit(38 + n) for n in range(4)]
    mtmp = [unit(42), unit(43)]
    ada_rows = [unit(40)[0:ADA_ROWS, 0:ADA_GROUP]] + [rstd[0:ADA_ROWS, 0:ADA_GROUP]] * (3 * DEPTH - 1)
    w_qb = silu.rearrange("p a n -> p (a n)")[:, 0:768].rearrange("p (k n) -> p k n", k=2)
    w_kvb = prod[:, 0, :]
    w_pool = prod[:, 1, 0:256].rearrange("p (g n) -> p g n", g=2)

    rpb_rows = nc.dram_tensor("rpb_rows", [DEPTH, 4, RPB_USED, GRID_W, RPB_COLS], F32).ap()
    ps = stack.enter_context(nc.psum_tensor("ps", [P, 8, TOK], F32))
    SUM_BANKS, PT_BANK, O_BANK, S_BANKS = (6, 3), 4, 5, 3
    ADA0_BANKS, ADA0_COLS = (4, 7), 5

    def ada_bank(sub):
        return 3 if sub == 1 else 0

    def ada_b_cols(l, sub):
        return cols[:, l * P + sub * 24:l * P + sub * 24 + 24]

    def norm_g_cols(l, sub):
        return cols[:, 72 + (l * 3 + sub) * KT:72 + (l * 3 + sub + 1) * KT]

    final_g = cols[:, 120:128]
    cond_cols = cols[:, P + 72:P + 88]

    def pool_scale_col(l, p):
        return cols[:, P + 88 + 2 * l + p:P + 89 + 2 * l + p]

    def q_g_col(l, p):
        return cols[:, P + 92 + 2 * l + p:P + 93 + 2 * l + p]

    def kv_g_col(l):
        return cols[:, P + 96 + l:P + 97 + l]

    def subln_col(l):
        return cols[:, P + 98 + l:P + 99 + l]

    eps_col = small[:, 0:1]
    subln_g = [small[:, 1 + l:2 + l] for l in range(DEPTH)]
    neg_lam = [small[:, 3 + l:4 + l] for l in range(DEPTH)]

    def neg_max(comp):
        return small[:, 8 + comp % 8:9 + comp % 8]

    def exp_bias(comp):
        return small[:, 16 + comp % 8:17 + comp % 8]

    def exp_sum(comp):
        return small[:, 24 + comp % 8:25 + comp % 8]

    def exp_inv(comp):
        return small[:, 32 + comp % 8:33 + comp % 8]

    def exp_inv2(comp):
        return small[:, 40 + comp % 8:41 + comp % 8]

    def rstd_count(q, half):
        return sum(len(halves(tokens(j // 3, j % 3))) for j in range(q)) + half + 1

    def scaled_ready(eng, q, k):
        if k in POOL_TILES:
            eng.wait_ge(pool_scaled, q * len(POOL_TILES) + POOL_TILES.index(k) + 1)
        else:
            eng.wait_ge(dve_scaled, q * (KT - len(POOL_TILES)) + k - len([j for j in POOL_TILES if j < k]) + 1)

    def norm_tmp_final(k):
        return unit(8 + k // 2)[:, k % 2 * LAT:(k % 2 + 1) * LAT]

    w_loaded = [sem(f"w_loaded{s}") for s in range(RING)]
    w_hi_ready, w_lo_ready = sem("w_hi_ready"), sem("w_lo_ready")
    w_used = sem("w_used")
    in_loaded, rows_loaded, tab_loaded, lam_loaded = sem("in_loaded"), sem("rows_loaded"), sem("tab_loaded"), sem("lam_loaded")
    consts_set, eps_set, ssq_reset = sem("consts_set"), sem("eps_set"), sem("ssq_reset")
    xt_ready, xt_copied = sem("xt_ready"), sem("xt_copied")
    cols_t_ready, cols_ready, cond_ready, s4_ready = sem("cols_t_ready"), sem("cols_ready"), sem("cond_ready"), sem("s4_ready")
    lam_step, lam_exp, lam_bc, lam_ready = sem("lam_step"), sem("lam_exp"), sem("lam_bc"), sem("lam_ready")
    ada_rows_copied = sem("ada_rows_copied")
    ada_cols_ready, mod_step, mods_ready, gates_ready = [sem(n) for n in ("ada_cols_ready", "mod_step", "mods_ready", "gates_ready")]
    h_ready, sq_ready, ssq_ready = sem("h_ready"), sem("sq_ready"), sem("ssq_ready")
    sums_ready, std_ready, rstd_ready = sem("sums_ready"), sem("std_ready"), sem("rstd_ready")
    dve_scaled, pool_step, pool_scaled = sem("dve_scaled"), sem("pool_step"), sem("pool_scaled")
    xh_ready, xl_ready = sem("xh_ready"), sem("xl_ready")
    silu_ready, prod_ready, hid_h_ready, hid_l_ready = sem("silu_ready"), sem("prod_ready"), sem("hid_h_ready"), sem("hid_l_ready")
    mix_loaded, pool_loaded, bias_loaded, bias_ready = sem("mix_loaded"), sem("pool_loaded"), sem("bias_loaded"), sem("bias_ready")
    rpb_stored = sem("rpb_stored")
    proj_ready = sem("proj_ready")
    pooled_t, pooled_ready, pool_y_t, y_pool_ready = sem("pooled_t"), sem("pooled_ready"), sem("pool_y_t"), sem("y_pool_ready")
    msq_ready, msum_ready, mstd_ready, mrstd_ready, mnorm_ready = [sem(n) for n in ("msq_ready", "msum_ready", "mstd_ready", "mrstd_ready", "mnorm_ready")]
    rot_ready, rope_step = sem("rot_ready"), sem("rope_step")

    mla_t, mla_ready, kr_spread, mrot_ready = [sem(n) for n in ("mla_t", "mla_ready", "kr_spread", "mrot_ready")]
    score_ready, biased, max_step, max_ready = [sem(n) for n in ("score_ready", "biased", "max_step", "max_ready")]
    exp_ready, inv_step, probs_ready = [sem(n) for n in ("exp_ready", "inv_step", "probs_ready")]
    probs_t, probs_t_copied, attn_t, attn_ready = [sem(n) for n in ("probs_t", "probs_t_copied", "attn_t", "attn_ready")]
    dsq_ready, dsum_ready, dstd_ready, dinv_ready, dnorm_ready = [sem(n) for n in ("dsq_ready", "dsum_ready", "dstd_ready", "dinv_ready", "dnorm_ready")]
    y_h_ready, y_l_ready = sem("y_h_ready"), sem("y_l_ready")
    branch_t, tanh_ready, gated, macc_ready, m_h_ready, m_l_ready = [sem(n) for n in ("branch_t", "tanh_ready", "gated", "macc_ready", "m_h_ready", "m_l_ready")]
    fin_ready, fin_t, fin_copied, out_stored = [sem(n) for n in ("fin_ready", "fin_t", "fin_copied", "out_stored")]

    def update_index(l, sub):
        return 1 + 3 * l + sub

    def tokens(l, sub):
        return LAT if (l, sub) == (DEPTH - 1, 2) else TOK

    def query_tokens(l):
        return TOK if l < DEPTH - 1 else LAT

    def halves(n):
        return [(0, slice(0, LAT)), (1, slice(LAT, TOK))][:n // LAT]

    units = [attention_units(l) for l in range(DEPTH)]
    unit0 = [0, len(units[0])]
    comp_at, n_comps = {}, 0
    for l in range(DEPTH):
        for n, u in enumerate(units[l]):
            k = 2 if u[0] == DIFF_BR else 1
            comp_at[l, n] = list(range(n_comps, n_comps + k))
            n_comps += k
    unit_of_comp = {cc: unit0[l] + n for (l, n), v in comp_at.items() for cc in v}
    na_before = {}
    seen = 0
    for l in range(DEPTH):
        for n, u in enumerate(units[l]):
            na_before[l, n] = seen
            seen += u[0] == NA_BR and not u[3]

    stages = mixing_stages()
    stage_units = [[[n for n, u in enumerate(units[l]) if u[0] == br] for br, _ in stages] for l in range(DEPTH)]
    PROJ_ALL = PROJ_SLOTS + len(PROJ_NA)

    def stage_events(l, k):
        items = stages[k][1]
        slot = base[l, 1, "mix"] + sum(len(before) for _, before in stages[:k])
        us = stage_units[l][k]

        def cost(item):
            if item[0] == "ada":
                return 1
            if item[0] == "proj" and PROJ_NA[item[1]][0] == "nv":
                return 0 if PROJ_NA[item[1]][1] == 0 else 10
            return 5 if l < DEPTH - 1 or item[0] == "proj" else 3

        def follows(m):
            return m > 0 and events[-1][0] == "item" and (items[m][0] == "branch" or (
                items[m][0] == "ada" and m + 1 < len(items) and items[m + 1][0] == "branch" and items[m - 1][0] == "gate"))

        total, spent = sum(cost(it) for it in items), 0
        done = 0
        events = []
        for n in range(len(us) + 1):
            if n < len(us):
                events.append(("unit", us[n]))
            while done < len(items) and (n == len(us) or follows(done) or (spent + cost(items[done]) / 2) * (len(us) + 1) <= (n + 1) * total):
                events.append(("item", slot + done, items[done]))
                spent += cost(items[done])
                done += 1
        if us:
            events.append(("close",))
        first_item = next(m for m, e in enumerate(events) if e[0] == "item")
        if k == 0:
            events[first_item + 1:first_item + 1] = [("pool_y",)]
        elif k == 1:
            events.insert(events.index(("unit", us[2])), ("split",))
            events.insert(events.index(("unit", us[1])), ("subnorm_end",))
            events.insert(first_item, ("subnorm",))
        elif k > 1:
            events[0:0] = [("split",)]
        return events

    def pooled_banks(l):
        return 5, (comp_at[l, 0][0] + 2) % S_BANKS

    def bank_uses(l):
        uses, tanhs, gates, projs = {}, 32 * l, 32 * l, PROJ_ALL * l + PROJ_SLOTS
        order = 0
        for k in range(len(stages)):
            for e in stage_events(l, k):
                if e[0] == "pool_y":
                    for p in range(2):
                        uses["pool_y", p] = (order, y_pool_ready, l + 1)
                        order += 1
                elif e[0] == "subnorm":
                    for p in range(2):
                        uses["subnorm", p] = (order, dstd_ready, 2 * l + p + 1)
                        order += 1
                elif e[0] == "item" and e[2][0] == "gate":
                    tanhs += 1
                    uses[e[2]] = (order, tanh_ready, tanhs)
                    order += 1
                elif e[0] == "item" and e[2][0] == "proj":
                    projs += 1
                    uses[e[2]] = (order, proj_ready, projs)
                    order += 1
                elif e[0] == "item" and e[2][0] == "branch":
                    for n in range(4):
                        gates += 1
                        uses["branch", e[2][1], 4 * e[2][2] + n] = (order, gated, gates)
                        order += 1
        return uses

    branch_order = [POOL_BR] + [br for br, _ in stages[:3]]
    uses = [bank_uses(l) for l in range(DEPTH)]
    use_at = [{v[0]: v for v in uses[l].values()} for l in range(DEPTH)]

    def stream_bank(l, key):
        return 6 + uses[l][key][0] % 2

    def bank_free(eng, l, key):
        order = uses[l][key][0]
        if order >= 2:
            _, reader, count = use_at[l][order - 2]
            eng.wait_ge(reader, count)

    def steps(eng, iters, body_slots, body, peel=False):
        if peel:
            for i in range(iters):
                body(i)
        else:
            with eng.Fori(0, iters) as i:
                body(i)

    rotary_slots = {base[l, 1, "proj"] + [what for what, _, _ in PROJ].index("kr") for l in range(DEPTH)}

    def rotary_slot(b, i, s):
        return isinstance(i, int) and b + s + AHEAD in rotary_slots

    def wide(w, at, kt):
        return w[:, at].rearrange("p (k a) n -> p k (a n)", k=kt)

    def four(w, at):
        return w[:, at].rearrange("p k (a n) -> p k a n", n=ROT)

    def four_of(w, at):
        return w[:, at, :, 0:ROT].unsqueeze(2).to_broadcast([P, KT, P // ROT, ROT])

    block = stack.enter_context(nc.Block())

    @block.sync
    def _(sp):
        sp.dma_start(tab[:, :], t["tables"]).then_inc(tab_loaded, 16)
        sp.dma_start(x_tok[:, 0:2, :], t["x"][0].rearrange("(t p) n -> p t n", p=P)).then_inc(in_loaded, 16)
        sp.dma_start(x_tok[:, 2:4, :], t["ctx"][0].rearrange("(t p) n -> p t n", p=P)).then_inc(in_loaded, 16)

        def repeat(first, last, body):
            with sp.Fori(first + 1, last + 1) as r:
                body(lambda m, c: r * m + (c - m))

        def fixed(i):
            return lambda m, c: i * m + c

        def load(b, i, body_slots, s, src, col, kt=KT, shape=None):
            at = (b + s) % RING
            freed = i(body_slots, b + s - RING + 1)
            if not isinstance(freed, int) or freed > 0:
                sp.wait_ge(w_lo_ready, freed)
            dst = wide(raw, at, shape) if shape else raw[:, at, 0:kt, :]
            sp.dma_start(dst, src(col)).then_inc(w_loaded[at], 16)

        ada_first = t["ada_w"][0].rearrange("(k p) n -> p k n", p=P)

        def load_ada0(i):
            for s in range(4):
                group, k4 = s // 2, s % 2 * 4
                load(0, i, 4, s, lambda col: ada_first[:, k4:k4 + 4, bass.ds(col, ADA_GROUP)], i(2 * ADA_GROUP, group * ADA_GROUP), shape=4)

        sp.wait_ge(rows_loaded, ROW_LOADS * 16)
        load_ada0(fixed(0))
        repeat(1, ADA_SLOTS // 4, load_ada0)
        for l in range(DEPTH):
            for sub in range(3):
                nl, nsub = (l, sub + 1) if sub < 2 else (l + 1, 0)
                ada = t["ada_w"][min(nl, DEPTH - 1)].rearrange("(k p) n -> p k n", p=P)
                ada_col = nsub * 3 * D
                if sub != 1:
                    w_in = t["ffn_w_in"][l, sub // 2].rearrange("(k p) n -> p k n", p=P)
                    w_out = t["ffn_w_out"][l, sub // 2].rearrange("(k p) n -> p k n", p=P)
                    b = base[l, sub, "in"]

                    def load_in(i, b=b, w_in=w_in):
                        for s in range(4):
                            load(b, i, 4, s, lambda col: w_in[:, :, bass.ds(col, P)], i(2 * P, s // 2 * P + s % 2 * FFN))
                    repeat(0, HT // 2, load_in)
                    b = base[l, sub, "out"]
                    per = out_slots(l, sub)

                    def load_out(i, b=b, w_out=w_out, ada=ada, per=per, ada_col=ada_col):
                        for c in range(4):
                            for part, (k0, kn) in enumerate(OUT_PARTS):
                                s = per * c + part * (per // 3)
                                if per == 6:
                                    group, k4 = (3 * c + part) // 2, (3 * c + part) % 2 * 4
                                    load(b, i, 24, s, lambda col: ada[:, k4:k4 + 4, bass.ds(col, ADA_GROUP)],
                                         i(6 * ADA_GROUP, ada_col + group * ADA_GROUP), shape=4)
                                    s += 1
                                load(b, i, 4 * per, s, lambda col: w_out[:, k0:k0 + kn, bass.ds(col, P)],
                                     i(4 * P, c * P), kn)
                    repeat(0, 2, load_out)
                else:
                    w_mix = t["mix_w_in"][l].rearrange("(k p) n -> p k n", p=P)
                    whole = lambda w: lambda c: w[:, :, c:c + P]
                    b = base[l, sub, "proj"]
                    for s, (_, _, col) in enumerate(PROJ):
                        load(b, fixed(0), 0, s, whole(w_mix), col)
                    s = base[l, sub, "mix"]
                    for _, items in stages:
                        for item in items:
                            if item[0] == "proj":
                                load(s, fixed(0), 0, 0, whole(w_mix), PROJ_NA[item[1]][2])
                            elif item[0] == "gate":
                                load(s, fixed(0), 0, 0, whole(w_mix), GATE_COL + item[1] * D + item[2] * P)
                            elif item[0] == "ada":
                                k4 = item[1] % 2 * 4
                                load(s, fixed(0), 0, 0, lambda col: ada[:, k4:k4 + 4, col:col + ADA_GROUP],
                                     ada_col + item[1] // 2 * ADA_GROUP, shape=4)
                            else:
                                w_branch = t["branch_w_out"][l, item[1]].rearrange("(k p) n -> p k n", p=P)
                                load(s, fixed(0), 0, 0, lambda col: w_branch[:, :, col:col + 4 * P], item[2] * 4 * P, shape=2)
                            s += 1
                    w_mo = t["mix_w_out"][l].rearrange("(k p) n -> p k n", p=P)
                    b = base[l, sub, "mixout"]

                    def load_mo(i, b=b, w_mo=w_mo):
                        for s in range(4):
                            load(b, i, 4, s, lambda col: w_mo[:, :, bass.ds(col, P)], i(4 * P, s * P))
                    repeat(0, 2, load_mo)
        for tt in range(2):
            sp.wait_ge(fin_copied, 2 * (tt + 1))
            sp.dma_start(t["out"][0, tt * P:(tt + 1) * P, :], out_tok[:, tt, :]).then_inc(out_stored, 16)
        sp.wait_ge(out_stored, 32)

    @block.gpsimd
    def _(pool):
        pool.dma_start(lam_row[:, 0:256], t["diff_lambda"].rearrange("l q d -> (l q d)").rearrange("(a n) -> a n", a=1)).then_inc(lam_loaded, 16)

        for l in range(DEPTH):
            for hd in range(4):
                first = NA_ROWS - GRID_ROWS
                src = t["na_rpb"][l, hd, first:first + RPB_USED, :].unsqueeze(1).to_broadcast([RPB_USED, GRID_W, RPB_COLS])
                pool.dma_start(rpb_rows[l, hd], src).then_inc(rpb_stored, 16)
        pool.wait_ge(rpb_stored, 16 * 4 * DEPTH)

        def norm(q, n):
            pool.wait_ge(mods_ready, q + 1)
            pool.wait_ge(rstd_ready, rstd_count(q, len(halves(n)) - 1))
            for j, k in enumerate(POOL_TILES):
                if k >= 4:
                    pool.wait_ge(xl_ready, q * KT + k - 3)
                tmp = norm_tmp[k % 4]
                pool.tensor_tensor(tmp[:, 0:n], h[:, k, 0:n], rstd[:, 0:n], ALU.mult).then_inc(pool_step, 1)
                pool.wait_ge(pool_step, q * len(POOL_TILES) + j + 1)
                for w, cols_of in halves(n):
                    last = pool.tensor_scalar(tmp[:, cols_of], tmp[:, cols_of], mods[:, q % 2, 8 + k, w:w + 1], None, ALU.mult)
                last.then_inc(pool_scaled, 1)

        for l in range(DEPTH):
            norm(3 * l, tokens(l, 0))
            norm(3 * l + 1, tokens(l, 1))
            pool.dma_start(w_qb, t["mla_w_qb"][l].rearrange("(k p) n -> p k n", p=P)).then_inc(mix_loaded, 16)
            pool.dma_start(w_kvb, t["mla_w_kvb"][l]).then_inc(mix_loaded, 16)
            pool.memset(w_pool, 0.0).then_inc(consts_set, 1)
            pool.wait_ge(consts_set, l + 1)
            for g in range(4):
                r = g % 2 * 64
                pool.dma_start(w_pool[r:r + 64, g // 2, r:r + 64], t["pool_w"][l, g]).then_inc(pool_loaded, 16)
            pool.dma_start(pool_mat, t["pool_mats"]).then_inc(pool_loaded, 16)
            pool.wait_ge(pool_y_t, l + 1)
            for hd in range(4):
                for r in range(GRID_ROWS):
                    src = bass.AP(tensor=rpb_rows.tensor,
                                  offset=(l * 4 + hd) * RPB_USED * GRID_W * RPB_COLS
                                  + (GRID_ROWS - 1 - r) * GRID_W * RPB_COLS + NA_COLS - 1,
                                  ap=[[RPB_COLS - 1, GRID_W], [GRID_W * RPB_COLS, GRID_ROWS], [1, GRID_W]])
                    pool.dma_start(bias[r % 2 * 64:r % 2 * 64 + 64, hd, r // 2], src).then_inc(bias_loaded, 16)
            pool.wait_ge(bias_loaded, 16 * 16 * (l + 1))
            for hd in range(4):
                for b in range(2):
                    pool.tensor_tensor(bias[:, hd, b], bias[:, hd, b],
                                       mask.unsqueeze(1).to_broadcast([P, GRID_ROWS, GRID_W]), ALU.add).then_inc(bias_ready, 1)
            n = query_tokens(l)
            for br in range(1, 4):
                for c in range(KT):
                    pool.wait_ge(gated, 32 * l + 8 * br + c + 1)
                    if br > 1:
                        pool.wait_ge(macc_ready, 24 * l + 8 * (br - 2) + c + 1)
                    acc = unit(U_MACC + c)[:, 0:n]
                    pool.tensor_tensor(acc, acc, mtmp[c % 2][:, 0:n], ALU.add).then_inc(macc_ready, 1)
            norm(3 * l + 2, tokens(l, 2))

    @block.tensor
    def _(pe):
        pe.wait_ge(tab_loaded, 16)
        pe.wait_ge(rows_loaded, 16 * ROW_LOADS)
        pe.transpose(ps[:, 6, 0:P], rows[:, 0, :], ident)
        pe.transpose(ps[:, 6, P:P + 100], rows[0:100, 1, :], ident[0:100, 0:100]).then_inc(cols_t_ready, 1)
        pe.wait_ge(in_loaded, 32)
        def transpose_input(k):
            if k >= 4:
                pe.wait_ge(xt_copied, k - 3)
            for tt in range(4):
                last = pe.transpose(ps[:, k % 4, tt * P:(tt + 1) * P], x_tok[:, tt, k * P:(k + 1) * P], ident)
            last.then_inc(xt_ready, 1)

        def three_passes(dst, hi, lo, mh, ml, first, last):
            pe.matmul(dst, lo, mh, start=first, stop=False)
            pe.matmul(dst, hi, ml, start=False, stop=False)
            return pe.matmul(dst, hi, mh, start=False, stop=last)

        def slot_products(b, i, body_slots, s, dst, mh, ml, kt=KT, first=True, last=True):
            at = (b + s) % RING
            pe.wait_ge(w_lo_ready, i * body_slots + (b + s + 1))
            for k in range(kt):
                mm = three_passes(dst, w_hi[:, at, k, :], w_lo[:, at, k, :], mh(k), ml(k),
                                  first and k == 0, last and k == kt - 1)
            mm.then_inc(w_used, 1)

        def ada_slot(b, i, body_slots, s, bank, part):
            at = (b + s) % RING
            pe.wait_ge(w_lo_ready, i * body_slots + (b + s + 1))
            hi, lo = wide(w_hi, at, 4), wide(w_lo, at, 4)
            for k in range(4):
                pe.matmul(ps[0:ADA_ROWS, bank, 0:ADA_GROUP], s4[:, 4 * part + k, :], lo[:, k, :], start=(part == 0 and k == 0), stop=False)
                mm = pe.matmul(ps[0:ADA_ROWS, bank, 0:ADA_GROUP], s4[:, 4 * part + k, :], hi[:, k, :], start=False, stop=(part == 1 and k == 3))
            mm.then_inc(w_used, 1)

        def ada_columns(q, i, group, bank, per=6):
            pe.wait_ge(ada_rows_copied, i * per + (q * ADA_GROUPS + group + 1))
            for n in range(2):
                mm = pe.matmul(ps[:, bank, bass.ds(i * (4 * per) + (ADA_GROUP + 4 * group + 2 * n), 2)],
                               ada_rows[q][:, n * P:(n + 1) * P], pair, start=True, stop=True)
            return mm

        def norm_sum(q, n):
            pe.wait_ge(ssq_ready, KT * (q + 1))
            for w, cols_of in halves(n):
                pe.matmul(ps[:, SUM_BANKS[w], 0:LAT], ones, ssq[:, cols_of], start=True, stop=True).then_inc(sums_ready, 1)

        def first_slots(q, b, banks, n):
            for k in range(KT):
                pe.wait_ge(xl_ready, q * KT + k + 1)
                for s in range(2):
                    if k == 0:
                        pe.wait_ge(w_lo_ready, b + s + 1)
                    at = (b + s) % RING
                    mm = three_passes(ps[:, banks[s], 0:n], w_hi[:, at, k, :], w_lo[:, at, k, :],
                                      xh[:, k, 0:n], xl[:, k, 0:n], k == 0, k == KT - 1)
                    if k == KT - 1:
                        mm.then_inc(w_used, 1)

        def ffn_phase(l, sub, f):
            n = tokens(l, sub)
            q = update_index(l, sub) - 1
            b = base[l, sub, "in"]

            def pair(i, p):
                for s in (2 * p, 2 * p + 1):
                    slot_products(b, i, 4, s, ps[:, s, 0:n], lambda k: xh[:, k, 0:n], lambda k: xl[:, k, 0:n])

            def body(i):
                for p in range(2):
                    if not isinstance(i, int):
                        pe.wait_ge(prod_ready, i * 2 + (f * HT + p - 1))
                    pair(i, p)
            first_slots(q, b, (0, 1), n)
            pair(0, 1)
            with pe.Fori(1, HT // 2) as i:
                body(i)

            b = base[l, sub, "out"]
            u = update_index(l, sub)

            per = out_slots(l, sub)

            def out_body(i):
                for c in range(4):
                    if not (isinstance(i, int) and i == 0):
                        pe.wait_ge(h_ready, i * 4 + ((u - 1) * KT + c - 3))
                    for part, (k0, kn) in enumerate(OUT_PARTS):
                        s = per * c + part * (per // 3)
                        if per == 6:
                            if isinstance(i, int) and i == 0 and c == 0 and part == 0:
                                pe.wait_ge(prod_ready, (f + 1) * HT - 1)
                            j = 3 * c + part
                            if j % 2 == 0 and j > 0:
                                ada_columns(3 * l + sub + 1, i, j // 2 - 1, 0)
                            ada_slot(b, i, 24, s, 0, j % 2)
                            s += 1
                        if isinstance(i, int) and i == 0 and c == 0:
                            pe.wait_ge(hid_l_ready, f * HT + k0 + kn)
                        slot_products(b, i, 4 * per, s, ps[:, 4 + c, 0:n],
                                      lambda k: hid_h[:, k0 + k, 0:n], lambda k: hid_l[:, k0 + k, 0:n],
                                      kn, part == 0, part == 2)
                if per == 6 and c == 3:
                    mm = ada_columns(3 * l + sub + 1, i, 5, 0)
                    if i == 1:
                        mm.then_inc(ada_cols_ready, 1)
            for i in range(2):
                out_body(i)

        def project(l, slot, what, banks):
            n = query_tokens(l) if what in QUERY_ONLY else TOK
            if what not in TOKEN_MAJOR:
                slot_products(slot, 0, 0, 0, ps[:, banks[0], 0:n], lambda k: xh[:, k, 0:n], lambda k: xl[:, k, 0:n])
                return
            at = (slot - 1) % RING
            assert at + 1 < RING
            pe.wait_ge(w_lo_ready, slot + 1)
            per = n // P // 2
            for tt in range(n // P):
                dst, tokens_of = ps[:, banks[tt // per], tt % per * 256:(tt % per + 1) * 256], slice(tt * P, (tt + 1) * P)
                for k in range(KT):
                    mm = three_passes(dst, xh[:, k, tokens_of], xl[:, k, tokens_of],
                                      w_hi[:, at:at + 2, k, :], w_lo[:, at:at + 2, k, :], k == 0, k == KT - 1)
            mm.then_inc(w_used, 2)

        def proj_phase(l):
            b = base[l, 1, "proj"]
            n = query_tokens(l)
            first_slots(3 * l + 1, b, (6, 7), n)
            for s, (what, c, _) in enumerate(PROJ):
                if s < 2 or (what in TOKEN_MAJOR and c == 0):
                    continue
                pe.wait_ge(proj_ready, l * PROJ_ALL + s - 1)
                project(l, b + s, what, (6, 7) if what in TOKEN_MAJOR else (6 + s % 2,))
                if s == 3:
                    latent_sums(l, n)
                elif s == 6:
                    latent_queries(l, n)
                elif s == 7:
                    latent_keys_values(l)
                elif s == 9:
                    rotations(l)
            pooled_sums(l, n)

        def latent_sums(l, n):
            pe.wait_ge(msq_ready, 3 * l + 3)
            pe.matmul(ps[:, 0, 0:n], ones, unit(U_P)[:, 0:n], start=True, stop=False)
            pe.matmul(ps[:, 0, 0:n], ones, unit(U_P + 1)[:, 0:n], start=False, stop=True)
            pe.matmul(ps[:, 1, :], ones, unit(U_P + 2), start=True, stop=True).then_inc(msum_ready, 1)

        def latent_queries(l, n):
            pe.wait_ge(mnorm_ready, l + 1)
            pe.wait_ge(mix_loaded, 32 * (l + 1))
            for hd in range(4):
                for k in range(2):
                    mm = pe.matmul(ps[0:96, 2 + hd, 0:n], w_qb[:, k, hd * 96:(hd + 1) * 96],
                                   unit(feat["qa", k])[:, 0:n], start=(k == 0), stop=(k == 1))
                mm.then_inc(mla_t, 1)

        def latent_keys_values(l):
            for hd in range(4):
                if hd >= 2:
                    pe.wait_ge(mla_ready, 10 * l + hd - 1)
                pe.matmul(ps[0:64, hd, :], w_kvb[:, hd * P:hd * P + 64], unit(feat["kva", 0]),
                          start=True, stop=True).then_inc(mla_t, 1)
            w_v = w_kvb.rearrange("p (h c) -> p h c", h=4)[:, :, 64:P]
            for tt in range(4):
                if tt % 2 == 0:
                    pe.wait_ge(mla_ready, 10 * l + 3 + tt // 2)
                mm = pe.matmul(ps[:, 4 + tt // 2, tt % 2 * 256:tt % 2 * 256 + 256],
                               unit(feat["kva", 0])[:, tt * P:(tt + 1) * P], w_v, start=True, stop=True)
                if tt % 2:
                    mm.then_inc(mla_t, 1)

        def rotations(l):
            pe.wait_ge(mla_ready, 10 * (l + 1))
            for n, key in enumerate(ROTATED):
                mm = pe.matmul(ps[:, n // 2, n % 2 * LAT:(n % 2 + 1) * LAT], perm, unit(feat[key])[:, 0:LAT], start=True, stop=True)
                if n % 2 or n == 4:
                    mm.then_inc(rot_ready, 1)
            for hd in range(4):
                mm = pe.matmul(ps[64:96, 3 + hd // 2, hd % 2 * LAT:(hd % 2 + 1) * LAT], perm[64:96, 64:96],
                               unit(MQ + hd)[64:96, 0:LAT], start=True, stop=True)
                if hd % 2:
                    mm.then_inc(mrot_ready, 1)

        def pooled_sums(l, n):
            pe.wait_ge(pool_loaded, 16 * 5 * (l + 1))
            pe.wait_ge(rope_step, l * ROPE_STEPS + 3 * len(ROTATED))
            u = token_major("pool")
            for g in range(4):
                r = g % 2 * 64
                for half in range(n // LAT):
                    for tt in range(2):
                        mm = pe.matmul(ps[r:r + 64, pooled_banks(l)[g // 2], half * LAT:(half + 1) * LAT],
                                       u[:, 2 * half + tt, g * 64:(g + 1) * 64], pool_mat[:, g, tt, :],
                                       start=(tt == 0), stop=(tt == 1))
            mm.then_inc(pooled_t, 1)

        def mixing_phase(l):
            us = units[l]
            pe.wait_ge(proj_ready, l * PROJ_ALL + PROJ_SLOTS)

            def scores(n):
                br, hd, b, is_ctx = us[n]
                q0 = (LAT if is_ctx else 0) + b * P
                k0 = LAT if is_ctx else 0
                for j, cc in enumerate(comp_at[l, n]):
                    if cc >= S_BANKS:
                        pe.wait_ge(exp_ready, cc - S_BANKS + 1)
                    if br == DIFF_BR:
                        r, rn, qt, kt = hd % 2 * 64 + j * 32, 32, feat["dq", hd // 2], feat["dk", hd // 2]
                    elif br == NA_BR:
                        r, rn, qt, kt = hd % 2 * 64, 64, feat["nq", hd // 2], feat["nk", hd // 2]
                    else:
                        r, rn, qt, kt = 0, 96, MQ + hd, MK + hd
                    pe.matmul(ps[:, cc % S_BANKS, 0:TOK - k0], unit(qt)[r:r + rn, q0:q0 + P],
                              unit(kt)[r:r + rn, k0:TOK], start=True, stop=True).then_inc(score_ready, 1)

            def transposes(n):
                u = unit0[l] + n
                _, _, _, is_ctx = us[n]
                pe.wait_ge(probs_ready, u + 1)
                if u >= 1:
                    pe.wait_ge(probs_t_copied, u)
                src = unit(U_P + comp_at[l, n][0] % 4)
                for kt in range(2 if is_ctx else 4):
                    mm = pe.transpose(ps[:, PT_BANK, kt * P:(kt + 1) * P], src[:, kt * P:(kt + 1) * P], ident)
                mm.then_inc(probs_t, 1)

            def values(n):
                br, hd, _, is_ctx = us[n]
                v = (unit0[l] + n) // 2
                pe.wait_ge(probs_t_copied, unit0[l] + n + 1)
                if v >= 1:
                    pe.wait_ge(attn_ready, v)
                vals = token_major({DIFF_BR: "dv", NA_BR: "nv", MLA_BR: "mv"}[br])
                pt = arena[:, U_PT + v % 2 * 2:U_PT + v % 2 * 2 + 2, :].rearrange("p a (t q) -> p (a t) q", q=256)
                r, kts = hd % 2 * 64, 2 if is_ctx else 4
                for kt in range(kts):
                    mm = pe.matmul(ps[r:r + 64, O_BANK, 0:256],
                                   vals[:, (2 if is_ctx else 0) + kt, hd * 64:(hd + 1) * 64], pt[:, kt, :],
                                   start=(kt == 0), stop=(kt == kts - 1))
                mm.then_inc(attn_t, 1)

            nt = query_tokens(l)

            def item(slot, it):
                if it[0] == "ada":
                    if it[1] % 2 == 0 and it[1] > 0:
                        ada_columns(3 * l + 2, 0, it[1] // 2 - 1, ada_bank(1))
                    ada_slot(slot, 0, 0, 0, ada_bank(1), it[1] % 2)
                elif it[0] == "branch":
                    at, br = slot % RING, it[1]
                    pe.wait_ge(w_lo_ready, slot + 1)
                    pe.wait_ge(y_l_ready, 4 * l + branch_order.index(br) + 1)
                    for c in range(4):
                        key = ("branch", br, 4 * it[2] + c)
                        bank_free(pe, l, key)
                        for k in range(2):
                            mm = three_passes(ps[:, stream_bank(l, key), 0:nt], w_hi[:, at, 4 * k + c, :], w_lo[:, at, 4 * k + c, :],
                                              y_h[:, k, 0:nt], y_l[:, k, 0:nt], k == 0, k == 1)
                        mm.then_inc(branch_t if c < 3 else w_used, 1)
                else:
                    bank_free(pe, l, it)
                    if it[0] == "proj":
                        what, c, _ = PROJ_NA[it[1]]
                        if what not in TOKEN_MAJOR:
                            project(l, slot, what, (stream_bank(l, it),))
                        elif c == 1:
                            project(l, slot, what, (stream_bank(l, ("proj", it[1] - 1)), stream_bank(l, it)))
                    else:
                        slot_products(slot, 0, 0, 0, ps[:, stream_bank(l, it), 0:nt], lambda k: xh[:, k, 0:nt], lambda k: xl[:, k, 0:nt])

            nt = query_tokens(l)

            for k in range(len(stages)):
                mine = stage_units[l][k]
                if k == 0:
                    scores(0)
                    pe.wait_ge(pooled_ready, l + 1)
                    scores(1)
                    pe.wait_ge(kr_spread, l + 1)
                    pe.wait_ge(rope_step, (l + 1) * ROPE_STEPS)
                for e in stage_events(l, k):
                    if e[0] == "unit":
                        n = e[1]
                        if n + 2 < len(us):
                            scores(n + 2)
                        transposes(n)
                        if n % 2 == 0 and n > mine[0]:
                            values(n - 1)
                    elif e[0] == "item":
                        item(e[1], e[2])
                    elif e[0] == "close":
                        values(mine[-1])
                    elif e[0] == "pool_y":
                        for p in range(2):
                            bank_free(pe, l, ("pool_y", p))
                            mm = pe.matmul(ps[:, stream_bank(l, ("pool_y", p)), 0:nt], w_pool[:, p, :], pooled[:, p, 0:nt], start=True, stop=True)
                        mm.then_inc(pool_y_t, 1)
                    elif e[0] == "subnorm":
                        for p in range(2):
                            bank_free(pe, l, ("subnorm", p))
                            pe.wait_ge(dsq_ready, 2 * l + p + 1)
                            pe.matmul(ps[:, stream_bank(l, ("subnorm", p)), 0:nt], blocks, sq[:, p, 0:nt],
                                      start=True, stop=True).then_inc(dsum_ready, 1)

            ada_columns(3 * l + 2, 0, ADA_GROUPS - 1, ada_bank(1)).then_inc(ada_cols_ready, 1)
            b = base[l, 1, "mixout"]
            u = update_index(l, 1)
            for i in range(2):
                for s in range(4):
                    at = (b + s) % RING
                    if i > 0:
                        pe.wait_ge(h_ready, (u - 1) * KT + i * 4 + s - 3)
                    else:
                        pe.wait_ge(gated, 32 * (l + 1))
                    pe.wait_ge(w_lo_ready, b + 4 * i + s + 1)
                    for k in range(KT):
                        if i == 0 and s == 0:
                            pe.wait_ge(m_l_ready, l * KT + k + 1)
                        mm = three_passes(ps[:, 4 + s, 0:nt], w_hi[:, at, k, :], w_lo[:, at, k, :],
                                          m_h[:, k, 0:nt], m_l[:, k, 0:nt], k == 0, k == KT - 1)
                    mm.then_inc(w_used, 1)

        for k in range(4):
            transpose_input(k)
        pe.wait_ge(s4_ready, 2)

        def first_ada(i):
            for s in range(4):
                ada_slot(0, i, 4, s, ADA0_BANKS[s // 2], s % 2)
                if s % 2 == 0 and not (isinstance(i, int) and i + s == 0):
                    ada_columns(0, i, s // 2 - 1, ADA0_COLS, per=2)
                if isinstance(i, int) and i == 0:
                    transpose_input(4 + s)
        first_ada(0)
        first_ada(1)
        norm_sum(0, TOK)
        with pe.Fori(2, ADA_SLOTS // 4) as i:
            first_ada(i)
        ada_columns(0, 0, ADA_GROUPS - 1, ADA0_COLS).then_inc(ada_cols_ready, 1)
        pe.wait_ge(lam_step, 3)
        pe.matmul(ps[:, ADA0_BANKS[0], 0:2], ones[0:1, :], lam_row[:, 400:402], start=True, stop=True).then_inc(lam_bc, 1)
        for l in range(DEPTH):
            for sub in range(3):
                if (l, sub) != (0, 0):
                    norm_sum(3 * l + sub, tokens(l, sub))
                if sub != 1:
                    ffn_phase(l, sub, 2 * l + sub // 2)
                else:
                    proj_phase(l)
                    mixing_phase(l)
        norm_sum(3 * DEPTH, LAT)
        for tt in range(2):
            for k in range(KT):
                pe.wait_ge(fin_ready, k + 1)
                mm = pe.transpose(ps[:, 2 * tt + k // 4, k % 4 * P:(k % 4 + 1) * P], norm_tmp_final(k)[:, tt * P:(tt + 1) * P], ident)
                if k % 4 == 3:
                    mm.then_inc(fin_t, 1)

    @block.scalar
    def _(act):
        def split(b, i, body_slots, s):
            at = (b + s + AHEAD) % RING
            act.wait_ge(w_loaded[at], i * (body_slots // RING * 16) + 16 * ((b + s + AHEAD) // RING + 1))
            if not (isinstance(i, int) and i * body_slots + b + s + AHEAD < RING):
                act.wait_ge(w_used, i * body_slots + (b + s + AHEAD - RING + 1))
            if rotary_slot(b, i, s):
                act.copy(four(w_hi, at), four_of(raw, at)).then_inc(w_hi_ready, 1)
                return
            act.copy(w_hi[:, at], raw[:, at]).then_inc(w_hi_ready, 1)

        def maybe_split(b, i, body_slots, s):
            if not isinstance(i, int) or i * body_slots + b + s + AHEAD < total_slots:
                split(b, i, body_slots, s)

        def squares(u, i, step, c, n):
            tile = i * step + c
            act.wait_ge(h_ready, i * step + ((u - 1) * KT + c + 1))
            act.wait_ge(ssq_ready, i * step + (u * KT + c - 1))
            act.activation(sq[:, c % 2, 0:n], h[:, bass.ds(tile, 1), 0:n].rearrange("p a n -> p (a n)"),
                           ACT.Square).then_inc(sq_ready, 1)

        def load_rows(r0, n, a, src):
            act.dma_start(rows[r0:r0 + n, a, :], src).then_inc(rows_loaded, 16)

        ada_b_rows = t["ada_b"].rearrange("l (r n) -> l r n", n=P)
        load_rows(0, 72, 0, ada_b_rows[0])
        load_rows(72, 48, 0, t["norm_g"].rearrange("l s (k n) -> (l s k) n", n=P))
        load_rows(120, 8, 0, t["final_norm_g"].rearrange("(k n) -> k n", n=P))
        load_rows(0, 72, 1, ada_b_rows[1])
        load_rows(72, 8, 1, t["c"].rearrange("b (k n) -> (b k) n", n=P))
        load_rows(80, 8, 1, t["c_ctx"].rearrange("(k n) -> k n", n=P))
        load_rows(88, 4, 1, t["pool_scale"].rearrange("l (k n) -> (l k) n", n=P))
        load_rows(92, 4, 1, t["mla_q_norm_g"].rearrange("l (k n) -> (l k) n", n=P))
        load_rows(96, 2, 1, t["mla_kv_norm_g"])
        for half in range(2):
            act.dma_start(rows[98:100, 1, half * 64:half * 64 + 64], t["diff_subln_g"]).then_inc(rows_loaded, 16)

        act.wait_ge(cols_ready, 1)
        act.activation(sc[:, :, :].rearrange("p w k -> p (w k)"), cond_cols, ACT.Silu).then_inc(cond_ready, 1)
        act.wait_ge(cond_ready, 1)
        act.copy(s4[:, :, 0:2].rearrange("p k w -> p w k"), sc[:, :, :]).then_inc(s4_ready, 1)
        def input_tile(k):
            act.wait_ge(xt_ready, k + 1)
            act.copy(h[:, k, :], ps[:, k % 4, :]).then_inc(xt_copied, 1)
            act.wait_ge(xt_copied, k + 1)
            if k >= 2:
                act.wait_ge(ssq_ready, k - 1)
            act.activation(sq[:, k % 2, :], h[:, k, :], ACT.Square).then_inc(sq_ready, 1)

        def copy_ada_rows(q, used, bank):
            act.wait_ge(w_used, used)
            act.copy(ada_rows[q], ps[0:ADA_ROWS, bank, 0:ADA_GROUP]).then_inc(ada_rows_copied, 1)

        def root(dst, src, width):
            return act.activation(dst, src, ACT.Sqrt, bias=eps_col, scale=1.0 / width)

        def deviations(q, n):
            for w, cols_of in halves(n):
                act.wait_ge(sums_ready, rstd_count(q, w))
                root(rstd[:, cols_of], ps[:, SUM_BANKS[w], 0:LAT], D).then_inc(std_ready, 1)

        def shift_tiles(q, n):
            for k in range(KT):
                scaled_ready(act, q, k)
                for w, cols_of in halves(n):
                    last = act.activation(xh[:, k, cols_of], norm_tmp[k % 4][:, cols_of], ACT.Identity, bias=mods[:, q % 2, k, w:w + 1])
                last.then_inc(xh_ready, 1)

        def ffn_phase(l, sub, f):
            n = tokens(l, sub)
            b = base[l, sub, "in"]

            def body(i):
                for p in range(2):
                    split(b, i, 4, 2 * p)
                    act.wait_ge(w_used, i * 4 + (b + 2 * p + 1))
                    if f * HT + p >= 2 or not isinstance(i, int):
                        act.wait_ge(prod_ready, i * 2 + (f * HT + p - 1))
                    act.activation(silu[:, p, 0:n], ps[:, 2 * p, 0:n], ACT.Silu).then_inc(silu_ready, 1)
                    split(b, i, 4, 2 * p + 1)
                    act.wait_ge(prod_ready, i * 2 + (f * HT + p + 1))
                    act.copy(hid_h[:, bass.ds(i * 2 + p, 1), 0:n].rearrange("p a n -> p (a n)"), prod[:, p, 0:n]).then_inc(hid_h_ready, 1)
            body(0)
            with act.Fori(1, HT // 2) as i:
                body(i)
            b = base[l, sub, "out"]
            u = update_index(l, sub)

            per = out_slots(l, sub)

            def out_body(i):
                for c in range(4):
                    for part in range(per):
                        maybe_split(b, i, 4 * per, per * c + part)
                        if per == 6 and part % 2 == 1 and (3 * c + part // 2) % 2 == 1:
                            copy_ada_rows(u, i * 24 + (b + per * c + part), 0)
                    squares(u, i, 4, c, n)
            steps(act, 2, 12, out_body, peel=(l, sub) == (DEPTH - 1, 2))

        def mix_phase(l):
            n = query_tokens(l)
            b = base[l, 1, "proj"]
            def projected(slot, what, c, banks):
                m = n if what in QUERY_ONLY else TOK
                if what in TOKEN_MAJOR:
                    if c == 0:
                        return
                    act.wait_ge(w_used, slot + 1)
                    per = m // P // 2
                    for j, bank in enumerate(banks):
                        act.copy(token_major(what)[:, j * per:(j + 1) * per, :],
                                 ps[:, bank, 0:per * 256].rearrange("p (t n) -> p t n", n=256)).then_inc(proj_ready, 1)
                    return
                act.wait_ge(w_used, slot + 1)
                bank = banks[0]
                if what in ("qa", "kva"):
                    j = c if what == "qa" else 2
                    act.activation(unit(U_P + j)[:, 0:m], ps[:, bank, 0:m], ACT.Square).then_inc(msq_ready, 1)
                if what == "nq":
                    act.mul(unit(feat[what, c])[:, 0:m], ps[:, bank, 0:m], 0.125).then_inc(proj_ready, 1)
                else:
                    act.copy(unit(feat[what, c])[:, 0:m], ps[:, bank, 0:m]).then_inc(proj_ready, 1)

            def mla_copies(first, last):
                for j in range(first, last):
                    act.wait_ge(mla_t, 10 * l + j + 1)
                    if j < 4:
                        act.copy(unit(MQ + j)[0:96, 0:n], ps[0:96, 2 + j, 0:n]).then_inc(mla_ready, 1)
                    elif j < 8:
                        act.copy(unit(MK + j - 4)[0:64, :], ps[0:64, j - 4, :]).then_inc(mla_ready, 1)
                    else:
                        act.copy(token_major("mv")[:, 2 * (j - 8):2 * (j - 8) + 2, :],
                                 ps[:, j - 4, :].rearrange("p (t n) -> p t n", t=2)).then_inc(mla_ready, 1)

            for s, (what, c, _) in enumerate(PROJ):
                split(b, 0, 0, s)
                projected(b + s, what, c, (6, 7) if what in TOKEN_MAJOR else (6 + s % 2,))
                if s == 3:
                    act.wait_ge(msum_ready, l + 1)
                    root(unit(U_P)[:, 0:n], ps[:, 0, 0:n], 256)
                    root(unit(U_P + 2), ps[:, 1, :], 128).then_inc(mstd_ready, 1)
                elif s == 6:
                    mla_copies(0, 4)
                elif s == 7:
                    mla_copies(4, 10)
            act.wait_ge(pooled_t, l + 1)
            act.copy(pooled[:, 0, 0:n], ps[:, pooled_banks(l)[0], 0:n])
            act.copy(pooled[:, 1, 0:n], ps[:, pooled_banks(l)[1], 0:n]).then_inc(pooled_ready, 1)
            us = units[l]

            def exps(m):
                br, _, _, is_ctx = us[m]
                width = CTX if is_ctx else TOK
                scale = {DIFF_BR: 32 ** -0.5, MLA_BR: 96 ** -0.5, NA_BR: 1.0}[br]
                for cc in comp_at[l, m]:
                    act.wait_ge(max_ready, cc + 1)
                    if cc >= 4:
                        act.wait_ge(probs_t, unit_of_comp[cc - 4] + 1)
                    act.activation(unit(U_P + cc % 4)[:, 0:width], ps[:, cc % S_BANKS, 0:width], ACT.Exp,
                                   bias=exp_bias(cc), scale=scale, accum_out=exp_sum(cc)).then_inc(exp_ready, 1)

            def copy_t(m):
                u = unit0[l] + m
                _, _, qb, is_ctx = us[m]
                v = u // 2
                act.wait_ge(probs_t, u + 1)
                if v >= 2:
                    act.wait_ge(attn_t, v - 1)
                kts = 2 if is_ctx else 4
                pt = arena[:, U_PT + v % 2 * 2:U_PT + v % 2 * 2 + 2, :].rearrange("p a (t q) -> p (a t) q", q=256)
                act.copy(pt[:, 0:kts, qb * P:(qb + 1) * P],
                         ps[:, PT_BANK, 0:kts * P].rearrange("p (t q) -> p t q", q=P)).then_inc(probs_t_copied, 1)

            def copy_out(m):
                br, hd, _, is_ctx = us[m]
                v = (unit0[l] + m) // 2
                act.wait_ge(attn_t, v + 1)
                r, q0 = hd % 2 * 64, LAT if is_ctx else 0
                act.wait_ge(y_l_ready, 4 * l + branch_order.index(br))
                act.copy(y[r:r + 64, hd // 2, q0:q0 + LAT], ps[r:r + 64, O_BANK, 0:LAT]).then_inc(attn_ready, 1)

            def item(slot, it):
                split(slot, 0, 0, 0)
                if it[0] == "ada" and it[1] % 2 == 1:
                    copy_ada_rows(3 * l + 2, slot + 1, ada_bank(1))
                elif it[0] == "proj":
                    what, c, _ = PROJ_NA[it[1]]
                    banks = (stream_bank(l, ("proj", it[1] - 1)), stream_bank(l, it)) if what in TOKEN_MAJOR and c == 1 else (stream_bank(l, it),)
                    projected(slot, what, c, banks)
                elif it[0] == "gate":
                    _, _, count = uses[l][it]
                    act.wait_ge(w_used, slot + 1)
                    if count > 4:
                        act.wait_ge(gated, (count - 1) // 4 * 4)
                    act.activation(tanh_buf[it[2] % 4][:, 0:n], ps[:, stream_bank(l, it), 0:n], ACT.Tanh, scale=0.5).then_inc(tanh_ready, 1)

            for k in range(len(stages)):
                mine = stage_units[l][k]
                if k == 0:
                    exps(0)
                    exps(1)
                for e in stage_events(l, k):
                    if e[0] == "unit":
                        m = e[1]
                        copy_t(m)
                        if m + 2 < len(us):
                            exps(m + 2)
                        if m % 2 == 0 and m > mine[0]:
                            copy_out(m - 1)
                    elif e[0] == "item":
                        item(e[1], e[2])
                    elif e[0] == "close":
                        copy_out(mine[-1])
                        if k == 0:
                            act.wait_ge(attn_ready, (unit0[l] + mine[-1] + 1) // 2)
                            for p in range(2):
                                act.activation(sq[:, p, 0:n], y[:, p, 0:n], ACT.Square).then_inc(dsq_ready, 1)
                    elif e[0] == "pool_y":
                        act.wait_ge(pool_y_t, l + 1)
                        for p in range(2):
                            last = act.activation(y[:, p, 0:n], ps[:, stream_bank(l, ("pool_y", p)), 0:n], ACT.Copy, scale=pool_scale_col(l, p))
                        last.then_inc(y_pool_ready, 1)
                        act.wait_ge(y_pool_ready, l + 1)
                        act.copy(y_h[:, :, 0:n], y[:, :, 0:n]).then_inc(y_h_ready, 1)
                    elif e[0] == "subnorm":
                        for p in range(2):
                            act.wait_ge(dsum_ready, 2 * l + p + 1)
                            root(sq[:, p, 0:n], ps[:, stream_bank(l, ("subnorm", p)), 0:n], 64).then_inc(dstd_ready, 1)
                    elif e[0] == "split":
                        if k == 1:
                            act.wait_ge(dnorm_ready, 2 * (l + 1))
                        else:
                            act.wait_ge(attn_ready, (unit0[l] + stage_units[l][k - 1][-1] + 1) // 2)
                        act.wait_ge(w_used, base[l, 1, "mix"] + sum(len(items) for _, items in stages[:k]))
                        act.copy(y_h[:, :, 0:n], y[:, :, 0:n]).then_inc(y_h_ready, 1)
            for c in range(KT):
                act.wait_ge(macc_ready, 24 * l + 16 + c + 1)
                act.copy(m_h[:, c, 0:n], unit(U_MACC + c)[:, 0:n]).then_inc(m_h_ready, 1)
            b = base[l, 1, "mixout"]
            u = update_index(l, 1)

            def out_body(i):
                for c in range(4):
                    split(b, i, 4, c)
                    squares(u, i, 4, c, n)
            steps(act, 2, 4, out_body)

        for k in range(AHEAD):
            input_tile(k)
            split(-AHEAD, 0, 0, k)

        def first_ada(i):
            for s in range(4):
                split(0, i, 4, s)
                if isinstance(i, int) and 4 * i + s + AHEAD < KT:
                    input_tile(4 * i + s + AHEAD)
                if s % 2 == 1:
                    copy_ada_rows(0, i * 4 + (s + 1), ADA0_BANKS[s // 2])
        first_ada(0)
        first_ada(1)
        act.wait_ge(eps_set, 1)
        deviations(0, TOK)
        act.wait_ge(lam_step, 2)
        act.activation(lam_row[:, 392:396], lam_row[:, 384:388], ACT.Exp).then_inc(lam_exp, 1)
        with act.Fori(2, ADA_SLOTS // 4) as i:
            first_ada(i)
        act.wait_ge(mods_ready, 1)
        for l in range(DEPTH):
            for sub in range(3):
                if (l, sub) != (0, 0):
                    deviations(3 * l + sub, tokens(l, sub))
                shift_tiles(3 * l + sub, tokens(l, sub))
                if sub != 1:
                    ffn_phase(l, sub, 2 * l + sub // 2)
                else:
                    mix_phase(l)
        deviations(3 * DEPTH, LAT)
        for tt in range(2):
            for a in range(2):
                act.wait_ge(fin_t, 2 * tt + a + 1)
                act.copy(out_tok[:, tt, a * 512:(a + 1) * 512], ps[:, 2 * tt + a, :]).then_inc(fin_copied, 1)

    @block.vector
    def _(dve):
        def split(b, i, body_slots, s):
            at = (b + s + AHEAD) % RING
            dve.wait_ge(w_hi_ready, i * body_slots + (b + s + AHEAD + 1))
            if rotary_slot(b, i, s):
                dve.tensor_tensor(four(w_lo, at), four_of(raw, at), four(w_hi, at), ALU.subtract).then_inc(w_lo_ready, 1)
                return
            dve.tensor_tensor(w_lo[:, at], raw[:, at], w_hi[:, at], ALU.subtract).then_inc(w_lo_ready, 1)

        def maybe_split(b, i, body_slots, s):
            if not isinstance(i, int) or i * body_slots + b + s + AHEAD < total_slots:
                split(b, i, body_slots, s)

        def add_squares(u, i, step, c, n):
            dve.wait_ge(sq_ready, i * step + (u * KT + c + 1))
            dve.wait_ge(ssq_ready, i * step + (u * KT + c))
            dve.tensor_tensor(ssq[:, 0:n], ssq[:, 0:n], sq[:, c % 2, 0:n], ALU.add).then_inc(ssq_ready, 1)

        dve.memset(eps_col, EPS).then_inc(eps_set, 1)
        dve.wait_ge(cols_t_ready, 1)
        dve.tensor_copy(cols[:, 0:P + 100], ps[:, 6, 0:P + 100]).then_inc(cols_ready, 1)
        dve.wait_ge(cols_ready, 1)
        for l in range(DEPTH):
            dve.tensor_scalar(subln_g[l], subln_col(l), 1.0 - LAM_INIT[l], None, ALU.mult).then_inc(cols_ready, 1)
        dve.wait_ge(s4_ready, 1)
        dve.tensor_tensor(s4[:, :, 2:4].rearrange("p k w -> p w k"), sc[:, :, :],
                          s4[:, :, 0:2].rearrange("p k w -> p w k"), ALU.subtract).then_inc(s4_ready, 1)
        dve.wait_ge(lam_loaded, 16)
        dl = lam_row[:, 0:256].rearrange("o (a b d) -> o a b d", a=4, b=2)
        dve.tensor_tensor(lam_row[:, 256:384].rearrange("o (a d) -> o a d", a=4), dl[:, :, 0, :], dl[:, :, 1, :], ALU.mult).then_inc(lam_step, 1)
        dve.wait_ge(lam_step, 1)
        dve.reduce_sum(lam_row[:, 384:388], lam_row[:, 256:384].rearrange("o (a d) -> o a d", a=4), AX_X).then_inc(lam_step, 1)

        def add_input_squares(k):
            dve.wait_ge(sq_ready, k + 1)
            if k == 0:
                dve.tensor_copy(ssq[:, :], sq[:, 0, :]).then_inc(ssq_ready, 1)
            else:
                dve.wait_ge(ssq_ready, k)
                dve.tensor_tensor(ssq[:, :], ssq[:, :], sq[:, k % 2, :], ALU.add).then_inc(ssq_ready, 1)

        def modulation(l, sub, bank):
            q = 3 * l + sub
            m = mods[:, q % 2]
            acc = ps[:, bank, ADA_GROUP:ADA_GROUP + 6 * KT].rearrange("p (n c) -> p n c", c=2)
            dve.wait_ge(ada_cols_ready, q + 1)
            dve.tensor_tensor(m, acc, ada_b_cols(l, sub).unsqueeze(2).to_broadcast([P, 3 * KT, 2]), ALU.add).then_inc(mod_step, 1)
            dve.wait_ge(mod_step, q + 1)
            dve.scalar_tensor_tensor(out=m[:, 8:16, :], in0=m[:, 8:16, :], scalar=1.0,
                                     in1=norm_g_cols(l, sub).unsqueeze(2).to_broadcast([P, KT, 2]), op0=ALU.add, op1=ALU.mult).then_inc(mods_ready, 1)
            dve.tensor_scalar(m[:, 16:24, :], m[:, 16:24, :], 0.5, None, ALU.mult).then_inc(gates_ready, 1)

        def inverse_deviations(q, n):
            for w, cols_of in halves(n):
                dve.wait_ge(std_ready, rstd_count(q, w))
                dve.reciprocal(rstd[:, cols_of], rstd[:, cols_of]).then_inc(rstd_ready, 1)

        def norm(l, sub):
            q, n = 3 * l + sub, tokens(l, sub)
            m = mods[:, q % 2]
            dve.wait_ge(mods_ready, q + 1)
            mine = [k for k in range(KT) if k not in POOL_TILES]

            def scale_upto(last):
                while mine and mine[0] <= last:
                    k = mine.pop(0)
                    if k >= 4:
                        dve.wait_ge(xl_ready, q * KT + k - 3)
                    for w, cols_of in halves(n):
                        dve.wait_ge(rstd_ready, rstd_count(q, w))
                        done = dve.scalar_tensor_tensor(out=norm_tmp[k % 4][:, cols_of], in0=h[:, k, cols_of],
                                                        scalar=m[:, 8 + k, w:w + 1], in1=rstd[:, cols_of], op0=ALU.mult, op1=ALU.mult)
                    done.then_inc(dve_scaled, 1)

            for k in range(KT):
                scale_upto(k + 1)
                scaled_ready(dve, q, k)
                dve.wait_ge(xh_ready, q * KT + k + 1)
                for w, cols_of in halves(n):
                    last = dve.scalar_tensor_tensor(out=xl[:, k, cols_of], in0=norm_tmp[k % 4][:, cols_of], scalar=m[:, k, w:w + 1],
                                                    in1=xh[:, k, cols_of], op0=ALU.add, op1=ALU.subtract)
                last.then_inc(xl_ready, 1)

        def update(l, sub, i, c, bank, n, used):
            u = update_index(l, sub)
            m = mods[:, (3 * l + sub) % 2]
            tile = i * 4 + c
            dve.wait_ge(w_used, used)
            hk = h[:, bass.ds(tile, 1), :].rearrange("p a n -> p (a n)")
            for w, cols_of in halves(n):
                gate = m[:, bass.ds(tile + 16, 1), w:w + 1].rearrange("p a n -> p (a n)")
                last = dve.scalar_tensor_tensor(out=hk[:, cols_of], in0=ps[:, bank, cols_of], scalar=gate,
                                                in1=hk[:, cols_of], op0=ALU.mult, op1=ALU.add)
            last.then_inc(h_ready, 1)

        def reset_squares(l, sub, n):
            dve.wait_ge(gates_ready, 3 * l + sub + 1)
            dve.memset(ssq[:, 0:n], 0.0).then_inc(ssq_reset, 1)
            dve.wait_ge(ssq_reset, update_index(l, sub))

        def ffn_phase(l, sub, f):
            n = tokens(l, sub)
            b = base[l, sub, "in"]

            def body(i):
                for p in range(2):
                    split(b, i, 4, 2 * p)
                    split(b, i, 4, 2 * p + 1)
                    dve.wait_ge(w_used, i * 4 + (b + 2 * p + 2))
                    dve.wait_ge(silu_ready, i * 2 + (f * HT + p + 1))
                    if f * HT + p >= 2 or not isinstance(i, int):
                        dve.wait_ge(hid_l_ready, i * 2 + (f * HT + p - 1))
                    dve.tensor_tensor(prod[:, p, 0:n], silu[:, p, 0:n], ps[:, 2 * p + 1, 0:n], ALU.mult).then_inc(prod_ready, 1)
                    dve.wait_ge(hid_h_ready, i * 2 + (f * HT + p + 1))
                    tile = bass.ds(i * 2 + p, 1)
                    dve.tensor_tensor(hid_l[:, tile, 0:n].rearrange("p a n -> p (a n)"), prod[:, p, 0:n],
                                      hid_h[:, tile, 0:n].rearrange("p a n -> p (a n)"), ALU.subtract).then_inc(hid_l_ready, 1)
            body(0)
            with dve.Fori(1, HT // 2) as i:
                body(i)
            b = base[l, sub, "out"]
            reset_squares(l, sub, n)

            per = out_slots(l, sub)

            def out_body(i):
                for c in range(4):
                    for part in range(per):
                        maybe_split(b, i, 4 * per, per * c + part)
                    update(l, sub, i, c, 4 + c, n, i * (4 * per) + (b + per * (c + 1)))
                    add_squares(update_index(l, sub), i, 4, c, n)
            steps(dve, 2, 12, out_body, peel=(l, sub) == (DEPTH - 1, 2))
            if per == 6:
                nl, nsub = (l, 1) if sub == 0 else (l + 1, 0)
                modulation(nl, nsub, 0)

        rope = [0]

        def rotate(dst, partner, rows_of):
            a, c = sq[rows_of, 0, 0:LAT], sq[rows_of, 1, 0:LAT]
            dve.tensor_tensor(a, partner, sin[rows_of, :], ALU.mult).then_inc(rope_step, 1)
            dve.tensor_tensor(c, dst, cos[rows_of, :], ALU.mult).then_inc(rope_step, 1)
            rope[0] += 2
            dve.wait_ge(rope_step, rope[0])
            rope[0] += 1
            return dve.tensor_tensor(dst, a, c, ALU.add).then_inc(rope_step, 1)

        def mix_phase(l):
            n = query_tokens(l)
            b = base[l, 1, "proj"]
            for s in range(PROJ_SLOTS):
                split(b, 0, 0, s)
                if s == 4:
                    dve.wait_ge(mstd_ready, l + 1)
                    dve.reciprocal(unit(U_P + 1)[:, 0:n], unit(U_P)[:, 0:n]).then_inc(mrstd_ready, 1)
                elif s == 5:
                    dve.reciprocal(unit(U_P + 3), unit(U_P + 2)).then_inc(mrstd_ready, 1)
                    dve.wait_ge(mrstd_ready, 2 * (l + 1))
                    for p in range(2):
                        qa = unit(feat["qa", p])[:, 0:n]
                        dve.scalar_tensor_tensor(out=qa, in0=qa, scalar=q_g_col(l, p), in1=unit(U_P + 1)[:, 0:n], op0=ALU.mult, op1=ALU.mult)
                    kva = unit(feat["kva", 0])
                    dve.scalar_tensor_tensor(out=kva, in0=kva, scalar=kv_g_col(l), in1=unit(U_P + 3), op0=ALU.mult, op1=ALU.mult).then_inc(mnorm_ready, 1)
                elif s == 10:
                    for j, key in enumerate(ROTATED):
                        dve.wait_ge(rot_ready, 3 * l + j // 2 + 1)
                        if j:
                            dve.wait_ge(rope_step, rope[0])
                        rotate(unit(feat[key])[:, 0:LAT], ps[:, j // 2, j % 2 * LAT:(j % 2 + 1) * LAT], slice(0, P))
                    dve.wait_ge(rope_step, rope[0])
                    for hd in range(4):
                        last = dve.tensor_copy(unit(MK + hd)[64:96, :], unit(feat["kr", 0])[64:96, :])
                    last.then_inc(kr_spread, 1)
                    rows_of = slice(64, 96)
                    for hd in range(4):
                        dve.wait_ge(mrot_ready, 2 * l + hd // 2 + 1)
                        dve.wait_ge(rope_step, rope[0])
                        rotate(unit(MQ + hd)[rows_of, 0:LAT], ps[rows_of, 3 + hd // 2, hd % 2 * LAT:(hd % 2 + 1) * LAT], rows_of)
            us = units[l]

            def maxima(m):
                br, hd, qb, is_ctx = us[m]
                width = CTX if is_ctx else TOK
                for cc in comp_at[l, m]:
                    bank = ps[:, cc % S_BANKS, 0:width]
                    dve.wait_ge(score_ready, cc + 1)
                    if br == NA_BR and not is_ctx:
                        dve.wait_ge(bias_ready, 8 * (l + 1))
                        dve.tensor_tensor(bank[:, 0:LAT], bank[:, 0:LAT],
                                          bias[:, hd, qb].rearrange("p i k -> p (i k)"), ALU.add).then_inc(biased, 1)
                        dve.wait_ge(biased, na_before[l, m] + 1)
                    if cc >= 8:
                        dve.wait_ge(exp_ready, cc - 7)
                    dve.tensor_reduce(neg_max(cc), bank, AX_X, ALU.max, negate=True).then_inc(max_step, 1)
                    dve.wait_ge(max_step, cc + 1)
                    scale = {DIFF_BR: 32 ** -0.5, MLA_BR: 96 ** -0.5, NA_BR: 1.0}[br]
                    dve.tensor_scalar(exp_bias(cc), neg_max(cc), scale, None, ALU.mult).then_inc(max_ready, 1)

            def normalise(m):
                br, _, _, is_ctx = us[m]
                width = CTX if is_ctx else TOK
                cs = comp_at[l, m]
                for cc in cs:
                    dve.wait_ge(exp_ready, cc + 1)
                    dve.reciprocal(exp_inv(cc), exp_sum(cc)).then_inc(inv_step, 1)
                dve.wait_ge(inv_step, inv_count(l, m) - (br == DIFF_BR) * 2)
                first = unit(U_P + cs[0] % 4)[:, 0:width]
                if br == DIFF_BR:
                    second = unit(U_P + cs[1] % 4)[:, 0:width]
                    dve.tensor_tensor(exp_inv2(cs[0]), exp_inv(cs[1]), neg_lam[l], ALU.mult).then_inc(inv_step, 1)
                    dve.tensor_scalar(first, first, exp_inv(cs[0]), None, ALU.mult).then_inc(inv_step, 1)
                    dve.wait_ge(inv_step, inv_count(l, m))
                    dve.scalar_tensor_tensor(out=first, in0=second, scalar=exp_inv2(cs[0]), in1=first,
                                             op0=ALU.mult, op1=ALU.add).then_inc(probs_ready, 1)
                else:
                    dve.tensor_scalar(first, first, exp_inv(cs[0]), None, ALU.mult).then_inc(probs_ready, 1)

            if l == 0:
                dve.wait_ge(lam_ready, 2)
            def item(slot, it):
                split(slot, 0, 0, 0)
                if it[0] != "branch":
                    return
                for c in range(4 * it[2], 4 * it[2] + 4):
                    _, _, count = uses[l]["branch", it[1], c]
                    if c % 4 < 3:
                        dve.wait_ge(branch_t, (count - 1) // 4 * 3 + c % 4 + 1)
                    else:
                        dve.wait_ge(w_used, slot + 1)
                    dve.wait_ge(tanh_ready, count)
                    if it[1] == branch_order[0]:
                        dst = unit(U_MACC + c)[:, 0:n]
                    else:
                        dst = mtmp[c % 2][:, 0:n]
                        done = count - 8 * (l + 1)
                        if done > 2:
                            dve.wait_ge(macc_ready, done - 2)
                    dve.scalar_tensor_tensor(out=dst, in0=tanh_buf[c % 4][:, 0:n], scalar=1.0,
                                             in1=ps[:, stream_bank(l, ("branch", it[1], c)), 0:n],
                                             op0=ALU.add, op1=ALU.mult).then_inc(gated, 1)

            def head_norm(p):
                dve.wait_ge(dstd_ready, 2 * l + p + 1)
                dve.reciprocal(sq[:, p, 0:n], sq[:, p, 0:n]).then_inc(dinv_ready, 1)
                dve.wait_ge(dinv_ready, 2 * l + p + 1)
                yd = y[:, p, 0:n]
                dve.scalar_tensor_tensor(out=yd, in0=yd, scalar=subln_g[l], in1=sq[:, p, 0:n], op0=ALU.mult, op1=ALU.mult).then_inc(dnorm_ready, 1)

            for k in range(len(stages)):
                if k == 0:
                    maxima(0)
                    maxima(1)
                    normalise(0)
                for e in stage_events(l, k):
                    if e[0] == "unit":
                        if e[1] + 1 < len(us):
                            normalise(e[1] + 1)
                        if e[1] + 2 < len(us):
                            maxima(e[1] + 2)
                    elif e[0] == "item":
                        item(e[1], e[2])
                    elif e[0] == "subnorm":
                        head_norm(0)
                    elif e[0] == "subnorm_end":
                        head_norm(1)
                    elif e[0] in ("split", "pool_y"):
                        dve.wait_ge(y_h_ready, 4 * l + k + 1)
                        dve.tensor_tensor(y_l[:, :, 0:n], y[:, :, 0:n], y_h[:, :, 0:n], ALU.subtract).then_inc(y_l_ready, 1)
            for c in range(KT):
                dve.wait_ge(m_h_ready, l * KT + c + 1)
                dve.tensor_tensor(m_l[:, c, 0:n], unit(U_MACC + c)[:, 0:n], m_h[:, c, 0:n], ALU.subtract).then_inc(m_l_ready, 1)
            modulation(l, 2, ada_bank(1))
            b = base[l, 1, "mixout"]
            reset_squares(l, 1, n)

            def out_body(i):
                for c in range(4):
                    split(b, i, 4, c)
                    update(l, 1, i, c, 4 + c, n, i * 4 + (b + c + 1))
                    add_squares(update_index(l, 1), i, 4, c, n)
            steps(dve, 2, 4, out_body)

        def inv_count(l, m):
            total = 0
            for ll in range(l + 1):
                for mm, u in enumerate(units[ll]):
                    if (ll, mm) > (l, m):
                        break
                    total += 4 if u[0] == DIFF_BR else 1
            return total

        for k in range(AHEAD):
            add_input_squares(k)
            split(-AHEAD, 0, 0, k)

        def first_ada(i):
            for s in range(4):
                split(0, i, 4, s)
                if isinstance(i, int) and 4 * i + s + AHEAD < KT:
                    add_input_squares(4 * i + s + AHEAD)
        first_ada(0)
        first_ada(1)
        dve.wait_ge(lam_exp, 1)
        e = lam_row[:, 392:396].rearrange("o (l a) -> o l a", l=2)
        dve.tensor_tensor(lam_row[:, 400:402], e[:, :, 1], e[:, :, 0], ALU.subtract).then_inc(lam_step, 1)
        inverse_deviations(0, TOK)
        with dve.Fori(2, ADA_SLOTS // 4) as i:
            first_ada(i)
        modulation(0, 0, ADA0_COLS)
        dve.wait_ge(lam_bc, 1)
        for l in range(DEPTH):
            dve.tensor_scalar(neg_lam[l], ps[:, ADA0_BANKS[0], l:l + 1], -LAM_INIT[l], None, ALU.add).then_inc(lam_ready, 1)
        for l in range(DEPTH):
            for sub in range(3):
                if (l, sub) != (0, 0):
                    inverse_deviations(3 * l + sub, tokens(l, sub))
                norm(l, sub)
                if sub != 1:
                    ffn_phase(l, sub, 2 * l + sub // 2)
                else:
                    mix_phase(l)
        q = 3 * DEPTH
        inverse_deviations(q, LAT)
        dve.wait_ge(rstd_ready, rstd_count(q, 0))
        for k in range(KT):
            dve.scalar_tensor_tensor(out=norm_tmp_final(k), in0=h[:, k, 0:LAT], scalar=final_g[:, k:k + 1],
                                     in1=rstd[:, 0:LAT], op0=ALU.mult, op1=ALU.mult).then_inc(fin_ready, 1)


def arena_offset(nc, arena):
    return nc.lookup_mloc(arena).addr


_INPUTS = ["x", "c", "ctx", "c_ctx", "ada_w", "ada_b", "norm_g", "ffn_w_in", "ffn_w_out", "mix_w_in",
           "pool_w", "pool_scale", "na_rpb", "diff_lambda", "diff_subln_g", "mla_q_norm_g",
           "mla_kv_norm_g", "mla_w_qb", "mla_w_kvb", "branch_w_out", "mix_w_out", "final_norm_g"]


def kernel(**inputs):
    import concourse.bacc as bacc
    from concourse.bass_utils import run_bass_kernel_spmd

    nc = bacc.Bacc("TRN2", target_bir_lowering=False, num_devices=1)
    arrays = {name: np.ascontiguousarray(inputs[name]) for name in _INPUTS}
    arrays["tables"] = host_constants()
    arrays["pool_mats"] = pool_matrices()
    aps = {name: nc.dram_tensor(f"in_{name}", a.shape, mybir.dt.from_np(a.dtype), kind="ExternalInput").ap()
           for name, a in arrays.items()}
    aps["out"] = nc.dram_tensor("out", (1, LAT, D), F32, kind="ExternalOutput").ap()
    backbone(nc, **aps)
    r = run_bass_kernel_spmd(nc, [{f"in_{name}": a for name, a in arrays.items()}], core_ids=[0])
    return r.results[0]["out"]
```
